# Optimizing a Trainium2 kernel written in Bass

```python
import jax, jax.numpy as jnp
from jax import lax
import numpy as np
import math
import jax
import jax.numpy as jnp

D_MODEL = 1024
BATCH = 1
SEQ = 512
DEPTH = 1

MIX_WIDTH = D_MODEL
GMLP_WIDTH = MIX_WIDTH // 2
RWKV_WIDTH = MIX_WIDTH - GMLP_WIDTH
HEAD_DIM = 64
GMLP_HEADS = GMLP_WIDTH // HEAD_DIM
RWKV_HEADS = RWKV_WIDTH // HEAD_DIM
CHUNK = 128
DECAY_LORA = 32
ICLR_LORA = 32
GATE_LORA = 96
RWKV_PROJ = 3 * RWKV_WIDTH + DECAY_LORA + ICLR_LORA + GATE_LORA
IN_WIDTH = 2 * GMLP_WIDTH + RWKV_PROJ
N_GROUPS = 4
EXPERTS_PER_GROUP = 8
N_EXPERTS = N_GROUPS * EXPERTS_PER_GROUP
TOP_K = 2
EXPERT_HIDDEN = 512
MOE_BLOCK = 128
RMS_EPS = 1e-6
LN_EPS = 1e-5
GN_EPS = 64e-5


def _rmsnorm(x, g):
    x32 = x.astype(jnp.float32)
    y = x32 * lax.rsqrt(jnp.mean(x32 * x32, axis=-1, keepdims=True) + RMS_EPS)
    return y.astype(x.dtype) * g

def _modulate(h, shift, scale):
    return h * (1 + scale[:, None, :]) + shift[:, None, :]

def _token_shift(z):
    return jnp.pad(z, ((0, 0), (1, 0), (0, 0)))[:, :-1]

def _gmlp_mixer(zu, zv, ln_w, ln_b, ws, bs):
    B, S, _ = zu.shape
    u = jax.nn.gelu(zu)
    v = jax.nn.gelu(zv)
    v32 = v.astype(jnp.float32)
    m = jnp.mean(v32, axis=-1, keepdims=True)
    var = jnp.mean(jnp.square(v32 - m), axis=-1, keepdims=True)
    v = ((v32 - m) * lax.rsqrt(var + LN_EPS)).astype(zu.dtype) * ln_w + ln_b
    vc = v.reshape(B, S // CHUNK, CHUNK, GMLP_HEADS, HEAD_DIM)
    w_causal = jnp.tril(ws)
    mixed = jnp.einsum('hts,bcshd->bcthd', w_causal, vc) + bs.T[None, None, :, :, None]
    return u * mixed.reshape(B, S, GMLP_WIDTH)

def _wkv7_scan(r, w, k, v, a, b):
    Bn, S, H, N = r.shape
    seq = tuple(jnp.moveaxis(t, 1, 0) for t in (r, w, k, v, a, b))

    def step(state, inp):
        r_t, w_t, k_t, v_t, a_t, b_t = inp
        sa = jnp.einsum('bhvk,bhk->bhv', state, a_t)
        state = (state * w_t[:, :, None, :] + sa[..., None] * b_t[:, :, None, :]
                 + v_t[..., None] * k_t[:, :, None, :])
        return state, jnp.einsum('bhvk,bhk->bhv', state, r_t)

    s0 = jnp.zeros((Bn, H, N, N), jnp.float32)
    _, y = lax.scan(step, s0, seq)
    return jnp.moveaxis(y, 0, 1)

def _rwkv7_mixer(z, mu, w0, w2, a0, a2, g2, k_k, k_a, r_k, gn_w, gn_b):
    B, S, _ = z.shape
    f32 = jnp.float32
    z = z + (_token_shift(z) - z) * mu
    W = RWKV_WIDTH
    r, k, v, xw, xa, xg = jnp.split(
        z, [W, 2 * W, 3 * W, 3 * W + DECAY_LORA, 3 * W + DECAY_LORA + ICLR_LORA], axis=-1)
    w_log = -jax.nn.softplus(-(w0 + jnp.tanh(xw) @ w2).astype(f32)) - 0.5
    decay = jnp.exp(-jnp.exp(w_log))
    a = jax.nn.sigmoid(a0 + xa @ a2)
    g = jax.nn.sigmoid(xg) @ g2
    hv = lambda t: t.reshape(B, S, RWKV_HEADS, HEAD_DIM)
    kk = hv(k * k_k).astype(f32)
    kk = kk / jnp.maximum(jnp.sqrt(jnp.sum(kk * kk, axis=-1, keepdims=True)), 1e-12)
    k = k * (1 + (a - 1) * k_a)
    r4, k4, v4, a4 = hv(r), hv(k), hv(v), hv(a)
    y = _wkv7_scan(r4.astype(f32), hv(decay), k4.astype(f32), v4.astype(f32),
                   -kk, kk * a4.astype(f32))
    m = jnp.mean(y, axis=-1, keepdims=True)
    var = jnp.mean(jnp.square(y - m), axis=-1, keepdims=True)
    y = ((y - m) * lax.rsqrt(var + GN_EPS)).reshape(B, S, W).astype(z.dtype) * gn_w + gn_b
    bonus = jnp.sum(r4 * k4 * r_k, axis=-1, keepdims=True) * v4
    return (y + bonus.reshape(B, S, W)) * g

def _hier_moe(h, rg_w, rg_b, re_w, re_b, w_gate, w_up, w_down):
    B, S, D = h.shape
    N = B * S
    f32 = jnp.float32
    ht = h.reshape(N, D)
    group_prob = jax.nn.softmax((ht @ rg_w + rg_b).astype(f32), axis=-1)
    g_p, g_idx = lax.top_k(group_prob, 1)
    exp_logits = (ht @ re_w + re_b).astype(f32).reshape(N, N_GROUPS, EXPERTS_PER_GROUP)
    sel = jnp.take_along_axis(exp_logits, g_idx[:, :, None], axis=1)[:, 0]
    e_p, e_idx = lax.top_k(jax.nn.softmax(sel, axis=-1), TOP_K)
    e_p = e_p / jnp.sum(e_p, axis=-1, keepdims=True)
    weights = g_p * e_p
    expert = g_idx * EXPERTS_PER_GROUP + e_idx
    A = N * TOP_K
    flat_e = expert.reshape(A)
    flat_w = weights.reshape(A)
    flat_tok = jnp.repeat(jnp.arange(N, dtype=jnp.int32), TOP_K)
    order = jnp.argsort(flat_e)
    se, stok, sw = flat_e[order], flat_tok[order], flat_w[order]
    counts = jnp.bincount(flat_e, length=N_EXPERTS)
    padded = (counts + MOE_BLOCK - 1) // MOE_BLOCK * MOE_BLOCK
    pad_end = jnp.cumsum(padded)
    pad_start = pad_end - padded
    start = jnp.cumsum(counts) - counts
    dest = pad_start[se] + jnp.arange(A) - start[se]
    n_blocks = -(-A // MOE_BLOCK) + N_EXPERTS
    P = n_blocks * MOE_BLOCK
    tok_buf = jnp.full((P,), N, jnp.int32).at[dest].set(stok)
    w_buf = jnp.zeros((P,), f32).at[dest].set(sw)
    block_e = jnp.minimum(
        jnp.searchsorted(pad_end, jnp.arange(n_blocks) * MOE_BLOCK, side='right'), N_EXPERTS - 1)
    x_pad = jnp.concatenate([ht, jnp.zeros((1, D), ht.dtype)], axis=0)
    xb = x_pad[tok_buf].reshape(n_blocks, MOE_BLOCK, D)

    def expert_block(args):
        xbk, e = args
        return (jax.nn.silu(xbk @ w_gate[e]) * (xbk @ w_up[e])) @ w_down[e]

    yb = lax.map(expert_block, (xb, block_e)).reshape(P, D)
    y = jnp.zeros((N + 1, D), yb.dtype).at[tok_buf].add(yb * w_buf[:, None].astype(yb.dtype))
    return y[:N].reshape(B, S, D)

def first_inputs(seed: int = 0) -> dict:
    key = jax.random.key(seed)
    ks = jax.random.split(key, 40)
    L, D = DEPTH, D_MODEL
    nrm = lambda k, shape, s: jax.random.normal(k, shape, jnp.float32) * s
    uni = lambda k, shape, lo, hi: jax.random.uniform(k, shape, jnp.float32, lo, hi)
    return {
        "x": nrm(ks[0], (BATCH, SEQ, D), 1.0),
        "c": nrm(ks[1], (BATCH, D), 1.0),
        "ada_w": nrm(ks[2], (L, D, 6 * D), 0.3 * D ** -0.5),
        "ada_b": nrm(ks[3], (L, 6 * D), 0.01),
        "norm1_g": 1.0 + nrm(ks[4], (L, D), 0.05),
        "w_in": nrm(ks[5], (L, D, IN_WIDTH), D ** -0.5),
        "gmlp_ln_w": 1.0 + nrm(ks[6], (L, GMLP_WIDTH), 0.05),
        "gmlp_ln_b": nrm(ks[7], (L, GMLP_WIDTH), 0.02),
        "gmlp_ws": nrm(ks[8], (L, GMLP_HEADS, CHUNK, CHUNK), CHUNK ** -0.5),
        "gmlp_bs": 1.0 + nrm(ks[9], (L, GMLP_HEADS, CHUNK), 0.1),
        "rwkv_mu": uni(ks[10], (L, RWKV_PROJ), 0.0, 1.0),
        "rwkv_w0": uni(ks[11], (L, RWKV_WIDTH), -6.0, 0.0),
        "rwkv_w2": nrm(ks[12], (L, DECAY_LORA, RWKV_WIDTH), 0.1),
        "rwkv_a0": nrm(ks[13], (L, RWKV_WIDTH), 0.5),
        "rwkv_a2": nrm(ks[14], (L, ICLR_LORA, RWKV_WIDTH), ICLR_LORA ** -0.5),
        "rwkv_g2": nrm(ks[15], (L, GATE_LORA, RWKV_WIDTH), GATE_LORA ** -0.5),
        "rwkv_k_k": 0.85 + nrm(ks[16], (L, RWKV_WIDTH), 0.05),
        "rwkv_k_a": 1.0 + nrm(ks[17], (L, RWKV_WIDTH), 0.05),
        "rwkv_r_k": nrm(ks[18], (L, RWKV_HEADS, HEAD_DIM), 0.1),
        "rwkv_gn_w": 1.0 + nrm(ks[19], (L, RWKV_WIDTH), 0.05),
        "rwkv_gn_b": nrm(ks[20], (L, RWKV_WIDTH), 0.02),
        "w_out": nrm(ks[21], (L, MIX_WIDTH, D), MIX_WIDTH ** -0.5),
        "norm2_g": 1.0 + nrm(ks[22], (L, D), 0.05),
        "router_group_w": nrm(ks[23], (L, D, N_GROUPS), D ** -0.5),
        "router_group_b": nrm(ks[24], (L, N_GROUPS), 0.01),
        "router_expert_w": nrm(ks[25], (L, D, N_EXPERTS), D ** -0.5),
        "router_expert_b": nrm(ks[26], (L, N_EXPERTS), 0.01),
        "moe_w_gate": nrm(ks[27], (L, N_EXPERTS, D, EXPERT_HIDDEN), D ** -0.5),
        "moe_w_up": nrm(ks[28], (L, N_EXPERTS, D, EXPERT_HIDDEN), D ** -0.5),
        "moe_w_down": nrm(ks[29], (L, N_EXPERTS, EXPERT_HIDDEN, D), EXPERT_HIDDEN ** -0.5),
        "final_norm_g": 1.0 + nrm(ks[30], (D,), 0.05),
    }

def first_block(x, c, ada_w, ada_b, norm1_g, w_in, gmlp_ln_w, gmlp_ln_b, gmlp_ws, gmlp_bs,
              rwkv_mu, rwkv_w0, rwkv_w2, rwkv_a0, rwkv_a2, rwkv_g2, rwkv_k_k, rwkv_k_a,
              rwkv_r_k, rwkv_gn_w, rwkv_gn_b, w_out, norm2_g, router_group_w, router_group_b,
              router_expert_w, router_expert_b, moe_w_gate, moe_w_up, moe_w_down,
              final_norm_g):
    for l in range(DEPTH):
        mod = c @ ada_w[l] + ada_b[l]
        shift1, scale1, gate1, shift2, scale2, gate2 = jnp.split(mod, 6, axis=-1)
        h = _modulate(_rmsnorm(x, norm1_g[l]), shift1, scale1)
        z = h @ w_in[l]
        zu, zv, zr = jnp.split(z, [GMLP_WIDTH, 2 * GMLP_WIDTH], axis=-1)
        y_a = _gmlp_mixer(zu, zv, gmlp_ln_w[l], gmlp_ln_b[l], gmlp_ws[l], gmlp_bs[l])
        y_b = _rwkv7_mixer(zr, rwkv_mu[l], rwkv_w0[l], rwkv_w2[l], rwkv_a0[l], rwkv_a2[l],
                           rwkv_g2[l], rwkv_k_k[l], rwkv_k_a[l], rwkv_r_k[l],
                           rwkv_gn_w[l], rwkv_gn_b[l])
        y = jnp.concatenate([y_a, y_b], axis=-1) @ w_out[l]
        x = x + gate1[:, None, :] * y
        h = _modulate(_rmsnorm(x, norm2_g[l]), shift2, scale2)
        y = _hier_moe(h, router_group_w[l], router_group_b[l], router_expert_w[l],
                      router_expert_b[l], moe_w_gate[l], moe_w_up[l], moe_w_down[l])
        x = x + gate2[:, None, :] * y
    return _rmsnorm(x, final_norm_g)


DEPTH_2 = 2

PLE_DIM = 256
N_EVEN = (DEPTH_2 + 1) // 2
N_ODD = DEPTH_2 // 2
SSD_HEADS = 16
SSD_HEAD_DIM = 64
SSD_INNER = SSD_HEADS * SSD_HEAD_DIM
SSD_GROUPS = 2
SSD_HPG = SSD_HEADS // SSD_GROUPS
SSD_STATE = 128
SSD_CONV = 4
SSD_CHUNK = 128
SSD_XBC = SSD_INNER + 2 * SSD_GROUPS * SSD_STATE
SC_DIM = 1024
SC_CONV = 3
MIX_IN = SSD_INNER + SSD_XBC + SSD_HEADS + 3 * SC_DIM
MIX_OUT = SSD_INNER + SC_DIM
ATTN_HEADS = 16
ATTN_KV_HEADS = 4
ATTN_GROUP = ATTN_HEADS // ATTN_KV_HEADS
ATTN_HEAD_DIM = 64
WINDOW = 128
ATTN_BLOCK = 128
QKV_DIM = (ATTN_HEADS + 2 * ATTN_KV_HEADS) * ATTN_HEAD_DIM
D_FF = ((8 * D_MODEL + 3 * 256 - 1) // (3 * 256)) * 256
ALPHA = (2 * DEPTH_2) ** 0.25
BETA = (8 * DEPTH_2) ** -0.25
RMS_EPS_2 = 1e-5


def layer_norm(x, g, b):
    xf = x.astype(jnp.float32)
    mu = jnp.mean(xf, axis=-1, keepdims=True)
    xc = xf - mu
    var = jnp.mean(xc * xc, axis=-1, keepdims=True)
    return (xc * lax.rsqrt(var + LN_EPS) * g.astype(jnp.float32) + b.astype(jnp.float32)).astype(x.dtype)

def causal_dwconv(x, w):
    k, c = w.shape
    return lax.conv_general_dilated(
        x, w[:, None, :].astype(x.dtype), window_strides=(1,), padding=[(k - 1, 0)],
        dimension_numbers=('NWC', 'WIO', 'NWC'), feature_group_count=c)

def ssd_mixer(z, xbc, dt_raw, conv_w, conv_b, dt_bias, a_log, d_skip, norm_w):
    f32 = jnp.float32
    bsz, seqlen, _ = z.shape
    nc = seqlen // SSD_CHUNK
    xbc = jax.nn.silu(causal_dwconv(xbc, conv_w) + conv_b.astype(xbc.dtype)).astype(f32)
    xs = xbc[..., :SSD_INNER].reshape(bsz, nc, SSD_CHUNK, SSD_GROUPS, SSD_HPG, SSD_HEAD_DIM)
    bm = xbc[..., SSD_INNER:SSD_INNER + SSD_GROUPS * SSD_STATE].reshape(bsz, nc, SSD_CHUNK, SSD_GROUPS, SSD_STATE)
    cm = xbc[..., SSD_INNER + SSD_GROUPS * SSD_STATE:].reshape(bsz, nc, SSD_CHUNK, SSD_GROUPS, SSD_STATE)
    dt = jax.nn.softplus(dt_raw.astype(f32) + dt_bias.astype(f32))
    a = -jnp.exp(a_log.astype(f32))
    dt = dt.reshape(bsz, nc, SSD_CHUNK, SSD_GROUPS, SSD_HPG)
    da = dt * a.reshape(SSD_GROUPS, SSD_HPG)
    xdt = xs * dt[..., None]
    a_cs = jnp.cumsum(da, axis=2)
    seg = a_cs[:, :, :, None] - a_cs[:, :, None, :]
    causal = jnp.tril(jnp.ones((SSD_CHUNK, SSD_CHUNK), dtype=bool))[:, :, None, None]
    decay_ls = jnp.exp(jnp.where(causal, seg, -jnp.inf))
    cb = jnp.einsum('bclgn,bcsgn->bclsg', cm, bm)
    y_diag = jnp.einsum('bclsgr,bcsgrp->bclgrp', cb[..., None] * decay_ls, xdt)
    decay_to_end = jnp.exp(a_cs[:, :, -1:] - a_cs)
    chunk_states = jnp.einsum('bclgn,bclgrp->bcgrpn', bm, xdt * decay_to_end[..., None])
    chunk_decay = jnp.exp(a_cs[:, :, -1])

    def step(h, inp):
        s_c, d_c = inp
        return h * d_c[..., None, None] + s_c, h

    h0 = jnp.zeros((bsz, SSD_GROUPS, SSD_HPG, SSD_HEAD_DIM, SSD_STATE), f32)
    _, h_in = lax.scan(step, h0, (jnp.moveaxis(chunk_states, 1, 0), jnp.moveaxis(chunk_decay, 1, 0)))
    h_in = jnp.moveaxis(h_in, 0, 1)
    y_off = jnp.einsum('bclgn,bcgrpn->bclgrp', cm, h_in) * jnp.exp(a_cs)[..., None]
    y = y_diag + y_off + xs * d_skip.astype(f32).reshape(SSD_GROUPS, SSD_HPG)[:, :, None]
    y = y.reshape(bsz, seqlen, SSD_INNER) * jax.nn.silu(z.astype(f32))
    yg = y.reshape(bsz, seqlen, SSD_GROUPS, SSD_INNER // SSD_GROUPS)
    yg = yg * lax.rsqrt(jnp.mean(yg * yg, axis=-1, keepdims=True) + RMS_EPS_2)
    return (yg.reshape(bsz, seqlen, SSD_INNER) * norm_w.astype(f32)).astype(z.dtype)

def ssd_shortconv_layer_mixer(x, w_in, conv_w, conv_b, dt_bias, a_log, d_skip, norm_w, sc_conv_w, w_out):
    proj = x @ w_in
    o1 = SSD_INNER
    o2 = o1 + SSD_XBC
    o3 = o2 + SSD_HEADS
    o4 = o3 + SC_DIM
    o5 = o4 + SC_DIM
    z, xbc, dt_raw = proj[..., :o1], proj[..., o1:o2], proj[..., o2:o3]
    sc_b, sc_c, sc_h = proj[..., o3:o4], proj[..., o4:o5], proj[..., o5:]
    y_ssd = ssd_mixer(z, xbc, dt_raw, conv_w, conv_b, dt_bias, a_log, d_skip, norm_w)
    y_sc = sc_b * causal_dwconv(sc_c * sc_h, sc_conv_w)
    return jnp.concatenate([y_ssd.astype(x.dtype), y_sc.astype(x.dtype)], axis=-1) @ w_out

def sliding_window_attention(x, w_qkv, b_qkv, sinks, w_o, b_o):
    bsz, seqlen, _ = x.shape
    nb = seqlen // ATTN_BLOCK
    qkv = x @ w_qkv + b_qkv
    nq = ATTN_HEADS * ATTN_HEAD_DIM
    nkv = ATTN_KV_HEADS * ATTN_HEAD_DIM
    q = qkv[..., :nq].reshape(bsz, nb, ATTN_BLOCK, ATTN_KV_HEADS, ATTN_GROUP, ATTN_HEAD_DIM)
    k = qkv[..., nq:nq + nkv].reshape(bsz, nb, ATTN_BLOCK, ATTN_KV_HEADS, ATTN_HEAD_DIM)
    v = qkv[..., nq + nkv:].reshape(bsz, nb, ATTN_BLOCK, ATTN_KV_HEADS, ATTN_HEAD_DIM)

    def with_prev(t):
        prev = jnp.concatenate([jnp.zeros_like(t[:, :1]), t[:, :-1]], axis=1)
        return jnp.concatenate([prev, t], axis=2)

    kk = with_prev(k)
    vv = with_prev(v)
    scale = ATTN_HEAD_DIM ** -0.5
    s = jnp.einsum('bnqkgd,bnskd->bnkgqs', q, kk, preferred_element_type=jnp.float32) * scale
    n_idx = jnp.arange(nb)[:, None, None]
    q_pos = n_idx * ATTN_BLOCK + jnp.arange(ATTN_BLOCK)[None, :, None]
    k_pos = (n_idx - 1) * ATTN_BLOCK + jnp.arange(2 * ATTN_BLOCK)[None, None, :]
    rel = q_pos - k_pos
    band = (rel >= 0) & (rel < WINDOW) & (k_pos >= 0)
    s = jnp.where(band[None, :, None, None], s, -jnp.inf)
    sink = sinks.astype(jnp.float32).reshape(ATTN_KV_HEADS, ATTN_GROUP)[None, None, :, :, None, None]
    sink = jnp.broadcast_to(sink, s.shape[:-1] + (1,))
    probs = jax.nn.softmax(jnp.concatenate([s, sink], axis=-1), axis=-1)[..., :-1]
    o = jnp.einsum('bnkgqs,bnskd->bnqkgd', probs.astype(vv.dtype), vv)
    return o.reshape(bsz, seqlen, nq) @ w_o + b_o

def swiglu(x, w_gate, w_up, w_down):
    return (jax.nn.silu(x @ w_gate) * (x @ w_up)) @ w_down

def second_inputs(seed: int = 0) -> dict:
    key = jax.random.key(seed)
    ks = jax.random.split(key, 32)
    f32 = jnp.float32

    def nrm(k, shape, scale):
        return jax.random.normal(k, shape, f32) * scale

    x = nrm(ks[0], (BATCH, SEQ, D_MODEL), 1.0)
    p = nrm(ks[1], (DEPTH_2, BATCH, SEQ, PLE_DIM), 1.0)
    w_in_mix = nrm(ks[2], (N_EVEN, D_MODEL, MIX_IN), D_MODEL ** -0.5)
    ssd_conv_w = nrm(ks[3], (N_EVEN, SSD_CONV, SSD_XBC), SSD_CONV ** -0.5)
    ssd_conv_b = nrm(ks[4], (N_EVEN, SSD_XBC), 0.02)
    dt0 = jnp.exp(jax.random.uniform(ks[5], (N_EVEN, SSD_HEADS), f32, math.log(1e-3), math.log(1e-1)))
    ssd_dt_bias = dt0 + jnp.log(-jnp.expm1(-dt0))
    ssd_a_log = jnp.log(jax.random.uniform(ks[6], (N_EVEN, SSD_HEADS), f32, 1.0, 16.0))
    ssd_d = 1.0 + nrm(ks[7], (N_EVEN, SSD_HEADS), 0.1)
    ssd_norm_w = 1.0 + nrm(ks[8], (N_EVEN, SSD_INNER), 0.02)
    sc_conv_w = nrm(ks[9], (N_EVEN, SC_CONV, SC_DIM), SC_CONV ** -0.5)
    w_out_mix = nrm(ks[10], (N_EVEN, MIX_OUT, D_MODEL), BETA * MIX_OUT ** -0.5)
    w_qkv = nrm(ks[11], (N_ODD, D_MODEL, QKV_DIM), D_MODEL ** -0.5)
    b_qkv = nrm(ks[12], (N_ODD, QKV_DIM), 0.02)
    attn_sinks = nrm(ks[13], (N_ODD, ATTN_HEADS), 0.5)
    w_o = nrm(ks[14], (N_ODD, ATTN_HEADS * ATTN_HEAD_DIM, D_MODEL), BETA * (ATTN_HEADS * ATTN_HEAD_DIM) ** -0.5)
    b_o = nrm(ks[15], (N_ODD, D_MODEL), 0.02)
    ln_mix_g = 1.0 + nrm(ks[16], (DEPTH_2, D_MODEL), 0.02)
    ln_mix_b = nrm(ks[17], (DEPTH_2, D_MODEL), 0.02)
    w_ffn_gate = nrm(ks[18], (DEPTH_2, D_MODEL, D_FF), D_MODEL ** -0.5)
    w_ffn_up = nrm(ks[19], (DEPTH_2, D_MODEL, D_FF), D_MODEL ** -0.5)
    w_ffn_down = nrm(ks[20], (DEPTH_2, D_FF, D_MODEL), BETA * D_FF ** -0.5)
    ln_ffn_g = 1.0 + nrm(ks[21], (DEPTH_2, D_MODEL), 0.02)
    ln_ffn_b = nrm(ks[22], (DEPTH_2, D_MODEL), 0.02)
    w_ple = nrm(ks[23], (DEPTH_2, PLE_DIM, D_MODEL), PLE_DIM ** -0.5)
    w_ple_gate = nrm(ks[24], (DEPTH_2, D_MODEL, D_MODEL), D_MODEL ** -0.5)
    b_ple_gate = nrm(ks[25], (DEPTH_2, D_MODEL), 0.02)
    return {'x': x, 'p': p, 'w_in_mix': w_in_mix, 'ssd_conv_w': ssd_conv_w, 'ssd_conv_b': ssd_conv_b,
            'ssd_dt_bias': ssd_dt_bias, 'ssd_a_log': ssd_a_log, 'ssd_d': ssd_d, 'ssd_norm_w': ssd_norm_w,
            'sc_conv_w': sc_conv_w, 'w_out_mix': w_out_mix, 'w_qkv': w_qkv, 'b_qkv': b_qkv,
            'attn_sinks': attn_sinks, 'w_o': w_o, 'b_o': b_o, 'ln_mix_g': ln_mix_g, 'ln_mix_b': ln_mix_b,
            'w_ffn_gate': w_ffn_gate, 'w_ffn_up': w_ffn_up, 'w_ffn_down': w_ffn_down,
            'ln_ffn_g': ln_ffn_g, 'ln_ffn_b': ln_ffn_b, 'w_ple': w_ple, 'w_ple_gate': w_ple_gate,
            'b_ple_gate': b_ple_gate}

def second_block(x, p, w_in_mix, ssd_conv_w, ssd_conv_b, ssd_dt_bias, ssd_a_log, ssd_d, ssd_norm_w,
              sc_conv_w, w_out_mix, w_qkv, b_qkv, attn_sinks, w_o, b_o, ln_mix_g, ln_mix_b,
              w_ffn_gate, w_ffn_up, w_ffn_down, ln_ffn_g, ln_ffn_b, w_ple, w_ple_gate, b_ple_gate):
    for i in range(DEPTH_2):
        j = i // 2
        if i % 2 == 0:
            mix = ssd_shortconv_layer_mixer(x, w_in_mix[j], ssd_conv_w[j], ssd_conv_b[j], ssd_dt_bias[j],
                                            ssd_a_log[j], ssd_d[j], ssd_norm_w[j], sc_conv_w[j], w_out_mix[j])
        else:
            mix = sliding_window_attention(x, w_qkv[j], b_qkv[j], attn_sinks[j], w_o[j], b_o[j])
        x = layer_norm(ALPHA * x + mix.astype(x.dtype), ln_mix_g[i], ln_mix_b[i])
        x = layer_norm(ALPHA * x + swiglu(x, w_ffn_gate[i], w_ffn_up[i], w_ffn_down[i]), ln_ffn_g[i], ln_ffn_b[i])
        gate = jax.nn.sigmoid(x @ w_ple_gate[i] + b_ple_gate[i])
        x = x + (p[i] @ w_ple[i]) * gate
    return x


def setup_inputs(seed=0):
    out = dict(first_inputs(seed))
    for name, value in second_inputs(seed + 1).items():
        if name != "x":
            out[name + "_2"] = value
    return out


def reference(
    x, c, ada_w, ada_b, norm1_g, w_in, gmlp_ln_w, gmlp_ln_b, gmlp_ws, gmlp_bs, rwkv_mu, rwkv_w0,
    rwkv_w2, rwkv_a0, rwkv_a2, rwkv_g2, rwkv_k_k, rwkv_k_a, rwkv_r_k, rwkv_gn_w, rwkv_gn_b,
    w_out, norm2_g, router_group_w, router_group_b, router_expert_w, router_expert_b,
    moe_w_gate, moe_w_up, moe_w_down, final_norm_g, p_2, w_in_mix_2, ssd_conv_w_2, ssd_conv_b_2,
    ssd_dt_bias_2, ssd_a_log_2, ssd_d_2, ssd_norm_w_2, sc_conv_w_2, w_out_mix_2, w_qkv_2,
    b_qkv_2, attn_sinks_2, w_o_2, b_o_2, ln_mix_g_2, ln_mix_b_2, w_ffn_gate_2, w_ffn_up_2,
    w_ffn_down_2, ln_ffn_g_2, ln_ffn_b_2, w_ple_2, w_ple_gate_2, b_ple_gate_2,
):
    x = first_block(
        x, c, ada_w, ada_b, norm1_g, w_in, gmlp_ln_w, gmlp_ln_b, gmlp_ws, gmlp_bs, rwkv_mu,
        rwkv_w0, rwkv_w2, rwkv_a0, rwkv_a2, rwkv_g2, rwkv_k_k, rwkv_k_a, rwkv_r_k, rwkv_gn_w,
        rwkv_gn_b, w_out, norm2_g, router_group_w, router_group_b, router_expert_w,
        router_expert_b, moe_w_gate, moe_w_up, moe_w_down, final_norm_g,
    )
    return second_block(
        x, p_2, w_in_mix_2, ssd_conv_w_2, ssd_conv_b_2, ssd_dt_bias_2, ssd_a_log_2, ssd_d_2,
        ssd_norm_w_2, sc_conv_w_2, w_out_mix_2, w_qkv_2, b_qkv_2, attn_sinks_2, w_o_2, b_o_2,
        ln_mix_g_2, ln_mix_b_2, w_ffn_gate_2, w_ffn_up_2, w_ffn_down_2, ln_ffn_g_2, ln_ffn_b_2,
        w_ple_2, w_ple_gate_2, b_ple_gate_2,
    )


_drawn_inputs = setup_inputs


def setup_inputs(seed=0):
    import zlib

    import numpy as np

    out = dict(_drawn_inputs(seed))
    spreads = {}
    factors = {'ada_b': 4.974,
     'norm1_g': 3.462,
     'gmlp_ln_w': 7.621,
     'gmlp_ln_b': 29.05,
     'gmlp_bs': 3.46,
     'rwkv_w2': 6.962,
     'rwkv_a0': 2.727,
     'rwkv_k_k': 26.138,
     'rwkv_k_a': 5.449,
     'rwkv_gn_w': 27.071,
     'rwkv_gn_b': 46.335,
     'norm2_g': 3.524,
     'router_group_b': 8.0,
     'router_expert_b': 22.628,
     'ssd_conv_b_2': 8.0,
     'ssd_d_2': 4.399,
     'ssd_norm_w_2': 29.595,
     'b_qkv_2': 8.0,
     'attn_sinks_2': 8.0,
     'b_o_2': 5.052,
     'b_ple_gate_2': 8.0}
    for name, (base, spread) in spreads.items():
        noise = np.random.default_rng([zlib.crc32(name.encode()), seed]).standard_normal(out[name].shape)
        drawn = base * np.exp(spread * noise) if base else spread * noise
        out[name] = jnp.asarray(drawn.astype(out[name].dtype))
    for name, factor in factors.items():
        out[name] = (out[name] * factor).astype(out[name].dtype)
    return out
```

```python
from contextlib import ExitStack

import numpy as np

import concourse.bass as bass
from concourse import mybir

ALU = mybir.AluOpType
ACT = mybir.ActivationFunctionType
AX = mybir.AxisListType
F32 = mybir.dt.float32
I32 = mybir.dt.int32

P = 128
SEQ = 512
D = 1024
KT = D // P
NCH = SEQ // P
HD = 64
LEVELS = 7
RING = 8
UNIT = 2048
N_EXP = 32
N_GRP = 4
EPG = N_EXP // N_GRP
HID = 512
CAP = 128
MAX_OVER = 7
SPLIT = SEQ // CAP
FF = 2816
ALPHA = 4 ** 0.25
NEG = -1e30
N_ATT = NCH * 8


Q_HEADS = [(2 * m + o) * 4 + g for m in range(2) for g in range(4) for o in range(2)]
Q_CHANNELS = np.array([h * HD + d for h in Q_HEADS for d in range(HD)])


def chan(v):
    v = np.asarray(v).reshape(-1)
    n = -(-v.size // P)
    out = np.zeros((n * P,), v.dtype)
    out[: v.size] = v
    return out.reshape(n, P).T


def every(v):
    v = np.asarray(v).reshape(-1)
    return np.broadcast_to(v, (P, v.size))


def rows(w, k0, nk, cols):
    w = np.asarray(w)[k0 * P:(k0 + nk) * P][:, cols]
    return w.reshape(nk, P, -1).transpose(1, 0, 2)


MU = [("mu_r", 0, 512), ("mu_k", 512, 1024), ("mu_v", 1024, 1536), ("mu_xw", 1536, 1568),
      ("mu_xa", 1568, 1600), ("mu_xg", 1600, 1696)]
PARAMS = [
    ("c", 8, lambda a: chan(a["c"])), ("ada_b", 48, lambda a: chan(a["ada_b"][0])),
    ("norm1_g", 8, lambda a: chan(a["norm1_g"][0])), ("norm2_g", 8, lambda a: chan(a["norm2_g"][0])),
    ("final_g", 8, lambda a: chan(a["final_norm_g"])),
] + [(n, -(-(hi - lo) // P), lambda a, lo=lo, hi=hi: chan(a["rwkv_mu"][0][lo:hi])) for n, lo, hi in MU] + [
    (n, 4, lambda a, key=key: chan(a[key][0]))
    for n, key in [("w0", "rwkv_w0"), ("a0", "rwkv_a0"), ("k_k", "rwkv_k_k"), ("k_a", "rwkv_k_a"),
                   ("r_k", "rwkv_r_k"), ("gn_w", "rwkv_gn_w"), ("gn_b", "rwkv_gn_b")]
] + [
    ("conv_w", 48, lambda a: np.concatenate([chan(a["ssd_conv_w_2"][0][t]) for t in range(4)], 1)),
    ("conv_b", 12, lambda a: chan(a["ssd_conv_b_2"][0])),
    ("sc_w", 24, lambda a: np.concatenate([chan(a["sc_conv_w_2"][0][t]) for t in range(3)], 1)),
    ("d_skip", 8, lambda a: chan(np.repeat(np.asarray(a["ssd_d_2"][0]), HD))),
    ("ssd_nw", 8, lambda a: chan(a["ssd_norm_w_2"][0])),
    ("dt_b", 1, lambda a: chan(a["ssd_dt_bias_2"][0])), ("a_log", 1, lambda a: chan(a["ssd_a_log_2"][0])),
    ("ln_mix_g", 16, lambda a: chan(a["ln_mix_g_2"])), ("ln_mix_b", 16, lambda a: chan(a["ln_mix_b_2"])),
    ("ln_ffn_g", 16, lambda a: chan(a["ln_ffn_g_2"])), ("ln_ffn_b", 16, lambda a: chan(a["ln_ffn_b_2"])),
    ("b_q", 8, lambda a: chan(np.asarray(a["b_qkv_2"][0])[Q_CHANNELS])),
    ("b_k", 2, lambda a: chan(a["b_qkv_2"][0][1024:1280])),
    ("b_o", 8, lambda a: chan(a["b_o_2"][0])), ("b_ple", 16, lambda a: chan(a["b_ple_gate_2"])),
    ("router_w", 288, lambda a: np.concatenate(
        [rows(a["router_group_w"][0], 0, 8, slice(None)), rows(a["router_expert_w"][0], 0, 8, slice(None))], 2)),
    ("router_b", 36, lambda a: every(np.concatenate([a["router_group_b"][0], a["router_expert_b"][0]]))),
    ("b_v", 256, lambda a: every(a["b_qkv_2"][0][1280:1536])),
    ("sinks", 16, lambda a: every(np.asarray(a["attn_sinks_2"][0])[Q_HEADS])),
]
PCOL, _n = {}, 0
for _name, _width, _ in PARAMS:
    PCOL[_name] = (_n, _width)
    _n += _width
N_PAR = _n


def cols(lo, hi):
    return slice(lo, hi)


def dense_plan():
    plan = []

    def unit(group, nk, nc, fill):
        plan.append((group, nk, nc, fill))

    def mat(group, key, layer, columns, k0=0, nk=KT):
        n = len(range(*columns.indices(1 << 20))) if isinstance(columns, slice) else len(columns)
        unit(group, nk, n, lambda a: rows(a[key][layer], k0, nk, columns))

    for j in range(24):
        mat(("ada", j), "ada_w", 0, cols(256 * j, 256 * j + 256))
    for h in range(2):
        mat(("zv",), "w_in", 0, cols(512, 1024), 4 * h, 4)
    for name, lo in (("zu", 0), ("r", 1024), ("k", 1536), ("v", 2048)):
        for j in range(2):
            mat((name, j), "w_in", 0, cols(lo + 256 * j, lo + 256 * j + 256))
    mat(("lora_wa",), "w_in", 0, cols(2560, 2624))
    mat(("lora_g",), "w_in", 0, cols(2624, 2720))

    def gm1(a):
        ws = np.asarray(a["gmlp_ws"][0]).transpose(2, 0, 1).reshape(P, 1024)
        return np.concatenate([ws, every(a["gmlp_ln_w"][0]), every(a["gmlp_ln_b"][0])], 1)

    def gm2(a):
        out = np.zeros((P, 4, 512), np.float32)
        bs = np.asarray(a["gmlp_bs"][0])
        for j in range(4):
            for o in range(2):
                out[64 * o:64 * o + 64, 0, P * j:P * j + P] = bs[2 * j + o]
        out[0:32, 1] = np.asarray(a["rwkv_w2"][0])
        out[0:32, 2] = np.asarray(a["rwkv_a2"][0])
        out[0:96, 3] = np.asarray(a["rwkv_g2"][0])
        return out

    unit(("gm1",), 1, UNIT, gm1)
    unit(("gm2",), 4, 512, gm2)
    for j in range(4):
        mat(("w_out", j), "w_out", 0, cols(256 * j, 256 * j + 256))
    n_first = len(plan)

    for j in range(8):
        mat(("sc_ch", j), "w_in_mix_2", 0,
            np.r_[3600 + P * j:3728 + P * j, 4624 + P * j:4752 + P * j])
    for j in range(4):
        mat(("sc_b", j), "w_in_mix_2", 0, cols(2576 + 256 * j, 2832 + 256 * j))
    for j in range(6):
        mat(("xbc", j), "w_in_mix_2", 0, cols(1024 + 256 * j, 1280 + 256 * j))
    mat(("dt",), "w_in_mix_2", 0, cols(2560, 2576))
    for j in range(4):
        mat(("z", j), "w_in_mix_2", 0, cols(256 * j, 256 * j + 256))
    for j in range(4):
        for h in range(2):
            mat(("mix_out", j), "w_out_mix_2", 0, cols(256 * j, 256 * j + 256), 8 * h)

    def ffn(layer):
        for j in range(22):
            unit(("gu", layer, j), KT, 256, lambda a, j=j: np.concatenate(
                [rows(a["w_ffn_gate_2"][layer], 0, 8, cols(P * j, P * j + P)),
                 rows(a["w_ffn_up_2"][layer], 0, 8, cols(P * j, P * j + P))], 2))
        for j in range(4):
            for k0, nk in ((0, 8), (8, 8), (16, 6)):
                mat(("down", layer, j), "w_ffn_down_2", layer, cols(256 * j, 256 * j + 256), k0, nk)
        for j in range(4):
            mat(("ple_g", layer, j), "w_ple_gate_2", layer, cols(256 * j, 256 * j + 256))
        for j in range(4):
            mat(("ple_w", layer, j), "w_ple_2", layer, cols(256 * j, 256 * j + 256), 0, 2)

    ffn(0)
    for j in range(4):
        mat(("q", j), "w_qkv_2", 0, Q_CHANNELS[256 * j:256 * j + 256])
    mat(("kk",), "w_qkv_2", 0, cols(1024, 1280))
    mat(("vv",), "w_qkv_2", 0, cols(1280, 1536))
    for j in range(4):
        unit(("wo", j), KT, 256, lambda a, j=j: rows(
            np.asarray(a["w_o_2"][0])[Q_CHANNELS], 0, 8, cols(256 * j, 256 * j + 256)))
    ffn(1)
    return plan, n_first


PLAN, N_FIRST = dense_plan()
MOE_UNITS = 6 * N_EXP
UNIT_NO = [n if n < N_FIRST else n + MOE_UNITS for n in range(len(PLAN))]
UNITS_OF = {}
for _i, (_g, _nk, _nc, _) in enumerate(PLAN):
    UNITS_OF.setdefault(_g, []).append((UNIT_NO[_i], _nk, _nc))
GROUPS = [g for g in dict.fromkeys(p[0] for p in PLAN) if g[0] not in ("ada", "zv", "gm1", "gm2")]
GROUPS = [("zv", 0), ("zv", 1)] + GROUPS
GROUP_NO = {g: i for i, g in enumerate(GROUPS)}


def aux_plan():
    a = [("ss", 1), ("mod",)]
    a += [("wl", j) for j in range(4)] + [("al", j) for j in range(4)]
    a += [("kn", j) for j in range(4)] + [("bon", j) for j in range(4)]
    a += [("gm", c) for c in range(4)]
    for c in range(NCH):
        a += [("bt", c), ("kt", c), ("vt", c)]
        a += [("ab", c, q) for q in range(4)] + [("ak", c, q) for q in range(4)]
        for lv in range(LEVELS):
            a += [("u", c, lv, q) for q in range(2)]
            if lv > 0:
                if lv < LEVELS - 1:
                    a += [("xn", c, lv, q) for q in range(2)]
                a += [("xt", c, lv, q) for q in range(2)]
        a += [("u0", c), ("sa", c), ("y", c)] + ([("st", c)] if c < NCH - 1 else [])
    a += [("gnm", j) for j in range(4)] + [("gnv", j) for j in range(4)] + [("gg", j) for j in range(4)]
    a += [("ss", 2), ("lg",), ("rank",)] + [("ht", m, h) for m in range(4) for h in range(2)] + [("idx",)]
    a += [("comb", m, h) for m in range(4) for h in range(2)] + [("ss", 3)]
    a += [("da_t",), ("last",)]
    a += [("bct", c) for c in range(4)] + [("xst", c, h) for c in range(4) for h in range(2)]
    a += [("cb", g) for g in range(2)]
    a += [("stt", c, g) for c in range(3) for g in range(2)]
    a += [("acs", 0), ("acs", 1)]
    for j in range(8):
        a += [("acs", h) for h in (2 * j + 2, 2 * j + 3) if h < 16] + [("yd", j)]
    a += [("gss", g) for g in range(2)]
    for layer in range(2):
        if layer == 1:
            for i in range(N_ATT + 3):
                a += [("sc", i)] if i < N_ATT else []
                a += [("pt", i - 2)] if 2 <= i < N_ATT + 2 else []
                a += [("pv", i - 3)] if i >= 3 else []
        for which in ("mix", "ffn"):
            a += [("lnm", which, layer), ("lnv", which, layer)]
    return a


AUX = aux_plan()
AUX_NO = {name: i for i, name in enumerate(AUX)}
assert len(AUX_NO) == len(AUX)



class Named:

    def __init__(self, nc, ctx):
        self.nc, self.ctx, self.made = nc, ctx, {}

    def __call__(self, name):
        if name not in self.made:
            self.made[name] = self.ctx.enter_context(self.nc.semaphore(name))
        return self.made[name]


class Steps:

    def __init__(self, eng, sem):
        self.eng, self.sem, self.n = eng, sem, 0

    def __call__(self, ins):
        self.n += 1
        ins.then_inc(self.sem, 1)
        self.eng.wait_ge(self.sem, self.n)


def last_unit(group):
    return UNITS_OF[group][-1][0]


def build(nc, x_t, params, w_dense, p_t, moe_gate, moe_up, moe_down, out_t, stop=None):
    ctx = ExitStack()
    with ctx:
        def sb(name, cols_, dt=F32):
            return ctx.enter_context(nc.sbuf_tensor(name, [P, cols_], dt))

        sem = Named(nc, ctx)
        ring = sb("ring", RING * UNIT)
        par = sb("par", N_PAR)
        masks = sb("masks", 12 * P)
        reset = sb("reset", SEQ)
        mod = sb("mod", 48)
        gain = sb("gain", 64)
        arena = sb("arena", 33600)
        psD = ctx.enter_context(nc.psum_tensor("psD", [P, 2, 2, 512], F32))
        psA = ctx.enter_context(nc.psum_tensor("psA", [P, 4, 512], F32))

        ident, ones, blk = (masks[:, P * i:P * i + P] for i in range(3))
        strict_u = masks[:, 3 * P:4 * P]
        pair = masks[:, 3 * P:5 * P].rearrange("p (a t) -> p a t", a=2)
        level = [masks[:, (5 + i) * P:(6 + i) * P] for i in range(LEVELS)]

        def pc(name, j=None, n=1):
            lo, w = PCOL[name]
            return par[:, lo:lo + w] if j is None else par[:, lo + j:lo + j + n]

        def flat(lo, n):
            return arena[:, lo:lo + n]

        def area(lo, tiles):
            return arena[:, lo:lo + tiles * SEQ].rearrange("p (k t) -> p k t", k=tiles)

        X, H, YC = area(0, 8), area(4096, 8), area(8192, 8)
        XF, HF, YF = flat(0, 4096), flat(4096, 4096), flat(8192, 4096)
        o = 12288
        R, K, V, KK, A, C, E = (area(o + 2048 * i, 4) for i in range(7))
        RF, KF, VF, KKF, AF, CF, EF = (flat(o + 2048 * i, 2048) for i in range(7))
        LO = area(o + 14336, 3)
        sp = o + 14336 + 1536
        BTK, KTK, VTK, UU, SAS = (flat(sp + 512 * i, 512) for i in range(5))
        ST, T2 = flat(sp + 2560, 512), flat(sp + 3072, 512)
        VTOK = area(sp + 2816, 4)
        T1 = area(sp + 1536, 1)
        small = flat(sp + 4864, 512)
        AR = HF.rearrange("p (j c a t) -> p j c a t", j=4, c=4, a=2)

        def ring_of(u, nk, nco):
            lo = (u % RING) * UNIT
            return ring[:, lo:lo + nk * nco].rearrange("p (k n) -> p k n", k=nk)

        def bank(name):
            return psA[:, AUX_NO[name] % 4, :]

        def dbank(group):
            return psD[:, GROUP_NO[group] % 2, :, :]

        def ready(eng, name):
            eng.wait_ge(sem("aux_ready"), AUX_NO[name] + 1)

        def freed(name):
            return sem(f"aux_free{AUX_NO[name] % 4}")

        def group_ready(eng, group):
            if group == ("zv", 0):
                eng.wait_ge(sem("zv_first"), 1)
            else:
                eng.wait_ge(sem("units_done"), last_unit(("zv",) if group[0] == "zv" else group) + 1)

        def group_freed(group):
            return sem(f"pair_free{GROUP_NO[group] % 2}")

        def loaded(eng, u):
            eng.wait_ge(sem(f"ring_full{u % RING}"), 16 * (u // RING + 1))

        LORAS = [(("lora_wa",), 0, 32, 0), (("lora_wa",), 1, 32, 1), (("lora_g",), 0, 96, 2)]
        VTMP = flat(sp + 2816, 2048)
        LM, UI = CF[:, 0:1024], CF[:, 1024:2048]
        XI, XT = EF[:, 0:1024], EF[:, 1024:2048]
        AB = RF.rearrange("p (h a t) -> p h a t", h=8, a=2)
        AK = KKF.rearrange("p (h a t) -> p h a t", h=8, a=2)

        BLOCKS = N_EXP + MAX_OVER
        row_token = nc.dram_tensor("row_token", (BLOCKS * CAP, 1), F32, kind="Internal").ap()
        token_rows = nc.dram_tensor("token_rows", (SEQ, D), F32, kind="Internal").ap()
        block_out = nc.dram_tensor("block_out", (BLOCKS * CAP, D), F32, kind="Internal").ap()
        spare = nc.dram_tensor("spare", (2, P), F32, kind="Internal").ap()
        ints = ctx.enter_context(nc.sbuf_tensor("ints", [P, 64], I32))
        idx = ints[:, 0:BLOCKS]
        pos_i = ints[:, 40:48]
        over_i = ints[:, 48:56]

        MB = 8192
        HT = flat(MB, 4096).rearrange("p (m d) -> p m d", m=4)
        msmall = flat(MB + 4096, 2560)
        at = [0]

        def take_small(n, *shape):
            lo = at[0]
            at[0] += n
            v = msmall[:, lo:lo + n]
            if len(shape) == 2:
                return v.rearrange("p (a b) -> p a b", a=shape[0])
            if len(shape) == 3:
                return v.rearrange("p (a b c) -> p a b c", a=shape[0], b=shape[1])
            return v
        LG, GD, GE, GV, OHG = (take_small(n, 4, n // 4) for n in (144, 16, 16, 16, 16))
        GM, GP, GS, M1, M2, E2, W1, W2, T4 = (take_small(4, 4, 1) for _ in range(9))
        SEL, D1, V8, OH1, SEL2, OH2 = (take_small(32, 4, 8) for _ in range(6))
        TMP = take_small(128, 4, 8, 4)
        OHA, OHB = take_small(128, 4, 4, 8), take_small(128, 4, 4, 8)
        OHS, RK, QQ, TA, TB = (take_small(128, 4, 32) for _ in range(5))
        CNT, OVB, INC, BAS, ONE = (take_small(32) for _ in range(5))
        POS, EO = take_small(8, 2, 4), take_small(8)
        DESC = take_small(8)
        EID, TOK = take_small(32), take_small(4)
        ZERO, TSB = take_small(P), take_small(P)

        XG = [flat(MB + 6656 + 1024 * i, 1024) for i in range(2)]
        XE = [flat(MB + 8704 + 1024 * i, 1024) for i in range(2)]
        SG, HB, HTE = (flat(MB + 10752 + 512 * i, 512) for i in range(3))
        YS = [flat(MB + 12288 + 1024 * i, 1024) for i in range(2)]
        YG = [flat(MB + 14336 + 1024 * i, 1024) for i in range(4)]
        gate_bank, up_bank, y_banks = psD[:, 0, 0, :], psD[:, 0, 1, :], psD[:, 1, :, :]
        x_banks, h_bank = psA[:, 0:2, :], psA[:, 2, :]
        U0 = N_FIRST

        def bc(ap, shape, axis):
            return ap.unsqueeze(axis).to_broadcast(shape)

        def expert_unit(e, j, tile):
            if j < 4:
                w = moe_gate if j < 2 else moe_up
                k0 = (j % 2) * 4 * P
                src = w[e, k0:k0 + 4 * P, :].rearrange("e (k p) n -> p (e k) n", p=P)
                return tile.rearrange("p (k n) -> p k n", k=4), src
            k0 = (j - 4) * 2 * P
            src = moe_down[e, k0:k0 + 2 * P, :].rearrange("e (k p) n -> p (e k) n", p=P)
            return tile.rearrange("p (k n) -> p k n", k=2), src

        def slot_tile(s):
            return ring[:, s * UNIT:(s + 1) * UNIT]

        def moe_sync(sp_):
            with sp_.Fori(0, N_EXP // 4) as i:
                for s in range(4):
                    for j in range(6):
                        u0 = U0 + 6 * s + j
                        sp_.wait_ge(sem("units_done"), i * 24 + (u0 - RING + 1))
                        sp_.wait_ge(sem("x_in"), 16)
                        dst, src = expert_unit(bass.ds(i * 4 + s, 1), j, slot_tile(u0 % RING))
                        sp_.dma_start(dst, src).then_inc(sem(f"ring_full{u0 % RING}"), 16)
            sp_.wait_ge(sem("units_done"), U0 + MOE_UNITS)
            sp_.wait_ge(sem("pos_ready"), 1)
            n_over = sp_.value_load(over_i[0:1, 7:8], min_val=0, max_val=MAX_OVER)
            with sp_.If(n_over > 0):
                for b in range(MAX_OVER):
                    ex = sp_.value_load(over_i[0:1, b:b + 1], min_val=0, max_val=N_EXP - 1)
                    for j in range(6):
                        dst, src = expert_unit(bass.ds(ex, 1), j, slot_tile(j))
                        sp_.dma_start(dst, src).then_inc(sem("o_weights"), 16)
                    sp_.wait_ge(sem("o_stored"), (b + 1) * 16)

        def moe_pool(pool, step):
            pool.wait_ge(sem("moe_start"), 1)
            step(pool.iota(TOK, [[P, 4]], base=0, channel_multiplier=1, allow_small_or_imprecise_dtypes=True))
            step(pool.iota(EID, [[1, 32]], base=0, channel_multiplier=0, allow_small_or_imprecise_dtypes=True))
            step(pool.iota(DESC, [[-1, 8]], base=8, channel_multiplier=0, allow_small_or_imprecise_dtypes=True))
            step(pool.memset(ONE, 1.0))
            step(pool.memset(ZERO, 0.0))
            step(pool.memset(YG[0], 0.0))
            pool.nop().then_inc(sem("moe_consts"), 1)
            for b in range(N_EXP, BLOCKS):
                pool.dma_start(block_out[b * CAP:(b + 1) * CAP, :], YG[0]).then_inc(sem("blocks_zero"), 16)
            table = row_token.rearrange("(b p) a -> b (p a)", p=CAP)
            pool.dma_start(table, ZERO[0:BLOCKS, :]).then_inc(sem("table_zero"), 16)
            pool.wait_ge(sem("table_zero"), 16)
            pool.wait_ge(sem("pos_ready"), 1)
            for ch in range(2):
                for m in range(4):
                    pool.indirect_dma_start(
                        row_token, bass.IndirectOffsetOnAxis(ap=pos_i[:, 4 * ch + m:4 * ch + m + 1], axis=0),
                        TOK[:, m:m + 1], None).then_inc(sem("table_set"), 16)
            pool.wait_ge(sem("table_set"), 128)
            pool.dma_start(TSB[0:BLOCKS, :], table).then_inc(sem("table_in"), 16)
            pool.wait_ge(sem("idx_ready"), 1)
            pool.wait_ge(sem("rows_out"), 16 * 4)

            for e in range(2):
                pool.indirect_dma_start(XG[e], None, token_rows,
                                        bass.IndirectOffsetOnAxis(ap=idx[:, e:e + 1], axis=0))\
                    .then_inc(sem(f"xg_in{e}"), 16)
            for e in range(2, N_EXP + 2):
                buf = e % 2
                pool.wait_ge(sem("xt_ready"), e - 1)
                pool.indirect_dma_start(XG[buf], None, token_rows,
                                        bass.IndirectOffsetOnAxis(ap=idx[:, e:e + 1], axis=0))\
                    .then_inc(sem(f"xg_in{buf}"), 16)
            n_over = pool.value_load(over_i[0:1, 7:8], min_val=0, max_val=MAX_OVER)
            for b_ in range(2):
                pool.wait_ge(sem(f"xg_in{b_}"), 16 * (N_EXP // 2 + 1))
            pool.wait_ge(sem("xt_ready"), N_EXP + 1)
            with pool.If(n_over > 0):
                for b in range(MAX_OVER):
                    pool.indirect_dma_start(XG[0], None, token_rows,
                                            bass.IndirectOffsetOnAxis(ap=idx[:, N_EXP + b:N_EXP + b + 1], axis=0))\
                        .then_inc(sem("o_x"), 16)
                    pool.wait_ge(sem("o_stored"), (b + 1) * 16)
            pool.wait_ge(sem("blocks_zero"), 16 * MAX_OVER)
            pool.wait_ge(sem("blocks_out"), 1)
            for m in range(4):
                for ch in range(2):
                    if m >= 2:
                        pool.wait_ge(sem("combined"), m - 1)
                    pool.indirect_dma_start(
                        YG[2 * (m % 2) + ch], None, block_out,
                        bass.IndirectOffsetOnAxis(ap=pos_i[:, 4 * ch + m:4 * ch + m + 1], axis=0))\
                        .then_inc(sem(f"y_in{m % 2}"), 16)

        def moe_act(act, step, root):
            act.wait_ge(sem("moe_start"), 1)
            act.activation(YF, XF, ACT.Square).then_inc(sem("sq2"), 1)
            root(small[:, :])
            for k in range(KT):
                act.wait_ge(sem("xn2"), k + 1)
                act.activation(H[:, k, :], H[:, k, :], ACT.Identity, bias=mod[:, 24 + k:25 + k])\
                   .then_inc(sem("h2"), 1)
            for b in range(2):
                act.dma_start(spare[b:b + 1, :], ident[0:1, :]).then_inc(sem(f"y_stored{b}"), 16)
            act.wait_ge(sem("gd"), 1)
            act.activation(GE, GD, ACT.Exp).then_inc(sem("ge"), 1)
            act.wait_ge(sem("e2_in"), 1)
            act.activation(E2, E2, ACT.Exp).then_inc(sem("e2"), 1)
            for m in range(4):
                for h in range(2):
                    n_ = ("ht", m, h)
                    ready(act, n_)
                    act.activation(HT[:, m, 512 * h:512 * h + 512], bank(n_), ACT.Copy).then_inc(freed(n_), 1)
                    act.wait_ge(freed(n_), AUX_NO[n_] // 4 + 1)
                act.dma_start(token_rows[P * m:P * m + P, :], HT[:, m, :]).then_inc(sem("rows_out"), 16)

            def x_copy(count, buf):
                act.wait_ge(sem("xt_ready"), count)
                act.activation(XE[buf], x_banks, ACT.Copy).then_inc(sem("xt_copied"), 1)

            act.wait_ge(sem("idx_ready"), 1)
            x_copy(1, 0)
            with act.Fori(0, N_EXP // 4) as i:
                for s in range(4):
                    e = i * 4 + (s + 1)
                    act.wait_ge(sem("units_done"), i * 24 + (U0 + 6 * s + 2))
                    act.wait_ge(sem("h_done"), e)
                    act.activation(SG, gate_bank, ACT.Silu).then_inc(sem("silu_done"), 1)
                    x_copy(i * 4 + (s + 2), (s + 1) % 2)
                    act.wait_ge(sem("units_done"), i * 24 + (U0 + 6 * s + 6))
                    act.wait_ge(sem(f"y_stored{s % 2}"), (i * 2 + (s // 2 + 1)) * 16)
                    act.activation(YS[s % 2][:, 0:512], y_banks[:, 0, :], ACT.Copy).then_inc(sem("y_half_a"), 1)
                    act.wait_ge(sem("y_half_a"), e)
                    act.wait_ge(sem("y_half_b"), e)
                    act.dma_start(block_out.rearrange("(b p) d -> b p d", p=CAP)[bass.ds(i * 4 + s, 1), :, :]
                                  .rearrange("b p d -> p (b d)"), YS[s % 2])\
                       .then_inc(sem(f"y_stored{s % 2}"), 16)
            for b in range(2):
                act.wait_ge(sem(f"y_stored{b}"), 16 * (N_EXP // 2 + 1))
            act.wait_ge(sem("blocks_zero"), 16 * MAX_OVER)
            n_over = act.value_load(over_i[0:1, 7:8], min_val=0, max_val=MAX_OVER)
            with act.If(n_over > 0):
                with act.Fori(0, MAX_OVER) as b:
                    act.wait_ge(sem("o_xt"), b + 1)
                    act.activation(XE[0], x_banks, ACT.Copy).then_inc(sem("o_xe"), 1)
                    act.wait_ge(sem("o_gu"), b + 1)
                    act.activation(SG, gate_bank, ACT.Silu).then_inc(sem("o_sg"), 1)
                    act.wait_ge(sem("o_y"), b + 1)
                    act.activation(YS[0], y_banks, ACT.Copy).then_inc(sem("o_ys"), 1)
                    act.wait_ge(sem("o_ys"), b + 1)
                    act.dma_start(block_out.rearrange("(b p) d -> b p d", p=CAP)[bass.ds(b + N_EXP, 1), :, :]
                                  .rearrange("b p d -> p (b d)"), YS[0]).then_inc(sem("o_stored"), 16)
                    act.wait_ge(sem("o_stored"), (b + 1) * 16)
            act.nop().then_inc(sem("blocks_out"), 1)
            act.wait_ge(sem("x_moe"), 8)
            act.activation(HF, XF, ACT.Square).then_inc(sem("sq3"), 1)
            root(small[:, :])

        def moe_vector(dve, step, take, inv_sqrt):
            dve.nop().then_inc(sem("moe_start"), 1)
            step(dve.scalar_tensor_tensor(gain[:, 0:8], mod[:, 32:40], 1.0, pc("norm2_g"), ALU.add, ALU.mult))
            ready(dve, ("ss", 2))
            take(("ss", 2), dve.tensor_scalar(small[:, :], bank(("ss", 2)), 1.0 / D, 1e-6, ALU.mult, ALU.add))
            inv_sqrt(dve.nop(), small[:, :])
            for k in range(KT):
                dve.scalar_tensor_tensor(H[:, k, :], X[:, k, :], gain[:, k:k + 1], small[:, :],
                                         ALU.mult, ALU.mult).then_inc(sem("xn2"), 1)
            dve.wait_ge(sem("moe_consts"), 1)
            lgb = ("lg",)
            ready(dve, lgb)
            take(lgb, dve.tensor_tensor(LG, bank(lgb)[:, 0:144].rearrange("p (m e) -> p m e", m=4),
                                        bc(pc("router_b"), [P, 4, 36], 1), ALU.add))

            def top(values, top_v, diff, weight, onehot, n):
                step(dve.tensor_reduce(top_v, values, AX.X, ALU.max))
                step(dve.tensor_tensor(diff, values, top_v.to_broadcast([P, 4, n]), ALU.subtract))
                step(dve.scalar_tensor_tensor(weight, diff, 0.0, bc(DESC[:, 0:n], [P, 4, n], 1),
                                              ALU.is_equal, ALU.mult))
                step(dve.tensor_reduce(T4, weight, AX.X, ALU.max))
                step(dve.tensor_tensor(onehot, weight, T4.to_broadcast([P, 4, n]), ALU.is_equal))

            top(LG[:, :, 0:4], GM, GD, GV, OHG, 4)
            dve.nop().then_inc(sem("gd"), 1)
            dve.wait_ge(sem("ge"), 1)
            step(dve.tensor_reduce(GS, GE, AX.X, ALU.add))
            step(dve.reciprocal(GP, GS))
            le = LG[:, :, 4:36].rearrange("p m (g e) -> p m e g", g=4)
            step(dve.tensor_tensor(TMP, le, bc(OHG, [P, 4, 8, 4], 2), ALU.mult))
            step(dve.tensor_reduce(SEL, TMP, AX.X, ALU.add))
            top(SEL, M1, D1, V8, OH1, 8)
            step(dve.scalar_tensor_tensor(SEL2, OH1, NEG, SEL, ALU.mult, ALU.add))
            top(SEL2, M2, D1, V8, OH2, 8)
            dve.tensor_tensor(E2, M2, M1, ALU.subtract).then_inc(sem("e2_in"), 1)
            dve.wait_ge(sem("e2"), 1)
            step(dve.tensor_scalar(T4, E2, 1.0, None, ALU.add))
            step(dve.reciprocal(T4, T4))
            step(dve.tensor_tensor(W1, GP, T4, ALU.mult))
            step(dve.tensor_tensor(W2, W1, E2, ALU.mult))
            for oh, full in ((OH1, OHA), (OH2, OHB)):
                step(dve.tensor_tensor(full, bc(OHG, [P, 4, 4, 8], 3), bc(oh, [P, 4, 4, 8], 2), ALU.mult))
            f32v = "p m g e -> p m (g e)"
            A32, B32 = OHA.rearrange(f32v), OHB.rearrange(f32v)
            step(dve.tensor_tensor(OHS, A32, B32, ALU.add))
            dve.nop().then_inc(sem("onehots"), 1)
            rk = ("rank",)
            ready(dve, rk)
            step(dve.tensor_copy(RK, bank(rk)[:, 0:128].rearrange("p (m e) -> p m e", m=4)))
            take(rk, dve.tensor_copy(CNT, bank(rk)[:, 128:160]))
            step(dve.tensor_scalar(OVB, CNT, float(CAP), None, ALU.is_gt))
            for n in range(2, SPLIT):
                step(dve.scalar_tensor_tensor(OVB, CNT, float(n * CAP), OVB, ALU.is_gt, ALU.add))
            step(dve.tensor_tensor_scan(INC, ONE, OVB, 0.0, ALU.mult, ALU.add))
            step(dve.tensor_tensor(BAS, INC, OVB, ALU.subtract))
            step(dve.scalar_tensor_tensor(BAS, EID, -1.0, BAS, ALU.mult, ALU.add))
            step(dve.tensor_scalar(BAS, BAS, float(N_EXP - 1), None, ALU.add))
            step(dve.tensor_scalar(QQ, RK, float(CAP), None, ALU.is_ge))
            for n in range(2, SPLIT):
                step(dve.scalar_tensor_tensor(QQ, RK, float(n * CAP), QQ, ALU.is_ge, ALU.add))
            step(dve.tensor_tensor(TA, QQ, bc(BAS, [P, 4, 32], 1), ALU.add))
            step(dve.scalar_tensor_tensor(TA, QQ, 0.0, TA, ALU.is_gt, ALU.mult))
            step(dve.tensor_tensor(TA, TA, QQ, ALU.subtract))
            step(dve.tensor_tensor(TA, TA, bc(EID, [P, 4, 32], 1), ALU.add))
            step(dve.scalar_tensor_tensor(TA, TA, float(CAP), RK, ALU.mult, ALU.add))
            for ch, oh in ((0, A32), (1, B32)):
                step(dve.tensor_tensor(TB, oh, TA, ALU.mult))
                step(dve.tensor_reduce(POS[:, ch, :], TB, AX.X, ALU.add))
            step(dve.tensor_copy(pos_i, POS.rearrange("p c m -> p (c m)")))
            for b in range(MAX_OVER):
                step(dve.tensor_scalar(TB[:, 0, :], INC, float(b), None, ALU.is_le))
                step(dve.tensor_reduce(EO[:, b:b + 1], TB[:, 0, :], AX.X, ALU.add))
            step(dve.tensor_scalar(EO[:, 0:MAX_OVER], EO[:, 0:MAX_OVER], float(N_EXP - 1), None, ALU.min))
            step(dve.tensor_copy(EO[:, 7:8], INC[:, 31:32]))
            dve.tensor_copy(over_i, EO).then_inc(sem("pos_ready"), 1)
            ix = ("idx",)
            ready(dve, ix)
            dve.tensor_copy(idx, bank(ix)[:, 0:BLOCKS]).then_inc(freed(ix), 1)
            dve.wait_ge(freed(ix), AUX_NO[ix] // 4 + 1)
            dve.nop().then_inc(sem("idx_ready"), 1)

            dve.nop().then_inc(sem("h_done"), 1)
            with dve.Fori(0, N_EXP // 4) as i:
                for s in range(4):
                    e = i * 4 + (s + 1)
                    dve.wait_ge(sem("units_done"), i * 24 + (U0 + 6 * s + 4))
                    dve.wait_ge(sem("silu_done"), e)
                    dve.tensor_tensor(HB, SG, up_bank, ALU.mult).then_inc(sem("h_done"), 1)
                    dve.wait_ge(sem("ht_ready"), e)
                    dve.tensor_copy(HTE, h_bank).then_inc(sem("ht_copied"), 1)
                    dve.wait_ge(sem("units_done"), i * 24 + (U0 + 6 * s + 6))
                    dve.wait_ge(sem(f"y_stored{s % 2}"), (i * 2 + (s // 2 + 1)) * 16)
                    dve.tensor_copy(YS[s % 2][:, 512:1024], y_banks[:, 1, :]).then_inc(sem("y_half_b"), 1)
            dve.wait_ge(sem("pos_ready"), 1)
            n_over = dve.value_load(over_i[0:1, 7:8], min_val=0, max_val=MAX_OVER)
            with dve.If(n_over > 0):
                with dve.Fori(0, MAX_OVER) as b:
                    dve.wait_ge(sem("o_sg"), b + 1)
                    dve.tensor_tensor(HB, SG, up_bank, ALU.mult).then_inc(sem("o_h"), 1)
                    dve.wait_ge(sem("o_ht"), b + 1)
                    dve.tensor_copy(HTE, h_bank).then_inc(sem("o_hte"), 1)
                    dve.wait_ge(sem("o_stored"), (b + 1) * 16)
            w1, w2 = W1.rearrange("p m a -> p (m a)"), W2.rearrange("p m a -> p (m a)")
            for m in range(4):
                y1, y2 = YG[2 * (m % 2)], YG[2 * (m % 2) + 1]
                dve.wait_ge(sem(f"y_in{m % 2}"), 32 * (m // 2 + 1))
                if m >= 1:
                    ready(dve, ("comb", m - 1, 1))
                step(dve.tensor_scalar(YS[0], y1, w1[:, m:m + 1], None, ALU.mult))
                dve.scalar_tensor_tensor(YS[0], y2, w2[:, m:m + 1], YS[0], ALU.mult, ALU.add)\
                   .then_inc(sem("combined"), 1)
                dve.wait_ge(sem("combined"), m + 1)
                for h in range(2):
                    n_ = ("comb", m, h)
                    ready(dve, n_)
                    v = SG.rearrange("p (k t) -> p k t", k=4)
                    take(n_, dve.tensor_tensor(v, bank(n_).rearrange("p (k t) -> p k t", k=4),
                                               bc(mod[:, 40 + 4 * h:44 + 4 * h], [P, 4, P], 2), ALU.mult))
                    xs = X[:, 4 * h:4 * h + 4, P * m:P * m + P]
                    step(dve.tensor_tensor(xs, xs, v, ALU.add))
                    dve.nop().then_inc(sem("x_moe"), 1)
            ready(dve, ("ss", 3))
            take(("ss", 3), dve.tensor_scalar(small[:, :], bank(("ss", 3)), 1.0 / D, 1e-6, ALU.mult, ALU.add))
            inv_sqrt(dve.nop(), small[:, :])
            for k in range(KT):
                step(dve.scalar_tensor_tensor(X[:, k, :], X[:, k, :], pc("final_g", k), small[:, :],
                                              ALU.mult, ALU.mult))
            dve.nop().then_inc(sem("x_first"), 1)
            if stop == 2:
                dve.nop().then_inc(sem("result"), 1)

        def moe_tensor(pe, aux, filled, dense, colsum):
            pe.wait_ge(sem("sq2"), 1)
            colsum(("ss", 2), lambda k: YC[:, k, :], KT)
            pe.wait_ge(sem("h2"), KT)
            out = aux(("lg",))
            rw = pc("router_w").rearrange("p (k e) -> p k e", k=KT)
            for m in range(4):
                for k in range(KT):
                    mm = pe.matmul(out[:, 36 * m:36 * m + 36], H[:, k, P * m:P * m + P], rw[:, k, :],
                                   start=(k == 0), stop=(k == KT - 1))
            filled(mm)
            out = aux(("rank",))
            pe.wait_ge(sem("onehots"), 1)
            for m in range(4):
                for m2 in range(m + 1):
                    mm = pe.matmul(out[:, 32 * m:32 * m + 32], strict_u if m2 == m else ones, OHS[:, m2, :],
                                   start=(m2 == 0), stop=(m2 == m))
            for m in range(4):
                mm = pe.matmul(out[:, 128:160], ones, OHS[:, m, :], start=(m == 0), stop=(m == 3))
            filled(mm)
            for m in range(4):
                for h in range(2):
                    out = aux(("ht", m, h))
                    for k in range(4):
                        mm = pe.transpose(out[:, P * k:P * k + P], H[:, 4 * h + k, P * m:P * m + P], ident)
                    filled(mm)
            out = aux(("idx",))
            pe.wait_ge(sem("table_in"), 16)
            filled(pe.transpose(out[:, 0:BLOCKS], TSB[0:BLOCKS, :], ident[0:BLOCKS, 0:BLOCKS]))

            def x_rows(count, buf, signal):
                for k in range(KT):
                    mm = pe.transpose(x_banks[:, k // 4, P * (k % 4):P * (k % 4) + P],
                                      XG[buf][:, P * k:P * k + P], ident)
                mm.then_inc(sem(signal), 1)

            def gate_up(bank_, xe, tiles):
                for i, t in enumerate(tiles):
                    w = t.rearrange("p (k n) -> p k n", k=4)
                    for k in range(4):
                        kk_ = 4 * i + k
                        mm = pe.matmul(bank_, xe[:, P * kk_:P * kk_ + P], w[:, k, :], start=(kk_ == 0), stop=(kk_ == 7))
                    yield mm

            def down(tiles):
                for i, t in enumerate(tiles):
                    w = t.rearrange("p (k n) -> p k n", k=2)
                    for h in range(2):
                        for k in range(2):
                            kk_ = 2 * i + k
                            mm = pe.matmul(y_banks[:, h, :], HTE[:, P * kk_:P * kk_ + P],
                                           w[:, k, 512 * h:512 * h + 512], start=(kk_ == 0), stop=(kk_ == 3))
                    yield mm

            def h_rows(signal):
                for k in range(4):
                    mm = pe.transpose(h_bank[:, P * k:P * k + P], HB[:, P * k:P * k + P], ident)
                mm.then_inc(sem(signal), 1)

            for n in range(4):
                pe.wait_ge(sem(f"aux_free{n}"), (AUX_NO[("idx",)] - n) // 4 + 1)
            for n in range(2):
                pe.wait_ge(sem(f"pair_free{n}"), sum(1 for g in GROUPS[:GROUP_NO[("w_out", 3)] + 1]
                                                     if GROUP_NO[g] % 2 == n))
            pe.wait_ge(sem("xg_in0"), 16)
            x_rows(1, 0, "xt_ready")
            with pe.Fori(0, N_EXP // 4) as i:
                for s in range(4):
                    u0 = U0 + 6 * s

                    def unit_in(j):
                        u = u0 + j
                        pe.wait_ge(sem(f"ring_full{u % RING}"), (i * 3 + (u // RING + 1)) * 16)
                        return slot_tile(u % RING)
                    pe.wait_ge(sem("xt_copied"), i * 4 + (s + 1))
                    for h in range(2):
                        t = unit_in(h)
                        w = t.rearrange("p (k n) -> p k n", k=4)
                        for k in range(4):
                            mm = pe.matmul(gate_bank, XE[s % 2][:, P * (4 * h + k):P * (4 * h + k) + P], w[:, k, :],
                                           start=(h + k == 0), stop=(4 * h + k == 7))
                        mm.then_inc(sem("units_done"), 1)
                    pe.wait_ge(sem("h_done"), i * 4 + (s + 1))
                    for h in range(2):
                        t = unit_in(2 + h)
                        w = t.rearrange("p (k n) -> p k n", k=4)
                        for k in range(4):
                            mm = pe.matmul(up_bank, XE[s % 2][:, P * (4 * h + k):P * (4 * h + k) + P], w[:, k, :],
                                           start=(h + k == 0), stop=(4 * h + k == 7))
                        mm.then_inc(sem("units_done"), 1)
                    pe.wait_ge(sem(f"xg_in{(s + 1) % 2}"), (i * 2 + ((s + 1) // 2 + 1)) * 16)
                    x_rows(None, (s + 1) % 2, "xt_ready")
                    pe.wait_ge(sem("h_done"), i * 4 + (s + 2))
                    h_rows("ht_ready")
                    pe.wait_ge(sem("ht_copied"), i * 4 + (s + 1))
                    for h in range(2):
                        t = unit_in(4 + h)
                        w = t.rearrange("p (k n) -> p k n", k=2)
                        for n in range(2):
                            for k in range(2):
                                kk_ = 2 * h + k
                                mm = pe.matmul(y_banks[:, n, :], HTE[:, P * kk_:P * kk_ + P],
                                               w[:, k, 512 * n:512 * n + 512], start=(kk_ == 0), stop=(kk_ == 3))
                        mm.then_inc(sem("units_done"), 1)
                    pe.wait_ge(sem("y_half_a"), i * 4 + (s + 1))
                    pe.wait_ge(sem("y_half_b"), i * 4 + (s + 1))
            pe.wait_ge(sem("xt_copied"), N_EXP + 1)
            pe.wait_ge(sem("pos_ready"), 1)
            n_over = pe.value_load(over_i[0:1, 7:8], min_val=0, max_val=MAX_OVER)
            with pe.If(n_over > 0):
                with pe.Fori(0, MAX_OVER) as b:
                    pe.wait_ge(sem("o_x"), (b + 1) * 16)
                    x_rows(None, 0, "o_xt")
                    pe.wait_ge(sem("o_xe"), b + 1)
                    pe.wait_ge(sem("o_weights"), (b + 1) * 96)
                    for mm in gate_up(gate_bank, XE[0], [slot_tile(0), slot_tile(1)]):
                        pass
                    for mm in gate_up(up_bank, XE[0], [slot_tile(2), slot_tile(3)]):
                        pass
                    mm.then_inc(sem("o_gu"), 1)
                    pe.wait_ge(sem("o_h"), b + 1)
                    h_rows("o_ht")
                    pe.wait_ge(sem("o_hte"), b + 1)
                    for mm in down([slot_tile(4), slot_tile(5)]):
                        pass
                    mm.then_inc(sem("o_y"), 1)
                    pe.wait_ge(sem("o_stored"), (b + 1) * 16)
            for m in range(4):
                pe.wait_ge(sem("combined"), m + 1)
                for h in range(2):
                    out = aux(("comb", m, h))
                    for k in range(4):
                        kk_ = 4 * h + k
                        mm = pe.transpose(out[:, P * k:P * k + P], YS[0][:, P * kk_:P * kk_ + P], ident)
                    filled(mm)
            pe.wait_ge(sem("sq3"), 1)
            colsum(("ss", 3), lambda k: H[:, k, :], KT)

        YS2, BC = area(4096, 16), area(12288, 4)
        XDT = flat(14336, 4096).rearrange("p (c n) -> p c n", c=4)
        HIN = [flat(18432 + 1024 * c, 1024) for c in range(3)]
        DT = [flat(21504 + 512 * i, 512) for i in range(8)]
        SELH = flat(21504, 2048).rearrange("p (h t) -> p h t", h=16)
        GB = [flat(25600 + 512 * i, 512) for i in range(4)]
        CE = [flat(27648 + 512 * i, 512) for i in range(4)]
        CBM = [flat(29696 + 512 * g, 512) for g in range(2)]
        BTOK = flat(30720, 1024).rearrange("p (c g n) -> p c g n", c=4, g=2)
        XDE = flat(31744, 1024)
        ACST, DTT, DEC, DEE = (flat(32768 + 64 * i, 64) for i in range(4))
        acst, dtt, dee = (t.rearrange("p (c h) -> p c h", c=4) for t in (ACST, DTT, DEE))
        dec = DEC.rearrange("p (h c) -> p h c", h=16)
        ZT = [GB[0], GB[1], GB[2], GB[3]]
        SQ = flat(14336, 4096)
        SQK = area(14336, 8)
        HIDE = area(4096, 22)
        SGT = [flat(15360 + 512 * i, 512) for i in range(2)]
        SQ2, SQ2K = flat(16384, 4096), area(16384, 8)
        SIG = area(20480, 8)
        PT = area(24576, 2)
        Q = area(4096, 8)
        KZ = [flat(8192 + 1024 * m, 1024).rearrange("p (o t) -> p o t", o=2) for m in range(2)]
        VA = flat(10240, 1024).rearrange("p (n v) -> p n v", n=4)
        OA = area(11264, 8)
        BAND = flat(15360, 256)
        PB = [flat(16384 + 512 * i, 512) for i in range(4)]
        PTB = [flat(18432 + 512 * i, 512) for i in range(2)]
        ATS = flat(19456, 64 * 8)
        TO = [flat(20480 + 512 * i, 512) for i in range(2)]

        def att(i):
            n, j = i // 8, i % 8
            return n, j, P if n == 0 else 2 * P

        def second_sync(sp_):
            pass

        def second_pool(pool, step):
            pool.wait_ge(sem("ple_done0"), 1)
            step(pool.memset(BAND, 0.0))
            step(pool.affine_select(out=BAND[:, 0:P], in_=BAND[:, 0:P], compare_op=ALU.is_gt, fill=NEG, base=0,
                                    pattern=[[1, P]], channel_multiplier=-1))
            step(pool.affine_select(out=BAND[:, P:2 * P], in_=BAND[:, P:2 * P], compare_op=ALU.is_ge, fill=NEG,
                                    base=0, pattern=[[-1, P]], channel_multiplier=1))
            for m in range(2):
                step(pool.memset(KZ[m][HD:P, 0, :], 0.0))
                step(pool.memset(KZ[m][0:HD, 1, :], 0.0))
            pool.nop().then_inc(sem("att_consts"), 1)

        def second_act(act, step, root):
            act.wait_ge(sem("x_first"), 1)
            for j in range(8):
                g = ("sc_ch", j)
                group_ready(act, g)
                if j >= 2:
                    act.wait_ge(sem("sc_prod"), j - 1)
                act.activation(GB[j % 2], dbank(g)[:, 0, :], ACT.Copy).then_inc(sem("sc_c"), 1)
            for q in range(12):
                g, b = ("xbc", q // 2), q % 2
                if b == 0:
                    group_ready(act, g)
                dst = YS2[:, q, :] if q < 8 else BC[:, q - 8, :]
                act.activation(dst, dbank(g)[:, b, :], ACT.Identity, scale=pc("conv_w", 36 + q),
                               bias=pc("conv_b", q)).then_inc(sem("conv_a"), 1)
                act.wait_ge(sem("conv_b"), q + 1)
                act.activation(dst, dst, ACT.Silu).then_inc(sem("xbc_done"), 1)
            act.wait_ge(sem("dt_abs"), 1)
            act.activation(DT[2][0:16], DT[1][0:16], ACT.Exp, scale=-1.0).then_inc(sem("dt_exp"), 1)
            act.activation(gain[0:16, 56:57], pc("a_log")[0:16], ACT.Exp).then_inc(sem("a_exp"), 1)
            for c in range(4):
                n_ = ("bct", c)
                ready(act, n_)
                act.activation(BTOK[:, c].rearrange("p g n -> p (g n)"), bank(n_)[:, 0:256], ACT.Copy)\
                   .then_inc(freed(n_), 1)
            act.wait_ge(sem("last_in"), 1)
            act.activation(DEE, DEE, ACT.Exp).then_inc(sem("last_exp"), 1)
            act.activation(DEC, DEC, ACT.Exp).then_inc(sem("last_exp"), 1)
            for h in range(16):
                n_ = ("acs", h)
                ready(act, n_)
                if h >= 4:
                    ready(act, ("yd", h // 2 - 2))
                act.wait_ge(sem("seg_min"), h + 1)
                act.activation(CE[h % 4], bank(n_), ACT.Exp).then_inc(freed(n_), 1)
                act.wait_ge(sem("seg"), h + 1)
                act.activation(GB[h % 4], GB[h % 4], ACT.Exp).then_inc(sem("seg_exp"), 1)
            for j in range(8):
                g = ("z", j // 2)
                if j % 2 == 0:
                    group_ready(act, g)
                if j >= 4:
                    act.wait_ge(sem("z_mul"), j - 3)
                if j == 0:
                    ready(act, ("yd", 7))
                act.activation(ZT[j % 4], dbank(g)[:, j % 2, :], ACT.Silu).then_inc(sem("z_silu"), 1)
            for j in range(8):
                act.wait_ge(sem("z_mul"), j + 1)
                act.activation(SQK[:, j, :], YS2[:, j, :], ACT.Square).then_inc(sem("y_sq"), 1)
            for g in range(2):
                root(small[:, :])

            def layer_norm(n):
                for k in range(KT):
                    act.wait_ge(sem("ln_c"), KT * n + k + 1)
                    act.activation(SQ2K[:, k, :], X[:, k, :], ACT.Square).then_inc(sem("ln_sq"), 1)
                root(small[:, :])
                which, layer = ("mix", "ffn")[n % 2], n // 2
                for k in range(KT):
                    act.wait_ge(sem("ln_s"), KT * n + k + 1)
                    act.activation(X[:, k, :], X[:, k, :], ACT.Identity, bias=pc(f"ln_{which}_b", 8 * layer + k))\
                       .then_inc(sem("ln_x"), 1)

            for layer in range(2):
                if layer == 1:
                    for i in range(N_ATT + 4):
                        if i < N_ATT:
                            n, j, w = att(i)
                            pb = PB[i % 4][:, 0:2 * w].rearrange("p (o s) -> p o s", o=2)
                            st = ATS[:, 16 * (i % 4):16 * (i % 4) + 16]
                            act.wait_ge(sem("att_max"), i + 1)
                            for o_ in range(2):
                                act.activation(pb[:, o_, :], pb[:, o_, :], ACT.Exp, bias=st[:, 2 + o_:3 + o_],
                                               accum_out=st[:, 4 + o_:5 + o_]).then_inc(sem("att_exp"), 1)
                            act.activation(st[:, 6:8], st[:, 6:8], ACT.Exp).then_inc(sem("att_exp"), 1)
                        if 2 <= i < N_ATT + 2:
                            k = i - 2
                            _, _, w = att(k)
                            n_ = ("pt", k)
                            ready(act, n_)
                            if k >= 2:
                                ready(act, ("pv", k - 2))
                            act.activation(PTB[k % 2][:, 0:2 * w], bank(n_)[:, 0:2 * w], ACT.Copy)\
                               .then_inc(freed(n_), 1)
                        if 3 <= i < N_ATT + 3:
                            k = i - 3
                            n, j, _ = att(k)
                            n_ = ("pv", k)
                            ready(act, n_)
                            act.activation(OA[:, j, P * n:P * n + P], bank(n_)[:, 0:P], ACT.Copy)\
                               .then_inc(freed(n_), 1)
                    for j in range(8):
                        g = ("wo", j // 2)
                        if j % 2 == 0:
                            group_ready(act, g)
                        if j >= 2:
                            act.wait_ge(sem("x_res1"), j - 1)
                        act.activation(TO[j % 2], dbank(g)[:, j % 2, :], ACT.Identity, bias=pc("b_o", j))\
                           .then_inc(sem("wo_bias"), 1)
                layer_norm(2 * layer)
                act.wait_ge(sem("ln_x"), KT * (2 * layer + 1))
                act.dma_start(PT, p_t[layer]).then_inc(sem("p_in"), 16)
                for j in range(22):
                    g = ("gu", layer, j)
                    group_ready(act, g)
                    if j >= 2:
                        act.wait_ge(sem(f"hidden{layer}"), j - 1)
                    act.activation(SGT[j % 2], dbank(g)[:, 0, :], ACT.Silu).then_inc(sem("ffn_silu"), 1)
                layer_norm(2 * layer + 1)
                for j in range(8):
                    g = ("ple_g", layer, j // 2)
                    if j % 2 == 0:
                        group_ready(act, g)
                    ins = act.activation(SIG[:, j, :], dbank(g)[:, j % 2, :], ACT.Sigmoid,
                                         bias=pc("b_ple", 8 * layer + j))
                    if j % 2 == 1:
                        ins.then_inc(group_freed(g), 1)
                    else:
                        ins.then_inc(sem("sig_half"), 1)

        def second_vector(dve, step, take, inv_sqrt):
            def done_with(g):
                dve.nop().then_inc(group_freed(g), 1)

            for j in range(8):
                g = ("sc_ch", j)
                group_ready(dve, g)
                dve.wait_ge(sem("sc_c"), j + 1)
                pr = GB[2 + j % 2]
                dve.tensor_tensor(pr, GB[j % 2], dbank(g)[:, 1, :], ALU.mult).then_inc(sem("sc_prod"), 1)
                dve.wait_ge(sem("sc_prod"), j + 1)
                done_with(g)
                y = YS2[:, 8 + j, :]
                step(dve.tensor_scalar(y, pr, pc("sc_w", 16 + j), None, ALU.mult))
                for t in (1, 2):
                    step(dve.scalar_tensor_tensor(y[:, t:SEQ], pr[:, 0:SEQ - t], pc("sc_w", 8 * (2 - t) + j),
                                                  y[:, t:SEQ], ALU.mult, ALU.add))
            for j in range(8):
                g = ("sc_b", j // 2)
                if j % 2 == 0:
                    group_ready(dve, g)
                step(dve.tensor_tensor(YS2[:, 8 + j, :], YS2[:, 8 + j, :], dbank(g)[:, j % 2, :], ALU.mult))
                if j % 2 == 1:
                    done_with(g)
            for q in range(12):
                g, b = ("xbc", q // 2), q % 2
                dst = YS2[:, q, :] if q < 8 else BC[:, q - 8, :]
                dve.wait_ge(sem("conv_a"), q + 1)
                for t in (1, 2, 3):
                    step(dve.scalar_tensor_tensor(dst[:, t:SEQ], dbank(g)[:, b, 0:SEQ - t],
                                                  pc("conv_w", 12 * (3 - t) + q), dst[:, t:SEQ], ALU.mult, ALU.add))
                dve.nop().then_inc(sem("conv_b"), 1)
                if b == 1:
                    done_with(g)
            g = ("dt",)
            group_ready(dve, g)
            x, ab, u, s_, s2, q_ = (DT[i][0:16] for i in range(6))
            step(dve.tensor_scalar(x, dbank(g)[0:16, 0, :], pc("dt_b")[0:16], None, ALU.add))
            done_with(g)
            dve.scalar_tensor_tensor(ab, x, -1.0, x, ALU.mult, ALU.max).then_inc(sem("dt_abs"), 1)
            dve.wait_ge(sem("dt_exp"), 1)
            step(dve.tensor_scalar(s_, u, 2.0, None, ALU.add))
            step(dve.reciprocal(s_, s_))
            step(dve.tensor_tensor(s_, s_, u, ALU.mult))
            step(dve.tensor_tensor(s2, s_, s_, ALU.mult))
            step(dve.tensor_scalar(q_, s2, 1.0 / 15, None, ALU.mult))
            for n in (13, 11, 9, 7, 5, 3):
                step(dve.scalar_tensor_tensor(q_, q_, 1.0 / n, s2, ALU.add, ALU.mult))
            step(dve.scalar_tensor_tensor(q_, q_, 1.0, s_, ALU.add, ALU.mult))
            step(dve.tensor_scalar(x, x, 0.0, None, ALU.max))
            step(dve.scalar_tensor_tensor(q_, q_, 2.0, x, ALU.mult, ALU.add))
            dve.wait_ge(sem("a_exp"), 1)
            da, acs = DT[6][0:16], DT[7][0:16]
            step(dve.tensor_scalar(da, q_, gain[0:16, 56:57], -1.0, ALU.mult, ALU.mult))
            step(dve.tensor_tensor_scan(acs, reset[0:16, :], da, 0.0, ALU.mult, ALU.add))
            step(dve.tensor_copy(SELH[0:16], ident[0:16, 0:16].unsqueeze(2).to_broadcast([16, 16, P])))
            last = acs.rearrange("h (c t) -> h c t", c=4)[:, :, P - 1]
            dl = DT[6][0:16, 0:64].rearrange("p (h c) -> p h c", h=16)
            step(dve.tensor_tensor(dl, ident[0:16, 0:16].unsqueeze(2).to_broadcast([16, 16, 4]),
                                   last.unsqueeze(1).to_broadcast([16, 16, 4]), ALU.mult))
            dve.nop().then_inc(sem("acs_ready"), 1)
            n_ = ("da_t",)
            ready(dve, n_)
            step(dve.tensor_copy(ACST, bank(n_)[:, 0:64]))
            take(n_, dve.tensor_copy(DTT, bank(n_)[:, 64:128]))
            n_ = ("last",)
            ready(dve, n_)
            step(dve.tensor_copy(DEC, bank(n_)[:, 0:64]))
            take(n_, dve.tensor_tensor(dee, bank(n_)[:, 0:64].rearrange("p (h c) -> p c h", h=16), acst, ALU.subtract))
            dve.nop().then_inc(sem("last_in"), 1)
            for c in range(4):
                for h in range(2):
                    n_ = ("xst", c, h)
                    ready(dve, n_)
                    take(n_, dve.tensor_tensor(
                        XDT[:, c, 512 * h:512 * h + 512].rearrange("p (h v) -> p h v", h=8),
                        bank(n_).rearrange("p (h v) -> p h v", h=8),
                        dtt[:, c, 8 * h:8 * h + 8].unsqueeze(2).to_broadcast([P, 8, HD]), ALU.mult))
            dve.nop().then_inc(sem("xdt"), 1)
            for g in range(2):
                n_ = ("cb", g)
                ready(dve, n_)
                take(n_, dve.tensor_tensor(CBM[g].rearrange("p (c t) -> p c t", c=4),
                                           bank(n_).rearrange("p (c t) -> p c t", c=4),
                                           pair[:, 1, :].unsqueeze(1).to_broadcast([P, 4, P]), ALU.mult))
            dve.wait_ge(sem("last_exp"), 2)
            for c in range(3):
                if c > 0:
                    ready(dve, ("stt", c - 1, 1))
                step(dve.tensor_tensor(XDE.rearrange("p (h v) -> p h v", h=16),
                                       XDT[:, c, :].rearrange("p (h v) -> p h v", h=16),
                                       dee[:, c, :].unsqueeze(2).to_broadcast([P, 16, HD]), ALU.mult))
                dve.nop().then_inc(sem("xde"), 1)
                for g in range(2):
                    n_ = ("stt", c, g)
                    hs_ = slice(512 * g, 512 * g + 512)
                    if c > 0:
                        step(dve.tensor_tensor(HIN[c][:, hs_].rearrange("p (h v) -> p h v", h=8),
                                               HIN[c - 1][:, hs_].rearrange("p (h v) -> p h v", h=8),
                                               dec[:, 8 * g:8 * g + 8, c:c + 1].to_broadcast([P, 8, HD]), ALU.mult))
                        ready(dve, n_)
                        take(n_, dve.tensor_tensor(HIN[c][:, hs_], HIN[c][:, hs_], bank(n_), ALU.add))
                    else:
                        ready(dve, n_)
                        take(n_, dve.tensor_copy(HIN[c][:, hs_], bank(n_)))
            dve.nop().then_inc(sem("hin"), 1)

            def head_out(j):
                n_ = ("yd", j)
                ready(dve, n_)
                take(n_, dve.scalar_tensor_tensor(YS2[:, j, :], YS2[:, j, :], pc("d_skip", j), bank(n_),
                                                  ALU.mult, ALU.add))

            for h in range(16):
                n_ = ("acs", h)
                ready(dve, n_)
                if h >= 4:
                    ready(dve, ("yd", h // 2 - 2))
                gb = GB[h % 4].rearrange("p (c t) -> p c t", c=4)
                sb_ = acst[:, :, h:h + 1].to_broadcast([P, 4, P])
                dve.tensor_tensor(gb, bank(n_).rearrange("p (c t) -> p c t", c=4), sb_, ALU.min)\
                   .then_inc(sem("seg_min"), 1)
                dve.wait_ge(sem("seg_min"), h + 1)
                dve.tensor_tensor(gb, gb, sb_, ALU.subtract).then_inc(sem("seg"), 1)
                dve.wait_ge(freed(n_), AUX_NO[n_] // 4 + 1)
                dve.tensor_tensor(CE[h % 4], CE[h % 4], BC[:, 2 + h // 8, :], ALU.mult).then_inc(sem("head_ce"), 1)
                dve.wait_ge(sem("seg_exp"), h + 1)
                dve.tensor_tensor(GB[h % 4], GB[h % 4], CBM[h // 8], ALU.mult).then_inc(sem("head_g"), 1)
                if h % 2 == 1 and h >= 3:
                    head_out(h // 2 - 1)
            head_out(7)
            for j in range(8):
                g = ("z", j // 2)
                dve.wait_ge(sem("z_silu"), j + 1)
                if j % 2 == 1:
                    done_with(g)
                dve.tensor_tensor(YS2[:, j, :], YS2[:, j, :], ZT[j % 4], ALU.mult).then_inc(sem("z_mul"), 1)
            for g in range(2):
                n_ = ("gss", g)
                ready(dve, n_)
                take(n_, dve.tensor_scalar(small[:, :], bank(n_), 1.0 / 512, 1e-5, ALU.mult, ALU.add))
                inv_sqrt(dve.nop(), small[:, :])
                for j in range(4 * g, 4 * g + 4):
                    step(dve.scalar_tensor_tensor(YS2[:, j, :], YS2[:, j, :], pc("ssd_nw", j), small[:, :],
                                                  ALU.mult, ALU.mult))
            dve.nop().then_inc(sem("y_ssd"), 1)

            def layer_norm(n):
                which, layer = ("mix", "ffn")[n % 2], n // 2
                m_, v_ = ("lnm", which, layer), ("lnv", which, layer)
                ready(dve, m_)
                for k in range(KT):
                    dve.scalar_tensor_tensor(X[:, k, :], bank(m_), -1.0 / D, X[:, k, :], ALU.mult, ALU.add)\
                       .then_inc(sem("ln_c"), 1)
                dve.wait_ge(sem("ln_c"), KT * (n + 1))
                dve.nop().then_inc(freed(m_), 1)
                ready(dve, v_)
                take(v_, dve.tensor_scalar(small[:, :], bank(v_), 1.0 / D, 1e-5, ALU.mult, ALU.add))
                inv_sqrt(dve.nop(), small[:, :])
                for k in range(KT):
                    dve.scalar_tensor_tensor(X[:, k, :], X[:, k, :], pc(f"ln_{which}_g", 8 * layer + k), small[:, :],
                                             ALU.mult, ALU.mult).then_inc(sem("ln_s"), 1)

            def residual(groups, src=None):
                for j in range(8):
                    g = groups[j // 2]
                    if j % 2 == 0:
                        group_ready(dve, g)
                    if src is not None:
                        dve.wait_ge(sem("wo_bias"), j + 1)
                    dve.scalar_tensor_tensor(X[:, j, :], X[:, j, :], ALPHA,
                                             dbank(g)[:, j % 2, :] if src is None else src[j % 2],
                                             ALU.mult, ALU.add).then_inc(sem("x_res"), 1)
                    residual.n += 1
                    dve.wait_ge(sem("x_res"), residual.n)
                    if src is not None:
                        dve.nop().then_inc(sem("x_res1"), 1)
                    if j % 2 == 1:
                        done_with(g)
            residual.n = 0

            for layer in range(2):
                if layer == 0:
                    residual([("mix_out", j) for j in range(4)])
                else:
                    attention(dve, step, take, done_with)
                    residual([("wo", j) for j in range(4)], TO)
                layer_norm(2 * layer)
                for j in range(22):
                    g = ("gu", layer, j)
                    group_ready(dve, g)
                    dve.wait_ge(sem("ffn_silu"), 22 * layer + j + 1)
                    dve.tensor_tensor(HIDE[:, j, :], SGT[j % 2], dbank(g)[:, 1, :], ALU.mult)\
                       .then_inc(sem(f"hidden{layer}"), 1)
                    dve.wait_ge(sem(f"hidden{layer}"), j + 1)
                    done_with(g)
                residual([("down", layer, j) for j in range(4)])
                layer_norm(2 * layer + 1)
                for j in range(8):
                    g = ("ple_w", layer, j // 2)
                    if j % 2 == 0:
                        group_ready(dve, g)
                    if j == 0:
                        gg = ("ple_g", layer, 3)
                        dve.wait_ge(group_freed(gg), GROUP_NO[gg] // 2 + 1)
                        dve.wait_ge(group_freed(("ple_g", layer, 2)), GROUP_NO[("ple_g", layer, 2)] // 2 + 1)
                    step(dve.tensor_tensor(SIG[:, j, :], SIG[:, j, :], dbank(g)[:, j % 2, :], ALU.mult))
                    step(dve.tensor_tensor(X[:, j, :], X[:, j, :], SIG[:, j, :], ALU.add))
                    if j % 2 == 1:
                        done_with(g)
                dve.nop().then_inc(sem(f"ple_done{layer}"), 1)
            dve.nop().then_inc(sem("result"), 1)

        def attention(dve, step, take, done_with):
            dve.wait_ge(sem("att_consts"), 1)
            for j in range(8):
                g = ("q", j // 2)
                if j % 2 == 0:
                    group_ready(dve, g)
                step(dve.tensor_scalar(Q[:, j, :], dbank(g)[:, j % 2, :], pc("b_q", j), HD ** -0.5, ALU.add, ALU.mult))
                if j % 2 == 1:
                    done_with(g)
            g = ("kk",)
            group_ready(dve, g)
            for m in range(2):
                for o_ in range(2):
                    hp = slice(HD * o_, HD * o_ + HD)
                    step(dve.tensor_scalar(KZ[m][hp, o_, :], dbank(g)[hp, m, :], pc("b_k", m)[hp], None, ALU.add))
            done_with(g)
            g = ("vv",)
            group_ready(dve, g)
            for b in range(2):
                step(dve.tensor_tensor(VA[:, 2 * b:2 * b + 2, :],
                                       dbank(g)[:, b, :].rearrange("p (n v) -> p n v", n=2),
                                       pc("b_v").unsqueeze(1).to_broadcast([P, 2, 256]), ALU.add))
            done_with(g)
            dve.nop().then_inc(sem("qkv"), 1)

            def scores(i):
                n, j, w = att(i)
                n_ = ("sc", i)
                ready(dve, n_)
                pb = PB[i % 4][:, 0:2 * w].rearrange("p (o s) -> p o s", o=2)
                st = ATS[:, 16 * (i % 4):16 * (i % 4) + 16]
                sink = pc("sinks")[:, 2 * j:2 * j + 2]
                if i >= 4:
                    ready(dve, ("pt", i - 4))
                take(n_, dve.tensor_tensor(pb, bank(n_)[:, 0:2 * w].rearrange("p (o s) -> p o s", o=2),
                                           BAND[:, 2 * P - w:2 * P].unsqueeze(1).to_broadcast([P, 2, w]), ALU.add))
                step(dve.tensor_reduce(st[:, 0:2], pb, AX.X, ALU.max))
                step(dve.tensor_tensor(st[:, 0:2], st[:, 0:2], sink, ALU.max))
                step(dve.tensor_tensor(st[:, 6:8], sink, st[:, 0:2], ALU.subtract))
                dve.tensor_scalar(st[:, 2:4], st[:, 0:2], -1.0, None, ALU.mult).then_inc(sem("att_max"), 1)

            def norm(i):
                n, j, w = att(i)
                pb = PB[i % 4][:, 0:2 * w].rearrange("p (o s) -> p o s", o=2)
                st = ATS[:, 16 * (i % 4):16 * (i % 4) + 16]
                dve.wait_ge(sem("att_exp"), 3 * (i + 1))
                step(dve.tensor_tensor(st[:, 4:6], st[:, 4:6], st[:, 6:8], ALU.add))
                step(dve.reciprocal(st[:, 4:6], st[:, 4:6]))
                dve.tensor_tensor(pb, pb, st[:, 4:6].unsqueeze(2).to_broadcast([P, 2, w]), ALU.mult)\
                   .then_inc(sem("probs"), 1)

            for i in range(N_ATT + 1):
                if i < N_ATT:
                    scores(i)
                if i >= 1:
                    norm(i - 1)

        def second_tensor(pe, aux, filled, dense, colsum):
            pe.wait_ge(sem("x_first"), 1)
            xr = lambda k: X[:, k, :]
            for j in range(8):
                dense(("sc_ch", j), xr)
            for j in range(4):
                dense(("sc_b", j), xr)
            for j in range(6):
                dense(("xbc", j), xr)
            dense(("dt",), xr, (16,))
            pe.wait_ge(sem("acs_ready"), 1)
            out = aux(("da_t",))
            for c in range(4):
                cs = slice(P * c, P * c + P)
                pe.transpose(out[:, 16 * c:16 * c + 16], DT[7][0:16, cs], ident[0:16, 0:16])
                mm = pe.transpose(out[:, 64 + 16 * c:80 + 16 * c], DT[5][0:16, cs], ident[0:16, 0:16])
            filled(mm)
            filled(pe.matmul(aux(("last",))[:, 0:64], ones[0:16, :], DT[6][0:16, 0:64], start=True, stop=True))
            pe.wait_ge(sem("xbc_done"), 12)
            for c in range(4):
                out = aux(("bct", c))
                for g in range(2):
                    mm = pe.transpose(out[:, P * g:P * g + P], BC[:, g, P * c:P * c + P], ident)
                filled(mm)
            for c in range(4):
                for h in range(2):
                    out = aux(("xst", c, h))
                    for k in range(4):
                        mm = pe.transpose(out[:, P * k:P * k + P], YS2[:, 4 * h + k, P * c:P * c + P], ident)
                    filled(mm)
            for g in range(2):
                out = aux(("cb", g))
                for c in range(4):
                    cs = slice(P * c, P * c + P)
                    mm = pe.matmul(out[:, cs], BC[:, g, cs], BC[:, 2 + g, cs], start=True, stop=True)
                filled(mm)
            for c in range(4):
                n_ = ("bct", c)
                pe.wait_ge(freed(n_), AUX_NO[n_] // 4 + 1)
            for c in range(3):
                pe.wait_ge(sem("xde"), c + 1)
                for g in range(2):
                    filled(pe.matmul(aux(("stt", c, g)), BTOK[:, c, g, :], XDE[:, 512 * g:512 * g + 512],
                                     start=True, stop=True))

            def spread(h):
                filled(pe.matmul(aux(("acs", h)), SELH[0:16, h, :], DT[7][0:16, :], start=True, stop=True))

            spread(0)
            spread(1)
            pe.wait_ge(sem("hin"), 1)
            for j in range(8):
                for h in (2 * j + 2, 2 * j + 3):
                    if h < 16:
                        spread(h)
                out = aux(("yd", j))
                pe.wait_ge(sem("head_ce"), 2 * j + 2)
                pe.wait_ge(sem("head_g"), 2 * j + 2)
                for o_ in range(2):
                    h = 2 * j + o_
                    for c in range(4):
                        cs = slice(P * c, P * c + P)
                        dst = out[HD * o_:HD * o_ + HD, cs]
                        mm = pe.matmul(dst, XDT[:, c, HD * h:HD * h + HD], GB[h % 4][:, cs], start=True, stop=(c == 0))
                        if c > 0:
                            mm = pe.matmul(dst, HIN[c - 1][:, HD * h:HD * h + HD], CE[h % 4][:, cs],
                                           start=False, stop=True)
                filled(mm)
            for j in range(4):
                dense(("z", j), xr)
            for g in range(2):
                pe.wait_ge(sem("y_sq"), 4 * g + 4)
                colsum(("gss", g), lambda k: SQK[:, 4 * g + k, :], 4)
            pe.wait_ge(sem("y_ssd"), 1)
            for j in range(4):
                dense(("mix_out", j), lambda k: YS2[:, k, :])

            def layer_norm(n):
                which, layer = ("mix", "ffn")[n % 2], n // 2
                out = aux(("lnm", which, layer))
                for k in range(KT):
                    pe.wait_ge(sem("x_res"), KT * n + k + 1)
                    mm = pe.matmul(out, ones, X[:, k, :], start=(k == 0), stop=(k == KT - 1))
                filled(mm)
                out = aux(("lnv", which, layer))
                for k in range(KT):
                    pe.wait_ge(sem("ln_sq"), KT * n + k + 1)
                    mm = pe.matmul(out, ones, SQ2K[:, k, :], start=(k == 0), stop=(k == KT - 1))
                filled(mm)
                pe.wait_ge(sem("ln_x"), KT * (n + 1))

            for layer in range(2):
                if layer == 1:
                    pe.wait_ge(sem("ple_done0"), 1)
                    for j in range(4):
                        dense(("q", j), xr)
                    dense(("kk",), xr)
                    g = ("vv",)
                    n = GROUP_NO[g]
                    pe.wait_ge(sem(f"pair_free{n % 2}"), n // 2)
                    u, nk, nco = UNITS_OF[g][0]
                    loaded(pe, u)
                    w = ring_of(u, nk, nco)
                    for m in range(4):
                        for k in range(KT):
                            mm = pe.matmul(psD[:, n % 2, m // 2, 256 * (m % 2):256 * (m % 2) + 256],
                                           X[:, k, P * m:P * m + P], w[:, k, :], start=(k == 0), stop=(k == KT - 1))
                    mm.then_inc(sem("units_done"), 1)
                    pe.wait_ge(sem("qkv"), 1)
                    for i in range(N_ATT + 3):
                        if i < N_ATT:
                            n, j, w_ = att(i)
                            k0 = P * n + P - w_
                            filled(pe.matmul(aux(("sc", i))[:, 0:2 * w_].rearrange("p (o s) -> p o s", o=2),
                                             Q[:, j, P * n:P * n + P], KZ[j // 4][:, :, k0:k0 + w_],
                                             start=True, stop=True))
                        if 2 <= i < N_ATT + 2:
                            k = i - 2
                            _, _, w_ = att(k)
                            out = aux(("pt", k))
                            pe.wait_ge(sem("probs"), k + 1)
                            for b in range(2 * w_ // P):
                                mm = pe.transpose(out[:, P * b:P * b + P], PB[k % 4][:, P * b:P * b + P], ident)
                            filled(mm)
                        if i >= 3:
                            k = i - 3
                            n, j, w_ = att(k)
                            nb = w_ // P
                            out = aux(("pv", k))
                            n_ = ("pt", k)
                            pe.wait_ge(freed(n_), AUX_NO[n_] // 4 + 1)
                            for o_ in range(2):
                                kv = 2 * (j // 4) + o_
                                for b in range(nb):
                                    mm = pe.matmul(out[HD * o_:HD * o_ + HD, 0:P],
                                                   VA[:, n - nb + 1 + b, HD * kv:HD * kv + HD],
                                                   PTB[k % 2][:, P * (nb * o_ + b):P * (nb * o_ + b) + P],
                                                   start=(b == 0), stop=(b == nb - 1))
                            filled(mm)
                    n_ = ("pv", N_ATT - 1)
                    pe.wait_ge(freed(n_), AUX_NO[n_] // 4 + 1)
                    for j in range(4):
                        dense(("wo", j), lambda k: OA[:, k, :])
                layer_norm(2 * layer)
                for j in range(22):
                    dense(("gu", layer, j), xr)
                pe.wait_ge(sem(f"hidden{layer}"), 22)
                for j in range(4):
                    dense(("down", layer, j), lambda k: HIDE[:, k, :])
                layer_norm(2 * layer + 1)
                for j in range(4):
                    dense(("ple_g", layer, j), xr)
                pe.wait_ge(sem("p_in"), 16 * (layer + 1))
                for j in range(4):
                    dense(("ple_w", layer, j), lambda k: PT[:, k, :])

        block = ctx.enter_context(nc.Block())

        def finish(sp_):
            sp_.wait_ge(sem("result"), 1)
            sp_.dma_start(out_t, XF).then_inc(sem("stored"), 16)
            sp_.wait_ge(sem("stored"), 16)

        @block.sync
        def _(sp_):
            sp_.dma_start(XF, x_t).then_inc(sem("x_in"), 16)
            sp_.dma_start(par[:, :], params).then_inc(sem("par_in"), 16)

            def load(i):
                u = UNIT_NO[i]
                _, nk, nco, _ = PLAN[i]
                if u >= RING:
                    sp_.wait_ge(sem("units_done"), u - RING + 1)
                lo = (u % RING) * UNIT
                sp_.dma_start(ring[:, lo:lo + nk * nco], w_dense[i, :, 0:nk * nco])\
                   .then_inc(sem(f"ring_full{u % RING}"), 16)

            for i in range(N_FIRST):
                load(i)
            if stop == 1:
                return finish(sp_)
            moe_sync(sp_)
            if stop == 2:
                return finish(sp_)
            for i in range(N_FIRST, len(PLAN)):
                load(i)
            second_sync(sp_)
            finish(sp_)

        @block.gpsimd
        def _(pool):
            step = Steps(pool, sem("pool_step"))
            step(pool.memset(masks[:, :], 1.0))
            step(pool.memset(blk, 0.0))
            step(pool.memset(blk[0:HD, 0:HD], 1.0))
            step(pool.memset(blk[HD:P, HD:P], 1.0))
            step(pool.memset(reset[:, :], 1.0))
            step(pool.memset(reset[:, :].rearrange("p (c t) -> p c t", c=NCH)[:, :, 0:1], 0.0))
            step(pool.affine_select(out=ident, in_=ident, compare_op=ALU.is_equal, fill=0.0, base=0,
                                    pattern=[[-1, P]], channel_multiplier=1))
            step(pool.affine_select(out=strict_u, in_=strict_u, compare_op=ALU.is_gt, fill=0.0,
                                    base=0, pattern=[[1, P]], channel_multiplier=-1))
            step(pool.affine_select(out=pair[:, 1, :], in_=pair[:, 1, :], compare_op=ALU.is_ge, fill=0.0,
                                    base=0, pattern=[[1, P]], channel_multiplier=-1))
            for i, m in enumerate(level):
                b = 1 << i
                v = m.rearrange("p (n w) -> p n w", w=2 * b)
                step(pool.memset(v[:, :, 0:b], 0.0))
                second = v[:, :, b:2 * b]
                step(pool.affine_select(out=second, in_=second, compare_op=ALU.is_ge, fill=0.0, base=0,
                                        pattern=[[-2 * b, P // (2 * b)], [0, b]], channel_multiplier=1))
                step(pool.affine_select(out=second, in_=second, compare_op=ALU.is_ge, fill=0.0, base=b - 1,
                                        pattern=[[2 * b, P // (2 * b)], [0, b]], channel_multiplier=-1))
            pool.nop().then_inc(sem("consts"), 1)
            u = last_unit(("gm1",))
            loaded(pool, u)
            ws = ring_of(u, 1, UNIT)[:, 0, 0:1024].rearrange("p (h t) -> p h t", h=8)
            pool.affine_select(out=ws, in_=ws, compare_op=ALU.is_ge, fill=0.0, base=0,
                               pattern=[[0, 8], [1, P]], channel_multiplier=-1).then_inc(sem("ws_causal"), 1)
            if stop == 1:
                return
            moe_pool(pool, step)
            if stop == 2:
                return
            second_pool(pool, step)

        @block.scalar
        def _(act):
            step = Steps(act, sem("act_step"))
            roots = [0]

            def root(ap):
                roots[0] += 1
                act.wait_ge(sem("root_in"), roots[0])
                act.activation(ap, ap, ACT.Sqrt).then_inc(sem("root_out"), 1)

            act.wait_ge(sem("x_in"), 16)
            act.activation(YF, XF, ACT.Square).then_inc(sem("sq1"), 1)
            act.wait_ge(sem("par_in"), 16)
            root(small[:, :])
            for k in range(KT):
                act.wait_ge(sem("xn1"), k + 1)
                act.activation(H[:, k, :], H[:, k, :], ACT.Identity, scale=gain[:, k:k + 1],
                               bias=mod[:, k:k + 1]).then_inc(sem("h1"), 1)
            for h in range(2):
                group_ready(act, ("zv", h))
                act.activation(VTOK[:, 2 * h:2 * h + 2, :], dbank(("zv", h)), ACT.Gelu_apprx_tanh)\
                   .then_inc(group_freed(("zv", h)), 1)
            for h in range(2):
                group_ready(act, ("zu", h))
                act.activation(YC[:, 2 * h:2 * h + 2, :], dbank(("zu", h)), ACT.Gelu_apprx_tanh)\
                   .then_inc(group_freed(("zu", h)), 1)
            root(small[:, 48:52])
            act.wait_ge(sem("omm"), 1)
            n = 0
            for name, buf in (("r", R), ("k", K), ("v", V)):
                for h in range(2):
                    group_ready(act, (name, h))
                    for b in range(2):
                        j = 2 * h + b
                        act.activation(buf[:, j, :], dbank((name, h))[:, b, :], ACT.Identity,
                                       scale=gain[:, 8 + n:9 + n]).then_inc(sem("shift_a"), 1)
                        n += 1
            for g, b, w, i in LORAS:
                if b == 0:
                    group_ready(act, g)
                act.activation(LO[0:w, i, :], dbank(g)[0:w, b, :], ACT.Identity,
                               scale=gain[0:w, 8 + n:9 + n]).then_inc(sem("shift_a"), 1)
                n += 1
            act.wait_ge(sem("shift_b"), 13)
            act.activation(LO[0:32, 0, :], LO[0:32, 0, :], ACT.Tanh).then_inc(sem("lora_w"), 1)
            act.wait_ge(sem("shift_b"), 15)
            act.activation(LO[0:96, 2, :], LO[0:96, 2, :], ACT.Sigmoid).then_inc(sem("lora_g"), 1)
            for j in range(4):
                ready(act, ("wl", j))
                act.activation(C[:, j, :], bank(("wl", j)), ACT.Sigmoid, bias=pc("w0", j))\
                   .then_inc(freed(("wl", j)), 1)
            for j in range(4):
                ready(act, ("al", j))
                act.activation(A[:, j, :], bank(("al", j)), ACT.Sigmoid, bias=pc("a0", j))\
                   .then_inc(freed(("al", j)), 1)
            act.wait_ge(sem("kk_raw"), 1)
            act.activation(EF, KKF, ACT.Square).then_inc(sem("kk_sq"), 1)
            for _ in range(4):
                root(T1[:, 0, :])
            act.wait_ge(sem("cum"), 1)
            act.activation(gain[:, 32:48], gain[:, 48:64], ACT.Exp).then_inc(sem("chunk_gain"), 1)
            for k_, name in ((0, "exp_r"), (1, "exp_a"), (2, "exp_b")):
                act.wait_ge(sem("cum"), k_ + 1)
                if k_ == 0:
                    ready(act, ("gm", 3))
                    act.activation(VTMP, EF, ACT.Exp).then_inc(sem(name), 1)
                elif k_ == 1:
                    act.activation(CF, CF, ACT.Exp).then_inc(sem(name), 1)
                else:
                    act.activation(EF, EF, ACT.Exp, scale=-1.0).then_inc(sem(name), 1)
            for c in range(NCH):
                for nm, buf in (("bt", BTK), ("kt", KTK), ("vt", VTK)):
                    ready(act, (nm, c))
                    if c > 0:
                        ready(act, ("st", c - 1))
                    act.activation(buf, bank((nm, c)), ACT.Copy).then_inc(freed((nm, c)), 1)
                for lv in range(LEVELS):
                    for q in range(2):
                        ready(act, ("u", c, lv, q))
                        act.activation(UI[:, 512 * q:512 * q + 512], bank(("u", c, lv, q)), ACT.Copy)\
                           .then_inc(freed(("u", c, lv, q)), 1)
                ready(act, ("u0", c))
                act.activation(UU, bank(("u0", c)), ACT.Copy).then_inc(freed(("u0", c)), 1)
                ready(act, ("sa", c))
                act.activation(SAS, bank(("sa", c)), ACT.Copy).then_inc(freed(("sa", c)), 1)
                ready(act, ("y", c))
                act.activation(V[:, :, P * c:P * c + P],
                               bank(("y", c)).rearrange("p (j t) -> p j t", j=4), ACT.Copy)\
                   .then_inc(freed(("y", c)), 1)
            for j in range(4):
                act.wait_ge(sem("gn_c"), j + 1)
                act.activation(C[:, j, :], E[:, j, :], ACT.Square).then_inc(sem("gn_sq"), 1)
            for _ in range(4):
                root(T1[:, 0, :])
            if stop == 1:
                return
            moe_act(act, step, root)
            if stop == 2:
                return
            second_act(act, step, root)

        @block.vector
        def _(dve):
            step = Steps(dve, sem("dve_step"))

            asked = [0]

            def inv_sqrt(ins, ap):
                asked[0] += 1
                ins.then_inc(sem("root_in"), 1)
                dve.wait_ge(sem("root_out"), asked[0])
                step(dve.reciprocal(ap, ap))

            def take(name, ins):
                ins.then_inc(freed(name), 1)
                dve.wait_ge(freed(name), AUX_NO[name] // 4 + 1)

            dve.wait_ge(sem("par_in"), 16)
            lo = PCOL["mu_r"][0]
            dve.tensor_scalar(gain[:, 8:23], par[:, lo:lo + 15], -1.0, 1.0, ALU.mult, ALU.add)\
               .then_inc(sem("omm"), 1)
            step(dve.tensor_scalar(gain[:, 24:28], pc("k_a"), -1.0, 1.0, ALU.mult, ALU.add))
            ready(dve, ("ss", 1))
            take(("ss", 1), dve.tensor_scalar(small[:, :], bank(("ss", 1)), 1.0 / D, 1e-6, ALU.mult, ALU.add))
            inv_sqrt(dve.nop(), small[:, :])
            ready(dve, ("mod",))
            take(("mod",), dve.tensor_tensor(mod[:, :], bank(("mod",))[:, 0:48], pc("ada_b"), ALU.add))
            step(dve.scalar_tensor_tensor(gain[:, 0:8], mod[:, 8:16], 1.0, pc("norm1_g"), ALU.add, ALU.mult))
            for k in range(KT):
                dve.tensor_tensor(H[:, k, :], X[:, k, :], small[:, :], ALU.mult).then_inc(sem("xn1"), 1)

            st6, agg = small[:, 0:24], small[:, 32:40]
            for h in range(2):
                dve.wait_ge(group_freed(("zv", h)), GROUP_NO[("zv", h)] // 2 + 1)
            for m in range(4):
                step(dve.bn_stats(st6[:, 6 * m:6 * m + 6], VTOK[:, m, :]))
                step(dve.bn_aggr(agg[:, 2 * m:2 * m + 2], st6[:, 6 * m:6 * m + 6]))
            var = agg.rearrange("p (m a) -> p m a", a=2)[:, :, 1]
            inv_sqrt(dve.tensor_scalar(small[:, 48:52], var, 1e-5, None, ALU.add), small[:, 48:52])
            g1 = ring_of(last_unit(("gm1",)), 1, UNIT)[:, 0, :]
            g2 = ring_of(last_unit(("gm2",)), 4, 512)
            for m in range(4):
                step(dve.tensor_scalar(VTOK[:, m, :], VTOK[:, m, :], agg[:, 2 * m:2 * m + 1],
                                       small[:, 48 + m:49 + m], ALU.subtract, ALU.mult))

            n = 0
            for name, buf in (("r", R), ("k", K), ("v", V)):
                for h in range(2):
                    for b in range(2):
                        j = 2 * h + b
                        dve.wait_ge(sem("shift_a"), n + 1)
                        ins = dve.scalar_tensor_tensor(
                            buf[:, j, 1:SEQ], dbank((name, h))[:, b, 0:SEQ - 1], pc("mu_r", n),
                            buf[:, j, 1:SEQ], ALU.mult, ALU.add)
                        ins.then_inc(sem("shift_b"), 1)
                        n += 1
                    dve.wait_ge(sem("shift_b"), n)
                    dve.nop().then_inc(group_freed((name, h)), 1)
            for g, b, w, i in LORAS:
                dve.wait_ge(sem("shift_a"), n + 1)
                dve.scalar_tensor_tensor(LO[0:w, i, 1:SEQ], dbank(g)[0:w, b, 0:SEQ - 1],
                                         pc("mu_r", n)[0:w], LO[0:w, i, 1:SEQ], ALU.mult, ALU.add)\
                   .then_inc(sem("shift_b"), 1)
                n += 1
                if b == 1 or i == 2:
                    dve.wait_ge(sem("shift_b"), n)
                    dve.nop().then_inc(group_freed(g), 1)

            loaded(dve, last_unit(("gm1",)))
            loaded(dve, last_unit(("gm2",)))
            for m in range(4):
                step(dve.tensor_tensor(VTOK[:, m, :], VTOK[:, m, :], g1[:, 1024:1536], ALU.mult))
                dve.tensor_tensor(VTOK[:, m, :], VTOK[:, m, :], g1[:, 1536:2048], ALU.add)\
                   .then_inc(sem("v_norm"), 1)
            for j in range(4):
                ins = dve.tensor_scalar(KK[:, j, :], K[:, j, :], pc("k_k", j), None, ALU.mult)
            step(ins)
            dve.nop().then_inc(sem("kk_raw"), 1)
            for j in range(4):
                dve.wait_ge(freed(("al", j)), AUX_NO[("al", j)] // 4 + 1)
                step(dve.tensor_scalar(T1[:, 0, :], A[:, j, :], pc("k_a", j), gain[:, 24 + j:25 + j],
                                       ALU.mult, ALU.add))
                step(dve.tensor_tensor(K[:, j, :], K[:, j, :], T1[:, 0, :], ALU.mult))
            for j in range(4):
                ready(dve, ("kn", j))
                take(("kn", j), dve.tensor_scalar(T1[:, 0, :], bank(("kn", j)), 1e-24, None, ALU.max))
                inv_sqrt(dve.nop(), T1[:, 0, :])
                step(dve.tensor_tensor(KK[:, j, :], KK[:, j, :], T1[:, 0, :], ALU.mult))
                step(dve.tensor_tensor(A[:, j, :], A[:, j, :], KK[:, j, :], ALU.mult))
            for j in range(4):
                dve.wait_ge(sem("kk_sq"), 1)
                ready(dve, ("kn", 3))
                dve.scalar_tensor_tensor(E[:, j, :], R[:, j, :], pc("r_k", j), K[:, j, :],
                                         ALU.mult, ALU.mult).then_inc(sem("rk"), 1)
            for j in range(4):
                ready(dve, ("bon", j))
                take(("bon", j), dve.tensor_tensor(YC[:, 4 + j, :], bank(("bon", j)), V[:, j, :], ALU.mult))
            step(dve.tensor_scalar(CF, CF, -float(np.exp(-0.5)), None, ALU.mult))
            for j in range(4):
                ready(dve, ("bon", 3))
                step(dve.tensor_tensor_scan(E[:, j, :], reset[:, :], C[:, j, :], 0.0, ALU.mult, ALU.add))
            half = small[:, 64:80]
            cum = EF.rearrange("p (g t) -> p g t", t=P)
            step(dve.tensor_scalar(half, cum[:, :, P - 1], 0.5, None, ALU.mult))
            hv = half.rearrange("p (j c) -> p j c", c=4)
            gv = gain[:, 48:64].rearrange("p (j c) -> p j c", c=4)
            step(dve.tensor_tensor(gv[:, :, 0:3], hv[:, :, 0:3], hv[:, :, 1:4], ALU.add))
            step(dve.tensor_copy(gv[:, :, 3:4], hv[:, :, 3:4]))
            step(dve.tensor_tensor(cum, cum, half.unsqueeze(2).to_broadcast([P, 16, P]), ALU.subtract))
            dve.nop().then_inc(sem("cum"), 1)
            step(dve.tensor_tensor(CF, EF, CF, ALU.subtract))
            dve.nop().then_inc(sem("cum"), 1)
            dve.wait_ge(sem("exp_r"), 1)
            dve.nop().then_inc(sem("cum"), 1)
            arr = [AR[:, j, :, 1, :] for j in range(4)]
            ara = [AR[:, j, :, 0, :] for j in range(4)]

            def cv(t, j):
                return t[:, j, :].rearrange("p (c t) -> p c t", c=4)
            vt = VTMP.rearrange("p (k t) -> p k t", k=4)
            for j in range(4):
                dve.tensor_tensor(arr[j], cv(R, j), cv(vt, j), ALU.mult).then_inc(sem("ar"), 1)
            dve.wait_ge(sem("exp_a"), 1)
            for j in range(4):
                dve.scalar_tensor_tensor(ara[j], cv(KK, j), -1.0, cv(C, j), ALU.mult, ALU.mult)\
                   .then_inc(sem("ar"), 1)
            dve.wait_ge(sem("exp_b"), 1)
            for j in range(4):
                dve.tensor_tensor(A[:, j, :], A[:, j, :], E[:, j, :], ALU.mult).then_inc(sem("bk"), 1)
                dve.tensor_tensor(K[:, j, :], K[:, j, :], E[:, j, :], ALU.mult).then_inc(sem("bk"), 1)
            dve.wait_ge(sem("bk"), 8)
            dve.wait_ge(sem("ar"), 8)
            for c in range(4):
                n_ = ("gm", c)
                ready(dve, n_)
                bs = g2[:, 0, :].rearrange("p (j t) -> p j t", j=4)
                t1 = T1[:, 0, :].rearrange("p (j t) -> p j t", j=4)
                take(n_, dve.tensor_tensor(t1, bank(n_).rearrange("p (j t) -> p j t", j=4), bs, ALU.add))
                step(dve.tensor_tensor(YC[:, 0:4, P * c:P * c + P], YC[:, 0:4, P * c:P * c + P], t1, ALU.mult))
            dve.nop().then_inc(sem("ya"), 1)

            for c in range(NCH):
                for q in range(4):
                    for nm, buf in (("ab", AB), ("ak", AK)):
                        pass
                for nm, buf in (("ab", AB), ("ak", AK)):
                    for q in range(4):
                        n_ = (nm, c, q)
                        ready(dve, n_)
                        if c > 0:
                            ready(dve, ("y", c - 1))
                        take(n_, dve.tensor_tensor(
                            buf[:, 4 * (q // 2) + q % 2:4 * (q // 2) + q % 2 + 3:2], bank(n_).rearrange("p (h a t) -> p h a t", h=2, a=2),
                            pair.unsqueeze(1).to_broadcast([P, 2, 2, P]), ALU.mult))
                idb = ident.unsqueeze(1).to_broadcast([P, 8, P])
                lmv, xiv, xtv = (t.rearrange("p (h t) -> p h t", h=8) for t in (LM, XI, XT))
                for lv in range(LEVELS):
                    if lv > 0:
                        ready(dve, ("u", c, lv - 1, 1))
                    step(dve.tensor_tensor(lmv, AB[:, :, 0, :], level[lv].unsqueeze(1).to_broadcast([P, 8, P]),
                                           ALU.mult))
                    dve.nop().then_inc(sem("lm"), 1)
                    if lv == 0:
                        step(dve.tensor_tensor(xtv, lmv, idb, ALU.add))
                        for q in range(2):
                            n_ = ("u", c, lv, q)
                            ready(dve, n_)
                            dve.wait_ge(freed(n_), AUX_NO[n_] // 4 + 1)
                            qs = slice(4 * q, 4 * q + 4)
                            step(dve.tensor_tensor(xiv[:, qs], UI.rearrange("p (h t) -> p h t", h=8)[:, qs],
                                                   idb[:, qs], ALU.add))
                            dve.nop().then_inc(sem("x_new"), 1)
                        continue
                    if lv < LEVELS - 1:
                        for q in range(2):
                            n_ = ("xn", c, lv, q)
                            ready(dve, n_)
                            take(n_, dve.tensor_tensor(XI[:, 512 * q:512 * q + 512], XI[:, 512 * q:512 * q + 512],
                                                       bank(n_), ALU.add))
                    for q in range(2):
                        n_ = ("xt", c, lv, q)
                        ready(dve, n_)
                        take(n_, dve.tensor_tensor(XT[:, 512 * q:512 * q + 512], XT[:, 512 * q:512 * q + 512],
                                                   bank(n_), ALU.add))
                        dve.nop().then_inc(sem("x_new"), 1)
                if c < NCH - 1:
                    n_ = ("st", c)
                    ready(dve, n_)
                    fac = gain[:, 32:48].rearrange("p (j c) -> p j c", c=4)[:, :, c:c + 1]\
                        .to_broadcast([P, 4, P])
                    stv = ST.rearrange("p (j v) -> p j v", j=4)
                    t1v = T2[:, :].rearrange("p (j v) -> p j v", j=4)
                    psv = bank(n_).rearrange("p (j v) -> p j v", j=4)
                    blkb = blk.unsqueeze(1).to_broadcast([P, 4, P])
                    dve.wait_ge(sem("chunk_gain"), 1)
                    take(n_, dve.tensor_tensor(t1v, psv, blkb, ALU.mult))
                    if c > 0:
                        step(dve.tensor_tensor(t1v, t1v, stv, ALU.add))
                    step(dve.tensor_tensor(stv, t1v, fac, ALU.mult))
                    dve.nop().then_inc(sem("state"), 1)

            for c in range(NCH):
                dve.wait_ge(freed(("y", c)), AUX_NO[("y", c)] // 4 + 1)
            for j in range(4):
                n_ = ("gnm", j)
                ready(dve, n_)
                take(n_, dve.scalar_tensor_tensor(E[:, j, :], bank(n_), -1.0 / HD, V[:, j, :], ALU.mult, ALU.add))
                dve.nop().then_inc(sem("gn_c"), 1)
            for j in range(4):
                n_ = ("gnv", j)
                ready(dve, n_)
                take(n_, dve.tensor_scalar(T1[:, 0, :], bank(n_), 1.0 / HD, 64e-5, ALU.mult, ALU.add))
                inv_sqrt(dve.nop(), T1[:, 0, :])
                step(dve.tensor_tensor(E[:, j, :], E[:, j, :], T1[:, 0, :], ALU.mult))
                step(dve.tensor_scalar(E[:, j, :], E[:, j, :], pc("gn_w", j), pc("gn_b", j), ALU.mult, ALU.add))
                step(dve.tensor_tensor(YC[:, 4 + j, :], YC[:, 4 + j, :], E[:, j, :], ALU.add))
            for j in range(4):
                n_ = ("gg", j)
                ready(dve, n_)
                take(n_, dve.tensor_tensor(YC[:, 4 + j, :], YC[:, 4 + j, :], bank(n_), ALU.mult))
            dve.nop().then_inc(sem("yb"), 1)
            for h in range(4):
                group_ready(dve, ("w_out", h))
                for b in range(2):
                    j = 2 * h + b
                    step(dve.scalar_tensor_tensor(X[:, j, :], dbank(("w_out", h))[:, b, :], mod[:, 16 + j:17 + j],
                                                  X[:, j, :], ALU.mult, ALU.add))
                dve.nop().then_inc(group_freed(("w_out", h)), 1)
            if stop == 1:
                dve.nop().then_inc(sem("result"), 1)
                return
            moe_vector(dve, step, take, inv_sqrt)
            if stop == 2:
                return
            second_vector(dve, step, take, inv_sqrt)

        @block.tensor
        def _(pe):
            done_aux = [0]

            def aux(name):
                n = done_aux[0]
                assert AUX[n] == name, (AUX[n], name)
                done_aux[0] += 1
                if n >= 4:
                    pe.wait_ge(sem(f"aux_free{n % 4}"), n // 4)
                return psA[:, n % 4, :]

            def filled(mm):
                mm.then_inc(sem("aux_ready"), 1)

            def dense(group, rhs, widths=(P, P)):
                n = GROUP_NO[group]
                if n >= 2:
                    pe.wait_ge(sem(f"pair_free{n % 2}"), n // 2)
                units = UNITS_OF[group]
                k0, total = 0, sum(nk for _, nk, _ in units)
                for u, nk, nco in units:
                    loaded(pe, u)
                    w = ring_of(u, nk, nco)
                    off = 0
                    for b, width in enumerate(widths):
                        for k in range(nk):
                            mm = pe.matmul(psD[0:width, n % 2, b, :], w[:, k, off:off + width], rhs(k0 + k),
                                           start=(k0 + k == 0), stop=(k0 + k == total - 1))
                        off += width
                    mm.then_inc(sem("units_done"), 1)
                    k0 += nk

            def colsum(name, src, tiles, m=ones):
                out = aux(name)
                for k in range(tiles):
                    mm = pe.matmul(out, m, src(k), start=(k == 0), stop=(k == tiles - 1))
                filled(mm)

            pe.wait_ge(sem("consts"), 1)
            pe.wait_ge(sem("sq1"), 1)
            colsum(("ss", 1), lambda k: YC[:, k, :], KT)
            pe.wait_ge(sem("par_in"), 16)
            out = aux(("mod",))
            for j in range(24):
                u, nk, nco = UNITS_OF[("ada", j)][0]
                loaded(pe, u)
                w = ring_of(u, nk, nco)
                for b in range(2):
                    for k in range(KT):
                        mm = pe.matmul(out[:, 2 * j + b:2 * j + b + 1], w[:, k, P * b:P * b + P],
                                       pc("c", k), start=(k == 0), stop=(k == KT - 1))
                mm.then_inc(sem("units_done"), 1)
            pe.matmul(out[:, 48:49], ident, pc("c", 0), start=True, stop=True).then_inc(sem("aux_ready"), 1)

            pe.wait_ge(sem("h1"), KT)
            zu = UNITS_OF[("zv",)]
            for h in range(2):
                for i, (u, nk, nco) in enumerate(zu):
                    loaded(pe, u)
                    w = ring_of(u, nk, nco)
                    for b in range(2):
                        m = 2 * h + b
                        for k in range(nk):
                            mm = pe.matmul(psD[:, h, b, :], H[:, 4 * i + k, P * m:P * m + P], w[:, k, :],
                                           start=(4 * i + k == 0), stop=(4 * i + k == KT - 1))
                    if h == 1:
                        mm.then_inc(sem("units_done"), 1)
                if h == 0:
                    mm.then_inc(sem("zv_first"), 1)
            for name in ("zu", "r", "k", "v"):
                for h in range(2):
                    dense((name, h), lambda k: H[:, k, :])
            dense(("lora_wa",), lambda k: H[:, k, :], (32, 32))
            dense(("lora_g",), lambda k: H[:, k, :], (96,))

            u1, u2 = last_unit(("gm1",)), last_unit(("gm2",))
            g2 = ring_of(u2, 4, 512)
            ws = ring_of(u1, 1, UNIT)[:, 0, 0:1024].rearrange("p (h t) -> p h t", h=8)
            loaded(pe, u2)
            pe.wait_ge(sem("lora_w"), 1)
            for j in range(4):
                filled(pe.matmul(aux(("wl", j)), g2[0:32, 1, P * j:P * j + P], LO[0:32, 0, :], start=True, stop=True))
            for j in range(4):
                filled(pe.matmul(aux(("al", j)), g2[0:32, 2, P * j:P * j + P], LO[0:32, 1, :], start=True, stop=True))
            pe.wait_ge(sem("kk_sq"), 1)
            for j in range(4):
                filled(pe.matmul(aux(("kn", j)), blk, E[:, j, :], start=True, stop=True))
            for j in range(4):
                pe.wait_ge(sem("rk"), j + 1)
                filled(pe.matmul(aux(("bon", j)), blk, E[:, j, :], start=True, stop=True))
            pe.wait_ge(sem("ws_causal"), 1)
            for c in range(4):
                pe.wait_ge(sem("v_norm"), c + 1)
                out = aux(("gm", c))
                for h in range(8):
                    mm = pe.matmul(out[HD * (h % 2):HD * (h % 2) + HD, P * (h // 2):P * (h // 2) + P],
                                   VTOK[:, c, HD * h:HD * h + HD], ws[:, h, :], start=True, stop=True)
                filled(mm)

            pe.wait_ge(sem("bk"), 8)
            for c in range(NCH):
                tk = slice(P * c, P * c + P)
                for nm, src in (("bt", A), ("kt", K), ("vt", V)):
                    out = aux((nm, c))
                    for j in range(4):
                        mm = pe.transpose(out[:, P * j:P * j + P], src[:, j, tk], ident)
                    filled(mm)
                pe.wait_ge(sem("ar"), 8)
                for nm, src in (("ab", A), ("ak", K)):
                    for q in range(4):
                        out = aux((nm, c, q))
                        hp = slice(HD * (q % 2), HD * (q % 2) + HD)
                        for i in range(2):
                            j = 2 * (q // 2) + i
                            mm = pe.matmul(out[:, 256 * i:256 * i + 256], src[hp, j, tk],
                                           AR[hp, j, c, :, :].rearrange("p a t -> p (a t)"), start=True, stop=True)
                        filled(mm)

                def hs(t, h):
                    return t[:, P * h:P * h + P]
                for lv in range(LEVELS):
                    pe.wait_ge(sem("lm"), LEVELS * c + lv + 1)
                    for q in range(2):
                        out = aux(("u", c, lv, q))
                        if lv > 0:
                            pe.wait_ge(sem("x_new"), 2 * (LEVELS * c + lv - 1) + q + 1)
                        for i in range(4):
                            mm = pe.matmul(out[:, P * i:P * i + P], hs(LM, 4 * q + i),
                                           ident if lv == 0 else hs(XI, 4 * q + i), start=True, stop=True)
                        filled(mm)
                    if lv == 0:
                        continue
                    if lv < LEVELS - 1:
                        for q in range(2):
                            n_ = ("u", c, lv, q)
                            out = aux(("xn", c, lv, q))
                            pe.wait_ge(freed(n_), AUX_NO[n_] // 4 + 1)
                            for i in range(4):
                                mm = pe.matmul(out[:, P * i:P * i + P], hs(XT, 4 * q + i), hs(UI, 4 * q + i),
                                               start=True, stop=True)
                            filled(mm)
                    for q in range(2):
                        n_ = ("u", c, lv, q)
                        out = aux(("xt", c, lv, q))
                        pe.wait_ge(freed(n_), AUX_NO[n_] // 4 + 1)
                        for i in range(4):
                            mm = pe.matmul(out[:, P * i:P * i + P], hs(UI, 4 * q + i), hs(XT, 4 * q + i),
                                           start=True, stop=True)
                        filled(mm)
                pe.wait_ge(sem("x_new"), 2 * LEVELS * (c + 1))
                if c > 0:
                    pe.wait_ge(sem("state"), c)
                out = aux(("u0", c))
                for h in range(8):
                    j = h // 2
                    if c > 0 and h % 2 == 0:
                        pe.matmul(out[:, P * j:P * j + P], AR[:, j, c, 0, :], ST[:, P * j:P * j + P],
                                  start=True, stop=False, skip_group_check=True)
                    mm = pe.matmul(out[:, HD * h:HD * h + HD], AK[:, h, 0, :], VTK[:, HD * h:HD * h + HD],
                                   start=(c == 0), stop=(c == 0 or h % 2 == 1), skip_group_check=(c > 0))
                filled(mm)
                out = aux(("sa", c))
                pe.wait_ge(freed(("u0", c)), AUX_NO[("u0", c)] // 4 + 1)
                for h in range(8):
                    mm = pe.matmul(out[:, HD * h:HD * h + HD], hs(XT, h), UU[:, HD * h:HD * h + HD],
                                   start=True, stop=True)
                filled(mm)
                out = aux(("y", c))
                pe.wait_ge(freed(("sa", c)), AUX_NO[("sa", c)] // 4 + 1)
                for h in range(8):
                    j, hp = h // 2, slice(HD * (h % 2), HD * (h % 2) + HD)
                    o_ = out[hp, P * j:P * j + P]
                    if c > 0:
                        pe.matmul(o_, ST[:, HD * h:HD * h + HD], AR[:, j, c, 1, :], start=True, stop=False)
                    pe.matmul(o_, SAS[:, HD * h:HD * h + HD], AB[:, h, 1, :], start=(c == 0), stop=False)
                    mm = pe.matmul(o_, VTK[:, HD * h:HD * h + HD], AK[:, h, 1, :], start=False, stop=True)
                filled(mm)
                if c < NCH - 1:
                    out = aux(("st", c))
                    for j in range(4):
                        ts_ = slice(P * j, P * j + P)
                        pe.matmul(out[:, ts_], BTK[:, ts_], SAS[:, ts_], start=True, stop=False)
                        mm = pe.matmul(out[:, ts_], KTK[:, ts_], VTK[:, ts_], start=False, stop=True)
                    filled(mm)
            for c in range(NCH):
                pe.wait_ge(freed(("y", c)), AUX_NO[("y", c)] // 4 + 1)
            for j in range(4):
                filled(pe.matmul(aux(("gnm", j)), blk, V[:, j, :], start=True, stop=True))
            for j in range(4):
                pe.wait_ge(sem("gn_sq"), j + 1)
                filled(pe.matmul(aux(("gnv", j)), blk, C[:, j, :], start=True, stop=True))
            pe.wait_ge(sem("lora_g"), 1)
            for j in range(4):
                mm = pe.matmul(aux(("gg", j)), g2[0:96, 3, P * j:P * j + P], LO[0:96, 2, :], start=True, stop=True)
                filled(mm)
            pe.wait_ge(sem("ya"), 1)
            pe.wait_ge(sem("yb"), 1)
            pe.nop().then_inc(sem("units_done"), 1)
            pe.nop().then_inc(sem("units_done"), 1)
            for h in range(4):
                dense(("w_out", h), lambda k: YC[:, k, :])
            if stop == 1:
                return
            moe_tensor(pe, aux, filled, dense, colsum)
            if stop == 2:
                return
            second_tensor(pe, aux, filled, dense, colsum)

STOP = None



def kernel(**inputs):
    from concourse import bacc
    from concourse.bass_utils import run_bass_kernel_spmd

    a = {k: np.asarray(v) for k, v in inputs.items()}
    dense = np.zeros((len(PLAN), P, UNIT), np.float32)
    for i, (_, nk, nco, fill) in enumerate(PLAN):
        dense[i, :, 0:nk * nco] = np.asarray(fill(a)).reshape(P, nk * nco)
    arrays = {
        "x_t": np.ascontiguousarray(a["x"][0].T.reshape(KT, P, SEQ).transpose(1, 0, 2)).reshape(P, KT * SEQ),
        "params": np.ascontiguousarray(np.concatenate(
            [np.asarray(fill(a)).reshape(P, w) for _, w, fill in PARAMS], 1)),
        "w_dense": dense,
        "p_t": np.ascontiguousarray(a["p_2"][:, 0].transpose(0, 2, 1).reshape(2, 2, P, SEQ).transpose(0, 2, 1, 3)),
        "moe_gate": np.ascontiguousarray(a["moe_w_gate"][0]),
        "moe_up": np.ascontiguousarray(a["moe_w_up"][0]),
        "moe_down": np.ascontiguousarray(a["moe_w_down"][0]),
    }
    nc = bacc.Bacc("TRN2", target_bir_lowering=False, num_devices=1)
    args = [nc.dram_tensor(n, v.shape, mybir.dt.from_np(v.dtype), kind="ExternalInput").ap()
            for n, v in arrays.items()]
    out = nc.dram_tensor("out_t", (P, KT * SEQ), F32, kind="ExternalOutput").ap()
    build(nc, *args, out, stop=STOP)
    got = run_bass_kernel_spmd(nc, [arrays], core_ids=[0]).results[0]["out_t"]
    return np.ascontiguousarray(np.asarray(got).reshape(P, KT, SEQ).transpose(2, 1, 0)).reshape(1, SEQ, D)
```

```python
from contextlib import ExitStack

import numpy as np

import concourse.bass as bass
from concourse import mybir

ALU = mybir.AluOpType
ACT = mybir.ActivationFunctionType
AX = mybir.AxisListType
F32 = mybir.dt.float32
I32 = mybir.dt.int32
F32R = mybir.dt.float32r

P = 128
SEQ = 512
D = 1024
KT = D // P
NCH = SEQ // P
HD = 64
LEVELS = 7
RAW = 4
RING = 8
UNIT = 2048
N_EXP = 32
N_GRP = 4
EPG = N_EXP // N_GRP
HID = 512
CAP = 128
MAX_OVER = 2 * SEQ // CAP - 1
SPLIT = SEQ // CAP
SBUF_AT = 16512
FF = 2816
FT = FF // P
HS = FT // 2 + 1
GATE_TILES = (range(HS), range(HS, FT))
HALF_UNITS = (((0, 6), (6, 5)), ((11, 6), (17, 5)))
ALPHA = 4 ** 0.25
NEG = -1e30
N_ATT = NCH * 8


Q_HEADS = [(2 * m + o) * 4 + g for m in range(2) for g in range(4) for o in range(2)]
Q_CHANNELS = np.array([h * HD + d for h in Q_HEADS for d in range(HD)])


def chan(v):
    v = np.asarray(v).reshape(-1)
    n = -(-v.size // P)
    out = np.zeros((n * P,), v.dtype)
    out[: v.size] = v
    return out.reshape(n, P).T


def every(v):
    v = np.asarray(v).reshape(-1)
    return np.broadcast_to(v, (P, v.size))


def rows(w, k0, nk, cols):
    w = np.asarray(w)[k0 * P:(k0 + nk) * P][:, cols]
    return w.reshape(nk, P, -1).transpose(1, 0, 2)


MU = [("mu_r", 0, 512), ("mu_k", 512, 1024), ("mu_v", 1024, 1536), ("mu_xw", 1536, 1568),
      ("mu_xa", 1568, 1600), ("mu_xg", 1600, 1696)]
PARAMS = [
    ("c", 8, lambda a: chan(a["c"])), ("ada_b", 48, lambda a: chan(a["ada_b"][0])),
    ("norm1_g", 8, lambda a: chan(a["norm1_g"][0])), ("norm2_g", 8, lambda a: chan(a["norm2_g"][0])),
    ("final_g", 8, lambda a: chan(a["final_norm_g"])),
] + [(n, -(-(hi - lo) // P), lambda a, lo=lo, hi=hi: chan(a["rwkv_mu"][0][lo:hi])) for n, lo, hi in MU] + [
    (n, 4, lambda a, key=key: chan(a[key][0]))
    for n, key in [("w0", "rwkv_w0"), ("a0", "rwkv_a0"), ("k_k", "rwkv_k_k"), ("k_a", "rwkv_k_a"),
                   ("r_k", "rwkv_r_k"), ("gn_w", "rwkv_gn_w"), ("gn_b", "rwkv_gn_b")]
] + [
    ("conv_w", 48, lambda a: np.concatenate([chan(a["ssd_conv_w_2"][0][t]) for t in range(4)], 1)),
    ("conv_b", 12, lambda a: chan(a["ssd_conv_b_2"][0])),
    ("sc_w", 24, lambda a: np.concatenate([chan(a["sc_conv_w_2"][0][t]) for t in range(3)], 1)),
    ("d_skip", 8, lambda a: chan(np.repeat(np.asarray(a["ssd_d_2"][0]), HD))),
    ("ssd_nw", 8, lambda a: chan(a["ssd_norm_w_2"][0])),
    ("dt_b", 1, lambda a: chan(a["ssd_dt_bias_2"][0])), ("a_log", 1, lambda a: chan(a["ssd_a_log_2"][0])),
    ("ln_mix_g", 16, lambda a: chan(a["ln_mix_g_2"])), ("ln_mix_b", 16, lambda a: chan(a["ln_mix_b_2"])),
    ("ln_ffn_g", 16, lambda a: chan(a["ln_ffn_g_2"])), ("ln_ffn_b", 16, lambda a: chan(a["ln_ffn_b_2"])),
    ("b_q", 8, lambda a: chan(np.asarray(a["b_qkv_2"][0])[Q_CHANNELS])),
    ("b_k", 2, lambda a: chan(a["b_qkv_2"][0][1024:1280])),
    ("b_o", 8, lambda a: chan(a["b_o_2"][0])), ("b_ple", 16, lambda a: chan(a["b_ple_gate_2"])),
    ("router_w", 288, lambda a: np.concatenate(
        [rows(a["router_group_w"][0], 0, 8, slice(None)), rows(a["router_expert_w"][0], 0, 8, slice(None))], 2)),
    ("router_b", 36, lambda a: every(np.concatenate([a["router_group_b"][0], a["router_expert_b"][0]]))),
    ("b_v", 256, lambda a: every(a["b_qkv_2"][0][1280:1536])),
    ("sinks", 16, lambda a: every(np.asarray(a["attn_sinks_2"][0])[Q_HEADS])),
]
PCOL, _n = {}, 0
for _name, _width, _ in PARAMS:
    PCOL[_name] = (_n, _width)
    _n += _width
N_PAR = _n


def cols(lo, hi):
    return slice(lo, hi)


def gm1(a):
    ws = np.asarray(a["gmlp_ws"][0]).transpose(2, 0, 1).reshape(P, 1024)
    return np.concatenate([ws, every(a["gmlp_ln_w"][0]), every(a["gmlp_ln_b"][0])], 1)


def gm2(a):
    out = np.zeros((P, 4, 512), np.float32)
    bs = np.asarray(a["gmlp_bs"][0])
    for j in range(4):
        for o in range(2):
            out[64 * o:64 * o + 64, 0, P * j:P * j + P] = bs[2 * j + o]
    out[0:32, 1] = np.asarray(a["rwkv_w2"][0])
    out[0:32, 2] = np.asarray(a["rwkv_a2"][0])
    out[0:96, 3] = np.asarray(a["rwkv_g2"][0])
    return out.reshape(P, UNIT)


def dense_plan():
    plan = []

    def unit(group, nk, nc, fill):
        plan.append((group, nk, nc, fill))

    def mat(group, key, layer, columns, k0=0, nk=KT):
        n = len(range(*columns.indices(1 << 20))) if isinstance(columns, slice) else len(columns)
        unit(group, nk, n, lambda a: rows(a[key][layer], k0, nk, columns))

    for j in range(8):
        mat(("ada", j), "ada_w", 0, cols(256 * j, 256 * j + 256))
    for h in range(2):
        mat(("zv",), "w_in", 0, cols(512, 1024), 4 * h, 4)
    for name, lo in (("zu", 0), ("r", 1024), ("k", 1536), ("v", 2048)):
        for j in range(2):
            mat((name, j), "w_in", 0, cols(lo + 256 * j, lo + 256 * j + 256))
    mat(("lora_wa",), "w_in", 0, cols(2560, 2624))
    mat(("lora_g",), "w_in", 0, cols(2624, 2720))

    for j in range(8, 24):
        mat(("ada", j), "ada_w", 0, cols(256 * j, 256 * j + 256))
    for j in range(4):
        mat(("w_out", j), "w_out", 0, cols(256 * j, 256 * j + 256))
    n_first = len(plan)

    for j in range(8):
        mat(("sc_ch", j), "w_in_mix_2", 0,
            np.r_[3600 + P * j:3728 + P * j, 4624 + P * j:4752 + P * j])
    for j in range(4):
        mat(("sc_b", j), "w_in_mix_2", 0, cols(2576 + 256 * j, 2832 + 256 * j))
    for j in range(6):
        mat(("xbc", j), "w_in_mix_2", 0, cols(1024 + 256 * j, 1280 + 256 * j))
    mat(("dt",), "w_in_mix_2", 0, cols(2560, 2576))
    for j in range(4):
        mat(("z", j), "w_in_mix_2", 0, cols(256 * j, 256 * j + 256))
    for j in range(4):
        for h in (1, 0):
            mat(("mix_out", j), "w_out_mix_2", 0, cols(256 * j, 256 * j + 256), 8 * h)

    def ffn(layer):
        for half in range(2):
            for j in GATE_TILES[half]:
                unit(("gu", layer, j), KT, 256, lambda a, j=j: np.concatenate(
                    [rows(a["w_ffn_gate_2"][layer], 0, 8, cols(P * j, P * j + P)),
                     rows(a["w_ffn_up_2"][layer], 0, 8, cols(P * j, P * j + P))], 2))
            for j in range(4):
                for k0, nk in HALF_UNITS[half]:
                    mat(("down", layer, half, j), "w_ffn_down_2", layer, cols(256 * j, 256 * j + 256), k0, nk)
        for j in range(4):
            mat(("ple_g", layer, j), "w_ple_gate_2", layer, cols(256 * j, 256 * j + 256))
        for j in range(4):
            mat(("ple_w", layer, j), "w_ple_2", layer, cols(256 * j, 256 * j + 256), 0, 2)

    ffn(0)
    for j in range(4):
        mat(("q", j), "w_qkv_2", 0, Q_CHANNELS[256 * j:256 * j + 256])
    mat(("kk",), "w_qkv_2", 0, cols(1024, 1280))
    mat(("vv",), "w_qkv_2", 0, cols(1280, 1536))
    for j in range(4):
        unit(("wo", j), KT, 256, lambda a, j=j: rows(
            np.asarray(a["w_o_2"][0])[Q_CHANNELS], 0, 8, cols(256 * j, 256 * j + 256)))
    ffn(1)
    return plan, n_first


PLAN, N_FIRST = dense_plan()
MOE_UNITS = 6 * N_EXP
SPLIT_UNITS = [i for i, p in enumerate(PLAN) if p[0][0] not in ("ada",)]
SPLIT_NO = {i: n for n, i in enumerate(SPLIT_UNITS)}
UNITS_OF = {}
for _i, (_g, _nk, _nc, _) in enumerate(PLAN):
    UNITS_OF.setdefault(_g, []).append((_i, _nk, _nc))
GROUPS = [g for g in dict.fromkeys(p[0] for p in PLAN) if g[0] not in ("ada", "zv")]
GROUPS = [("zv", 0), ("zv", 1)] + GROUPS
GROUP_NO = {g: i for i, g in enumerate(GROUPS)}


def aux_plan():
    a = [("ss", 1)] + [("mr", 0, j) for j in range(8)] + [("mod",)]
    a += [("wl", j) for j in range(4)] + [("al", j) for j in range(4)]
    a += [("kn", j) for j in range(4)] + [("bon", j) for j in range(4)]
    a += [("gm", c) for c in range(4)]
    for c in range(NCH):
        a += [("bt", c), ("kt", c), ("vt", c)]
        a += [("ab", c, q) for q in range(4)] + [("ak", c, q) for q in range(4)]
        for lv in range(LEVELS):
            a += [("u", c, lv, q) for q in range(2)]
            if 1 <= lv <= 4:
                a += [("mr", c + 1, lv - 1)]
            if lv > 0:
                for q in range(2):
                    if lv < LEVELS - 1:
                        a += [("xn", c, lv, q)]
                    a += [("xt", c, lv, q)]
                if lv in (2, 4):
                    a += [("mo", c, lv // 2 - 1)]
        a += [("u0", c), ("sa", c), ("y", c)] + ([("st", c)] if c < NCH - 1 else [])
    a += [("gnm", j) for j in range(4)] + [("gnv", j) for j in range(4)] + [("gg", j) for j in range(4)]
    a += [("ss", 2), ("lg",)] + [("ht", m, h) for m in range(4) for h in range(2)] + [("rank",), ("idx",)]
    a += [("comb", m, h) for m in range(4) for h in range(2)] + [("ss", 3)]
    a += [("da_t",), ("last",)]
    a += [("bct", c) for c in range(4)] + [("xst", c, h) for c in range(4) for h in range(2)]
    a += [("cb", g) for g in range(2)]
    a += [("stt", c, g) for c in range(3) for g in range(2)]
    a += [("acs", 0), ("acs", 1)]
    for j in range(8):
        a += [("acs", h) for h in (2 * j + 2, 2 * j + 3) if h < 16] + [("yd", j)]
    a += [("gss", g) for g in range(2)]
    for layer in range(2):
        if layer == 1:
            for i in range(N_ATT + 3):
                a += [("sc", i)] if i < N_ATT else []
                a += [("pt", i - 2)] if 2 <= i < N_ATT + 2 else []
                a += [("pv", i - 3)] if i >= 3 else []
        for which in ("mix", "ffn"):
            a += [("lnm", which, layer), ("lnv", which, layer)]
    return a


AUX = aux_plan()
AUX_NO = {name: i for i, name in enumerate(AUX)}
assert len(AUX_NO) == len(AUX)


def act_split_plan():
    a = [(n, k) for n in ("h1", "yc", "x0", "z") for k in range(KT)]
    a += [("ys", k) for k in range(8, 16)] + [("ys", k) for k in range(8)]
    for layer in range(2):
        if layer == 1:
            a += [(n, k) for n in ("q", "oa") for k in range(KT)]
        a += [(("gu", layer), k) for k in range(KT)] + [(("hid", layer), j) for j in range(FT)]
        a += [(("ple", layer), k) for k in range(KT)] + [(("pt", layer), k) for k in range(2)]
    return a


PART_NO = {name: i for i, name in enumerate(act_split_plan())}



class Named:

    def __init__(self, nc, ctx):
        self.nc, self.ctx, self.made = nc, ctx, {}

    def __call__(self, name):
        if name not in self.made:
            self.made[name] = self.ctx.enter_context(self.nc.semaphore(name))
        return self.made[name]


class Steps:

    def __init__(self, eng, sem):
        self.eng, self.sem, self.n = eng, sem, 0

    def __call__(self, ins):
        self.n += 1
        ins.then_inc(self.sem, 1)
        self.eng.wait_ge(self.sem, self.n)


def last_unit(group):
    return UNITS_OF[group][-1][0]


def build(nc, x_t, params, w_dense, p_t, moe_gate, moe_up, moe_down, out_t, stop=None):
    ctx = ExitStack()
    with ctx:
        at_byte = [SBUF_AT]

        def sb(name, cols_):
            at = at_byte[0]
            at_byte[0] += -(-cols_ * 4 // 32) * 32
            return nc.alloc_sbuf_tensor_at(name, [P, cols_], F32, offset=at)

        sem = Named(nc, ctx)
        ring = sb("ring", RING * UNIT)
        ring_r = nc.alloc_sbuf_tensor_at("ring_r", [P, 4 * UNIT], F32R, offset=SBUF_AT + RAW * UNIT * 4)
        par = sb("par", N_PAR)
        masks = sb("masks", 12 * P)
        reset = sb("reset", SEQ)
        mod = sb("mod", 48)
        gain = sb("gain", 64)
        arena_at = at_byte[0]
        arena = sb("arena", 33600)
        rounded = {}
        psD = ctx.enter_context(nc.psum_tensor("psD", [P, 2, 2, 512], F32))
        psA = ctx.enter_context(nc.psum_tensor("psA", [P, 4, 512], F32))

        ident, ones, blk = (masks[:, P * i:P * i + P] for i in range(3))
        strict_u = masks[:, 3 * P:4 * P]
        pair = masks[:, 3 * P:5 * P].rearrange("p (a t) -> p a t", a=2)
        level = [masks[:, (5 + i) * P:(6 + i) * P] for i in range(LEVELS)]

        def pc(name, j=None, n=1):
            lo, w = PCOL[name]
            return par[:, lo:lo + w] if j is None else par[:, lo + j:lo + j + n]

        def flat(lo, n):
            return arena[:, lo:lo + n]

        def area(lo, tiles):
            return arena[:, lo:lo + tiles * SEQ].rearrange("p (k t) -> p k t", k=tiles)

        X, H, YC = area(0, 8), area(4096, 8), area(8192, 8)
        XF, HF, YF = flat(0, 4096), flat(4096, 4096), flat(8192, 4096)
        o = 12288
        R, K, V, KK, A, C, E = (area(o + 2048 * i, 4) for i in range(7))
        RF, KF, VF, KKF, AF, CF, EF = (flat(o + 2048 * i, 2048) for i in range(7))
        LO = area(o + 14336, 3)
        sp = o + 14336 + 1536
        BTK, KTK, VTK, UU, SAS = (flat(sp + 512 * i, 512) for i in range(5))
        ST, T2 = flat(sp + 2560, 512), flat(sp + 3072, 512)
        VTOK = area(sp + 2816, 4)
        T1 = area(sp + 1536, 1)
        NB = area(sp, 4)
        small = flat(sp + 4864, 512)
        AR = HF.rearrange("p (j c a t) -> p j c a t", j=4, c=4, a=2)

        def ring_of(u, nk, nco):
            lo = (u % RAW) * UNIT
            return ring[:, lo:lo + nk * nco].rearrange("p (k n) -> p k n", k=nk)

        def bank(name):
            return psA[:, AUX_NO[name] % 4, :]

        def dbank(group):
            return psD[:, GROUP_NO[group] % 2, :, :]

        def ready(eng, name):
            eng.wait_ge(sem("aux_ready"), AUX_NO[name] + 1)

        def freed(name):
            return sem(f"aux_free{AUX_NO[name] % 4}")

        def group_ready(eng, group):
            eng.wait_ge(sem("units_done"), last_unit(("zv",) if group[0] == "zv" else group) + 1)

        def group_freed(group):
            return sem(f"pair_free{GROUP_NO[group] % 2}")

        def loaded(eng, u):
            eng.wait_ge(sem(f"ring_full{u % RAW}"), 16 * (u // RAW + 1))

        def parts_of(u, nk, nco):
            lo = 2 * (SPLIT_NO[u] % 2) * UNIT
            return [ring_r[:, lo + UNIT * i:lo + UNIT * i + nk * nco].rearrange("p (k n) -> p k n", k=nk)
                    for i in range(2)]

        def area_r(lo, tiles):
            if (lo, tiles) not in rounded:
                rounded[lo, tiles] = nc.alloc_sbuf_tensor_at(f"rounded{lo}_{tiles}", [P, tiles * SEQ], F32R,
                                                             offset=arena_at + 4 * lo)
            return rounded[lo, tiles][:, :].rearrange("p (k t) -> p k t", k=tiles)

        def parts(hi, lo, tiles):
            return area_r(hi, tiles), area_r(lo, tiles)

        class Ahead:

            def __init__(self, cut):
                self.cut, self.n, self.limit = cut, 0, N_FIRST - 1

            def __call__(self, u):
                while self.n < len(SPLIT_UNITS) and SPLIT_UNITS[self.n] <= min(u, self.limit):
                    self.cut(self.n)
                    self.n += 1

            def enter(self, group):
                self(last_unit(("zv",) if group[0] == "zv" else group) + 1)

            def leave(self, group):
                self(last_unit(("zv",) if group[0] == "zv" else group) + 2)

        def part_ready(eng, name, k):
            eng.wait_ge(sem("x_lo"), PART_NO[(name, k)] + 1)

        def part_hi_ready(eng, name, k):
            eng.wait_ge(sem("x_hi"), PART_NO[(name, k)] + 1)

        g1_at, g2_at = ((RAW + 2 * (SPLIT_NO[last_unit((g,))] % 2)) * UNIT for g in ("lora_g", "lora_wa"))
        G1, G2 = ring[:, g1_at:g1_at + UNIT], ring[:, g2_at:g2_at + UNIT].rearrange("p (k n) -> p k n", k=4)

        LORAS = [(("lora_wa",), 0, 32, 0), (("lora_wa",), 1, 32, 1), (("lora_g",), 0, 96, 2)]
        VTMP = flat(sp + 2816, 2048)
        LM = [CF[:, 0:1024], flat(o + 14336, 1024)]
        UI = CF[:, 1024:2048]
        MROW0, MROW = flat(sp, 2048), small
        H_P = parts(o + 3 * 2048, o + 5 * 2048, 8)
        YC_P = parts(o, o + 4 * 2048, 8)
        XI, XT = EF[:, 0:1024], EF[:, 1024:2048]
        AB = RF.rearrange("p (h a t) -> p h a t", h=8, a=2)
        AK = KKF.rearrange("p (h a t) -> p h a t", h=8, a=2)

        BLOCKS = N_EXP + MAX_OVER
        X0_P = parts(14336, 27648, 8)
        row_token = nc.dram_tensor("row_token", (BLOCKS * CAP, 1), F32, kind="Internal").ap()
        token_rows = nc.dram_tensor("token_rows", (SEQ, D), F32, kind="Internal").ap()
        block_out = nc.dram_tensor("block_out", (BLOCKS * CAP, D), F32, kind="Internal").ap()
        spare = nc.dram_tensor("spare", (2, P), F32, kind="Internal").ap()
        ints = nc.alloc_sbuf_tensor_at("ints", [P, 64], I32, offset=at_byte[0])
        idx = ints[:, 0:BLOCKS]
        pos_i = ints[:, 40:48]
        over_i = ints[:, 48:56]

        MB = 8192
        HT = flat(MB, 4096).rearrange("p (m d) -> p m d", m=4)
        msmall = flat(MB + 4096, 2560)
        at = [0]

        def take_small(n, *shape):
            lo = at[0]
            at[0] += n
            v = msmall[:, lo:lo + n]
            if len(shape) == 2:
                return v.rearrange("p (a b) -> p a b", a=shape[0])
            if len(shape) == 3:
                return v.rearrange("p (a b c) -> p a b c", a=shape[0], b=shape[1])
            return v
        LG, GD, GE, GV, OHG = (take_small(n, 4, n // 4) for n in (144, 16, 16, 16, 16))
        GM, GP, GS, M1, M2, E2, W1, W2, T4 = (take_small(4, 4, 1) for _ in range(9))
        SEL, D1, V8, OH1, SEL2, OH2 = (take_small(32, 4, 8) for _ in range(6))
        TMP = take_small(128, 4, 8, 4)
        OHA, OHB = take_small(128, 4, 4, 8), take_small(128, 4, 4, 8)
        OHS, RK, QQ, TA, TB = (take_small(128, 4, 32) for _ in range(5))
        CNT, OVB, INC, BAS, ONE = (take_small(32) for _ in range(5))
        POS, EO = take_small(8, 2, 4), take_small(8)
        DESC = take_small(8)
        EID, TOK = take_small(32), take_small(4)
        ZERO, TSB = take_small(P), take_small(P)

        XG = [flat(MB + 6656 + 1024 * i, 1024) for i in range(2)]
        XO = flat(MB + 8704, 1024)
        SG, HB, HO = (flat(MB + 10752 + 512 * i, 512) for i in range(3))
        XEP = [area_r(MB + 8704 + 1024 * i, 2) for i in range(2)]
        XEP = [[v, w] for v, w in zip(XEP, (area_r(MB + 22528 + 1024 * i, 2) for i in range(2)))]
        HTP = [area_r(MB + 11776, 1), area_r(MB + 24576, 1)]
        W3 = area_r(MB + 18432, 8)
        YS = [flat(MB + 12288 + 1024 * i, 1024) for i in range(2)]
        YG = [flat(MB + 14336 + 1024 * i, 1024) for i in range(4)]
        gate_bank, up_bank, y_banks = psD[:, 0, 0, :], psD[:, 0, 1, :], psD[:, 1, :, :]
        x_banks, h_bank = psA[:, 0:2, :], psA[:, 2, :]
        PARTS = 3
        USED0, CUT0 = PARTS, RAW

        def expert_parts(j):
            b = j % PARTS
            if b < 2:
                return [ring_r[:, (2 * b + i) * UNIT:(2 * b + i + 1) * UNIT] for i in range(2)]
            return [W3.rearrange("p k t -> p (k t)")[:, i * UNIT:(i + 1) * UNIT] for i in range(2)]

        def bc(ap, shape, axis):
            return ap.unsqueeze(axis).to_broadcast(shape)

        def expert_unit(e, j, tile):
            if j < 4:
                w = moe_gate if j < 2 else moe_up
                k0 = (j % 2) * 4 * P
                src = w[e, k0:k0 + 4 * P, :].rearrange("e (k p) n -> p (e k) n", p=P)
                return tile.rearrange("p (k n) -> p k n", k=4), src
            k0 = (j - 4) * 2 * P
            src = moe_down[e, k0:k0 + 2 * P, :].rearrange("e (k p) n -> p (e k) n", p=P)
            return tile.rearrange("p (k n) -> p k n", k=2), src

        def slot_tile(s):
            return ring[:, s * UNIT:(s + 1) * UNIT]

        def moe_sync(sp_):
            sp_.wait_ge(sem("units_done"), N_FIRST)
            with sp_.Fori(0, N_EXP // 4) as i:
                for s in range(4):
                    for j in range(6):
                        v = 6 * s + j
                        sp_.wait_ge(sem("m_lo"), i * 24 + (v + 1))
                        sp_.wait_ge(sem("x_in"), 16)
                        dst, src = expert_unit(bass.ds(i * 4 + s, 1), j, slot_tile(v % RAW))
                        sp_.dma_start(dst, src).then_inc(sem(f"m_full{v % RAW}"), 16)
            for j in range(PARTS):
                sp_.wait_ge(sem("m_lo"), MOE_UNITS + j + 1)
                dst, src = expert_unit(slice(N_EXP - 1, N_EXP), j, slot_tile(j % RAW))
                sp_.dma_start(dst, src).then_inc(sem(f"m_full{j % RAW}"), 16)
            sp_.wait_ge(sem("m_used"), USED0 + MOE_UNITS)
            sp_.wait_ge(sem("m_lo"), CUT0 + MOE_UNITS + PARTS)
            sp_.wait_ge(sem("over_ready"), 1)
            n_over = sp_.value_load(over_i[0:1, 7:8], min_val=0, max_val=MAX_OVER)
            with sp_.If(n_over > 0):
                for b in range(MAX_OVER):
                    ex = sp_.value_load(over_i[0:1, b:b + 1], min_val=0, max_val=N_EXP - 1)
                    for j in range(6):
                        dst, src = expert_unit(bass.ds(ex, 1), j, slot_tile(j))
                        sp_.dma_start(dst, src).then_inc(sem("o_weights"), 16)
                    sp_.wait_ge(sem("o_stored"), (b + 1) * 16)

        def moe_pool(pool, step):
            pool.wait_ge(sem("moe_start"), 1)
            step(pool.iota(TOK, [[P, 4]], base=0, channel_multiplier=1, allow_small_or_imprecise_dtypes=True))
            step(pool.iota(EID, [[1, 32]], base=0, channel_multiplier=0, allow_small_or_imprecise_dtypes=True))
            step(pool.iota(DESC, [[-1, 8]], base=8, channel_multiplier=0, allow_small_or_imprecise_dtypes=True))
            step(pool.memset(ONE, 1.0))
            step(pool.memset(ZERO, 0.0))
            step(pool.memset(YG[0], 0.0))
            pool.nop().then_inc(sem("moe_consts"), 1)
            for b in range(N_EXP, BLOCKS):
                pool.dma_start(block_out[b * CAP:(b + 1) * CAP, :], YG[0]).then_inc(sem("blocks_zero"), 16)
            table = row_token.rearrange("(b p) a -> b (p a)", p=CAP)
            pool.dma_start(table, ZERO[0:BLOCKS, :]).then_inc(sem("table_zero"), 16)
            pool.wait_ge(sem("table_zero"), 16)
            pool.wait_ge(sem("pos_ready"), 1)
            for ch in range(2):
                for m in range(4):
                    pool.indirect_dma_start(
                        row_token, bass.IndirectOffsetOnAxis(ap=pos_i[:, 4 * ch + m:4 * ch + m + 1], axis=0),
                        TOK[:, m:m + 1], None).then_inc(sem("table_set"), 16)
            pool.wait_ge(sem("table_set"), 128)
            pool.dma_start(TSB[0:BLOCKS, :], table).then_inc(sem("table_in"), 16)
            pool.wait_ge(sem("idx_ready"), 1)
            pool.wait_ge(sem("rows_out"), 16 * 4)

            for e in range(2):
                pool.indirect_dma_start(XG[e], None, token_rows,
                                        bass.IndirectOffsetOnAxis(ap=idx[:, e:e + 1], axis=0))\
                    .then_inc(sem(f"xg_in{e}"), 16)
            for e in range(2, N_EXP + 2):
                buf = e % 2
                pool.wait_ge(sem("xt_ready"), e - 1)
                pool.indirect_dma_start(XG[buf], None, token_rows,
                                        bass.IndirectOffsetOnAxis(ap=idx[:, e:e + 1], axis=0))\
                    .then_inc(sem(f"xg_in{buf}"), 16)
            n_over = pool.value_load(over_i[0:1, 7:8], min_val=0, max_val=MAX_OVER)
            for b_ in range(2):
                pool.wait_ge(sem(f"xg_in{b_}"), 16 * (N_EXP // 2 + 1))
            pool.wait_ge(sem("xt_ready"), N_EXP + 1)
            with pool.If(n_over > 0):
                for b in range(MAX_OVER):
                    pool.indirect_dma_start(XG[0], None, token_rows,
                                            bass.IndirectOffsetOnAxis(ap=idx[:, N_EXP + b:N_EXP + b + 1], axis=0))\
                        .then_inc(sem("o_x"), 16)
                    pool.wait_ge(sem("o_stored"), (b + 1) * 16)
            pool.wait_ge(sem("blocks_zero"), 16 * MAX_OVER)
            pool.wait_ge(sem("blocks_out"), 1)
            for m in range(4):
                for ch in range(2):
                    if m >= 2:
                        pool.wait_ge(sem("combined"), m - 1)
                    pool.indirect_dma_start(
                        YG[2 * (m % 2) + ch], None, block_out,
                        bass.IndirectOffsetOnAxis(ap=pos_i[:, 4 * ch + m:4 * ch + m + 1], axis=0))\
                        .then_inc(sem(f"y_in{m % 2}"), 16)

        def moe_act(act, step, root, ahead, x_hi):
            for k in range(KT):
                act.wait_ge(sem("x_mixed"), k + 1)
                act.activation(YC[:, k, :], X[:, k, :], ACT.Square).then_inc(sem("sq2"), 1)
            root(small[:, :])
            for k in range(KT):
                act.wait_ge(sem("xn2"), k + 1)
                act.activation(H[:, k, :], H[:, k, :], ACT.Identity, bias=mod[:, 24 + k:25 + k])\
                   .then_inc(sem("h2"), 1)
            for b in range(2):
                act.dma_start(spare[b:b + 1, :], ident[0:1, :]).then_inc(sem(f"y_stored{b}"), 16)
            act.wait_ge(sem("gd"), 1)
            act.activation(GE, GD, ACT.Exp).then_inc(sem("ge"), 1)
            for m in range(4):
                if m == 2:
                    act.wait_ge(sem("e2_in"), 1)
                    act.activation(E2, E2, ACT.Exp).then_inc(sem("e2"), 1)
                for h in range(2):
                    n_ = ("ht", m, h)
                    ready(act, n_)
                    act.activation(HT[:, m, 512 * h:512 * h + 512], bank(n_), ACT.Copy).then_inc(freed(n_), 1)
                    act.wait_ge(freed(n_), AUX_NO[n_] // 4 + 1)
                act.dma_start(token_rows[P * m:P * m + P, :], HT[:, m, :]).then_inc(sem("rows_out"), 16)

            def x_copy(count, buf):
                act.wait_ge(sem("xt_ready"), count)
                act.activation(XEP[buf][0], x_banks, ACT.Copy).then_inc(sem("xe_hi"), 1)

            def m_cut(i, v):
                act.wait_ge(sem(f"m_full{v % RAW}"), (i * 6 + (v // RAW + 1)) * 16)
                act.wait_ge(sem("m_used"), i * 24 + (v + 1))
                act.activation(expert_parts(v)[0], slot_tile(v % RAW), ACT.Copy).then_inc(sem("m_hi"), 1)

            act.wait_ge(sem("idx_ready"), 1)
            act.wait_ge(sem("units_done"), N_FIRST)
            act.nop().then_inc(sem("m_used"), USED0)
            act.nop().then_inc(sem("y_copied"), 1)
            for v in range(PARTS):
                m_cut(0, v)
            x_copy(1, 0)
            with act.Fori(0, N_EXP // 4) as i:
                for s in range(4):
                    e = i * 4 + (s + 1)
                    m_cut(i, 6 * s + 3)
                    act.wait_ge(sem("m_used"), i * 24 + (USED0 + 6 * s + 2))
                    act.wait_ge(sem("h_done"), e)
                    act.activation(SG, gate_bank, ACT.Silu).then_inc(sem("silu_done"), 1)
                    m_cut(i, 6 * s + 4)
                    x_copy(i * 4 + (s + 2), (s + 1) % 2)
                    act.wait_ge(sem("ht_ready"), e)
                    act.activation(HTP[0][:, 0, :], h_bank, ACT.Copy).then_inc(sem("ht_hi"), 1)
                    m_cut(i, 6 * s + 5)
                    for v in range(6 * s + 6, 6 * s + 9):
                        m_cut(i, v)
                    act.wait_ge(sem("m_used"), i * 24 + (USED0 + 6 * s + 6))
                    act.wait_ge(sem(f"y_stored{s % 2}"), (i * 2 + (s // 2 + 1)) * 16)
                    act.activation(YS[s % 2], y_banks, ACT.Copy).then_inc(sem("y_copied"), 1)
                    act.wait_ge(sem("y_copied"), i * 4 + (s + 2))
                    act.dma_start(block_out.rearrange("(b p) d -> b p d", p=CAP)[bass.ds(i * 4 + s, 1), :, :]
                                  .rearrange("b p d -> p (b d)"), YS[s % 2])\
                       .then_inc(sem(f"y_stored{s % 2}"), 16)
            for b in range(2):
                act.wait_ge(sem(f"y_stored{b}"), 16 * (N_EXP // 2 + 1))
            act.wait_ge(sem("blocks_zero"), 16 * MAX_OVER)
            n_over = act.value_load(over_i[0:1, 7:8], min_val=0, max_val=MAX_OVER)
            with act.If(n_over > 0):
                with act.Fori(0, MAX_OVER) as b:
                    act.wait_ge(sem("o_xt"), b + 1)
                    act.activation(XO, x_banks, ACT.Copy).then_inc(sem("o_xe"), 1)
                    act.wait_ge(sem("o_gu"), b + 1)
                    act.activation(SG, gate_bank, ACT.Silu).then_inc(sem("o_sg"), 1)
                    act.wait_ge(sem("o_y"), b + 1)
                    act.activation(YS[0], y_banks, ACT.Copy).then_inc(sem("o_ys"), 1)
                    act.wait_ge(sem("o_ys"), b + 1)
                    act.dma_start(block_out.rearrange("(b p) d -> b p d", p=CAP)[bass.ds(b + N_EXP, 1), :, :]
                                  .rearrange("b p d -> p (b d)"), YS[0]).then_inc(sem("o_stored"), 16)
                    act.wait_ge(sem("o_stored"), (b + 1) * 16)
            act.nop().then_inc(sem("blocks_out"), 1)
            ahead.limit = len(PLAN)
            ahead(N_FIRST + 1)
            for h in range(2):
                act.wait_ge(sem("x_moe"), 7 + h)
                act.activation(HF[:, 2048 * h:2048 * h + 2048], XF[:, 2048 * h:2048 * h + 2048], ACT.Square)\
                   .then_inc(sem("sq3"), 1)
            root(small[:, :])
            for k in range(KT):
                act.wait_ge(sem("x_final"), k + 1)
                x_hi(X0_P[0][:, k, :], X[:, k, :])

        def moe_vector(dve, step, take, inv_sqrt, ahead, x_lo):
            dve.nop().then_inc(sem("m_lo"), CUT0)
            dve.nop().then_inc(sem("moe_start"), 1)
            step(dve.scalar_tensor_tensor(gain[:, 0:8], mod[:, 32:40], 1.0, pc("norm2_g"), ALU.add, ALU.mult))
            ready(dve, ("ss", 2))
            take(("ss", 2), dve.tensor_scalar(small[:, :], bank(("ss", 2)), 1.0 / D, 1e-6, ALU.mult, ALU.add))
            inv_sqrt(dve.nop(), small[:, :])
            for k in range(KT):
                dve.scalar_tensor_tensor(H[:, k, :], X[:, k, :], gain[:, k:k + 1], small[:, :],
                                         ALU.mult, ALU.mult).then_inc(sem("xn2"), 1)
            dve.wait_ge(sem("moe_consts"), 1)
            lgb = ("lg",)
            ready(dve, lgb)
            take(lgb, dve.tensor_tensor(LG, bank(lgb)[:, 0:144].rearrange("p (m e) -> p m e", m=4),
                                        bc(pc("router_b"), [P, 4, 36], 1), ALU.add))

            def top(values, top_v, diff, weight, onehot, n):
                step(dve.tensor_reduce(top_v, values, AX.X, ALU.max))
                step(dve.tensor_tensor(diff, values, top_v.to_broadcast([P, 4, n]), ALU.subtract))
                step(dve.scalar_tensor_tensor(weight, diff, 0.0, bc(DESC[:, 0:n], [P, 4, n], 1),
                                              ALU.is_equal, ALU.mult))
                step(dve.tensor_reduce(T4, weight, AX.X, ALU.max))
                step(dve.tensor_tensor(onehot, weight, T4.to_broadcast([P, 4, n]), ALU.is_equal))

            top(LG[:, :, 0:4], GM, GD, GV, OHG, 4)
            dve.nop().then_inc(sem("gd"), 1)
            dve.wait_ge(sem("ge"), 1)
            step(dve.tensor_reduce(GS, GE, AX.X, ALU.add))
            step(dve.reciprocal(GP, GS))
            le = LG[:, :, 4:36].rearrange("p m (g e) -> p m e g", g=4)
            step(dve.tensor_tensor(TMP, le, bc(OHG, [P, 4, 8, 4], 2), ALU.mult))
            step(dve.tensor_reduce(SEL, TMP, AX.X, ALU.add))
            top(SEL, M1, D1, V8, OH1, 8)
            step(dve.scalar_tensor_tensor(SEL2, OH1, NEG, SEL, ALU.mult, ALU.add))
            top(SEL2, M2, D1, V8, OH2, 8)
            dve.tensor_tensor(E2, M2, M1, ALU.subtract).then_inc(sem("e2_in"), 1)
            dve.wait_ge(sem("e2"), 1)
            step(dve.tensor_scalar(T4, E2, 1.0, None, ALU.add))
            step(dve.reciprocal(T4, T4))
            step(dve.tensor_tensor(W1, GP, T4, ALU.mult))
            step(dve.tensor_tensor(W2, W1, E2, ALU.mult))
            for oh, full in ((OH1, OHA), (OH2, OHB)):
                step(dve.tensor_tensor(full, bc(OHG, [P, 4, 4, 8], 3), bc(oh, [P, 4, 4, 8], 2), ALU.mult))
            f32v = "p m g e -> p m (g e)"
            A32, B32 = OHA.rearrange(f32v), OHB.rearrange(f32v)
            step(dve.tensor_tensor(OHS, A32, B32, ALU.add))
            dve.nop().then_inc(sem("onehots"), 1)
            rk = ("rank",)
            ready(dve, rk)
            step(dve.tensor_copy(RK, bank(rk)[:, 0:128].rearrange("p (m e) -> p m e", m=4)))
            take(rk, dve.tensor_copy(CNT, bank(rk)[:, 128:160]))
            step(dve.tensor_scalar(OVB, CNT, float(CAP), None, ALU.is_gt))
            for n in range(2, SPLIT):
                step(dve.scalar_tensor_tensor(OVB, CNT, float(n * CAP), OVB, ALU.is_gt, ALU.add))
            step(dve.tensor_tensor_scan(INC, ONE, OVB, 0.0, ALU.mult, ALU.add))
            step(dve.tensor_tensor(BAS, INC, OVB, ALU.subtract))
            step(dve.scalar_tensor_tensor(BAS, EID, -1.0, BAS, ALU.mult, ALU.add))
            step(dve.tensor_scalar(BAS, BAS, float(N_EXP - 1), None, ALU.add))
            step(dve.tensor_scalar(QQ, RK, float(CAP), None, ALU.is_ge))
            for n in range(2, SPLIT):
                step(dve.scalar_tensor_tensor(QQ, RK, float(n * CAP), QQ, ALU.is_ge, ALU.add))
            step(dve.tensor_tensor(TA, QQ, bc(BAS, [P, 4, 32], 1), ALU.add))
            step(dve.scalar_tensor_tensor(TA, QQ, 0.0, TA, ALU.is_gt, ALU.mult))
            step(dve.tensor_tensor(TA, TA, QQ, ALU.subtract))
            step(dve.tensor_tensor(TA, TA, bc(EID, [P, 4, 32], 1), ALU.add))
            step(dve.scalar_tensor_tensor(TA, TA, float(CAP), RK, ALU.mult, ALU.add))
            for ch, oh in ((0, A32), (1, B32)):
                step(dve.tensor_tensor(TB, oh, TA, ALU.mult))
                step(dve.tensor_reduce(POS[:, ch, :], TB, AX.X, ALU.add))
            dve.tensor_copy(pos_i, POS.rearrange("p c m -> p (c m)")).then_inc(sem("pos_ready"), 1)
            for b in range(MAX_OVER):
                step(dve.tensor_scalar(TB[:, 0, :], INC, float(b), None, ALU.is_le))
                step(dve.tensor_reduce(EO[:, b:b + 1], TB[:, 0, :], AX.X, ALU.add))
            step(dve.tensor_scalar(EO[:, 0:MAX_OVER], EO[:, 0:MAX_OVER], float(N_EXP - 1), None, ALU.min))
            step(dve.tensor_copy(EO[:, 7:8], INC[:, 31:32]))
            dve.tensor_copy(over_i, EO).then_inc(sem("over_ready"), 1)
            ix = ("idx",)
            ready(dve, ix)
            dve.tensor_copy(idx, bank(ix)[:, 0:BLOCKS]).then_inc(freed(ix), 1)
            dve.wait_ge(freed(ix), AUX_NO[ix] // 4 + 1)
            dve.nop().then_inc(sem("idx_ready"), 1)

            def m_cut(i, v):
                dve.wait_ge(sem("m_hi"), i * 24 + (v + 1))
                hi, lo_ = expert_parts(v)
                dve.tensor_tensor(lo_, slot_tile(v % RAW), hi, ALU.subtract).then_inc(sem("m_lo"), 1)

            def x_rest(count, buf):
                dve.wait_ge(sem("xe_hi"), count)
                dve.tensor_tensor(XEP[buf][1], x_banks, XEP[buf][0], ALU.subtract).then_inc(sem("xe_lo"), 1)

            for v in range(PARTS):
                m_cut(0, v)
            x_rest(1, 0)
            dve.nop().then_inc(sem("h_done"), 1)
            with dve.Fori(0, N_EXP // 4) as i:
                for s in range(4):
                    e = i * 4 + (s + 1)
                    for v in range(6 * s + 3, 6 * s + 5):
                        m_cut(i, v)
                    dve.wait_ge(sem("m_used"), i * 24 + (USED0 + 6 * s + 4))
                    dve.wait_ge(sem("silu_done"), e)
                    dve.tensor_tensor(HB, SG, up_bank, ALU.mult).then_inc(sem("h_done"), 1)
                    dve.wait_ge(sem("ht_hi"), e)
                    dve.tensor_tensor(HTP[1][:, 0, :], h_bank, HTP[0][:, 0, :], ALU.subtract).then_inc(sem("ht_lo"), 1)
                    m_cut(i, 6 * s + 5)
                    x_rest(i * 4 + (s + 2), (s + 1) % 2)
                    for v in range(6 * s + 6, 6 * s + 9):
                        m_cut(i, v)
            dve.wait_ge(sem("over_ready"), 1)
            n_over = dve.value_load(over_i[0:1, 7:8], min_val=0, max_val=MAX_OVER)
            with dve.If(n_over > 0):
                with dve.Fori(0, MAX_OVER) as b:
                    dve.wait_ge(sem("o_sg"), b + 1)
                    dve.tensor_tensor(HB, SG, up_bank, ALU.mult).then_inc(sem("o_h"), 1)
                    dve.wait_ge(sem("o_ht"), b + 1)
                    dve.tensor_copy(HO, h_bank).then_inc(sem("o_hte"), 1)
                    dve.wait_ge(sem("o_stored"), (b + 1) * 16)
            ahead.limit = len(PLAN)
            ahead(N_FIRST + 1)
            w1, w2 = W1.rearrange("p m a -> p (m a)"), W2.rearrange("p m a -> p (m a)")
            for m in range(4):
                y1, y2 = YG[2 * (m % 2)], YG[2 * (m % 2) + 1]
                dve.wait_ge(sem(f"y_in{m % 2}"), 32 * (m // 2 + 1))
                if m >= 1:
                    ready(dve, ("comb", m - 1, 1))
                step(dve.tensor_scalar(YS[0], y1, w1[:, m:m + 1], None, ALU.mult))
                dve.scalar_tensor_tensor(YS[0], y2, w2[:, m:m + 1], YS[0], ALU.mult, ALU.add)\
                   .then_inc(sem("combined"), 1)
                dve.wait_ge(sem("combined"), m + 1)
                for h in range(2):
                    n_ = ("comb", m, h)
                    ready(dve, n_)
                    v = SG.rearrange("p (k t) -> p k t", k=4)
                    take(n_, dve.tensor_tensor(v, bank(n_).rearrange("p (k t) -> p k t", k=4),
                                               bc(mod[:, 40 + 4 * h:44 + 4 * h], [P, 4, P], 2), ALU.mult))
                    xs = X[:, 4 * h:4 * h + 4, P * m:P * m + P]
                    step(dve.tensor_tensor(xs, xs, v, ALU.add))
                    dve.nop().then_inc(sem("x_moe"), 1)
            ready(dve, ("ss", 3))
            take(("ss", 3), dve.tensor_scalar(small[:, :], bank(("ss", 3)), 1.0 / D, 1e-6, ALU.mult, ALU.add))
            inv_sqrt(dve.nop(), small[:, :])
            for k in range(KT + 1):
                if k < KT:
                    dve.scalar_tensor_tensor(X[:, k, :], X[:, k, :], pc("final_g", k), small[:, :],
                                             ALU.mult, ALU.mult).then_inc(sem("x_final"), 1)
                if k >= 1:
                    x_lo("x0", k - 1, X0_P, X[:, k - 1, :])
            if stop == 2:
                dve.wait_ge(sem("x_final"), KT)
                dve.nop().then_inc(sem("result"), 1)

        def moe_tensor(pe, aux, filled, dense, colsum, product):
            colsum(("ss", 2), lambda k: YC[:, k, :], KT, ready_at=("sq2", lambda k: k + 1))
            pe.wait_ge(sem("h2"), KT)
            out = aux(("lg",))
            rw = pc("router_w").rearrange("p (k e) -> p k e", k=KT)
            for m in range(4):
                for k in range(KT):
                    mm = pe.matmul(out[:, 36 * m:36 * m + 36], H[:, k, P * m:P * m + P], rw[:, k, :],
                                   start=(k == 0), stop=(k == KT - 1))
            filled(mm)
            for m in range(4):
                for h in range(2):
                    out = aux(("ht", m, h))
                    for k in range(4):
                        mm = pe.transpose(out[:, P * k:P * k + P], H[:, 4 * h + k, P * m:P * m + P], ident)
                    filled(mm)
            out = aux(("rank",))
            pe.wait_ge(sem("onehots"), 1)
            for m in range(4):
                for m2 in range(m + 1):
                    mm = pe.matmul(out[:, 32 * m:32 * m + 32], strict_u if m2 == m else ones, OHS[:, m2, :],
                                   start=(m2 == 0), stop=(m2 == m))
            for m in range(4):
                mm = pe.matmul(out[:, 128:160], ones, OHS[:, m, :], start=(m == 0), stop=(m == 3))
            filled(mm)
            out = aux(("idx",))
            pe.wait_ge(sem("table_in"), 16)
            filled(pe.transpose(out[:, 0:BLOCKS], TSB[0:BLOCKS, :], ident[0:BLOCKS, 0:BLOCKS]))

            def x_rows(count, buf, signal):
                for k in range(KT):
                    mm = pe.transpose(x_banks[:, k // 4, P * (k % 4):P * (k % 4) + P],
                                      XG[buf][:, P * k:P * k + P], ident)
                mm.then_inc(sem(signal), 1)

            def gate_up(bank_, xe, tiles):
                for i, t in enumerate(tiles):
                    w = t.rearrange("p (k n) -> p k n", k=4)
                    for k in range(4):
                        kk_ = 4 * i + k
                        mm = pe.matmul(bank_, xe[:, P * kk_:P * kk_ + P], w[:, k, :], start=(kk_ == 0), stop=(kk_ == 7))
                    yield mm

            def down(tiles):
                for i, t in enumerate(tiles):
                    w = t.rearrange("p (k n) -> p k n", k=2)
                    for h in range(2):
                        for k in range(2):
                            kk_ = 2 * i + k
                            mm = pe.matmul(y_banks[:, h, :], HO[:, P * kk_:P * kk_ + P],
                                           w[:, k, 512 * h:512 * h + 512], start=(kk_ == 0), stop=(kk_ == 3))
                    yield mm

            def h_rows(signal):
                for k in range(4):
                    mm = pe.transpose(h_bank[:, P * k:P * k + P], HB[:, P * k:P * k + P], ident)
                mm.then_inc(sem(signal), 1)

            for n in range(4):
                pe.wait_ge(sem(f"aux_free{n}"), (AUX_NO[("idx",)] - n) // 4 + 1)
            for n in range(2):
                pe.wait_ge(sem(f"pair_free{n}"), sum(1 for g in GROUPS[:GROUP_NO[("w_out", 3)] + 1]
                                                     if GROUP_NO[g] % 2 == n))
            pe.wait_ge(sem("xg_in0"), 16)
            x_rows(1, 0, "xt_ready")
            with pe.Fori(0, N_EXP // 4) as i:
                for s in range(4):
                    def unit_in(j):
                        pe.wait_ge(sem("m_lo"), i * 24 + (CUT0 + 6 * s + j + 1))
                        return [t.rearrange("p (k n) -> p k n", k=4 if j < 4 else 2) for t in expert_parts(j)]

                    def tile_x(kk_):
                        return [v[:, kk_ // 4, P * (kk_ % 4):P * (kk_ % 4) + P] for v in XEP[s % 2]]
                    pe.wait_ge(sem("xe_lo"), i * 4 + (s + 1))
                    for j in range(4):
                        if j == 2:
                            pe.wait_ge(sem("h_done"), i * 4 + (s + 1))
                        w = unit_in(j)
                        for k in range(4):
                            kk_ = 4 * (j % 2) + k
                            mm = product(gate_bank if j < 2 else up_bank, tile_x(kk_), [v[:, k, :] for v in w],
                                         kk_ == 0, kk_ == 7)
                        mm.then_inc(sem("m_used"), 1)
                    pe.wait_ge(sem(f"xg_in{(s + 1) % 2}"), (i * 2 + ((s + 1) // 2 + 1)) * 16)
                    x_rows(None, (s + 1) % 2, "xt_ready")
                    pe.wait_ge(sem("h_done"), i * 4 + (s + 2))
                    h_rows("ht_ready")
                    pe.wait_ge(sem("ht_lo"), i * 4 + (s + 1))
                    pe.wait_ge(sem("y_copied"), i * 4 + (s + 1))
                    for h in range(2):
                        w = unit_in(4 + h)
                        for n in range(2):
                            for k in range(2):
                                kk_ = 2 * h + k
                                mm = product(y_banks[:, n, :], [v[:, 0, P * kk_:P * kk_ + P] for v in HTP],
                                             [v[:, k, 512 * n:512 * n + 512] for v in w], kk_ == 0, kk_ == 3)
                        mm.then_inc(sem("m_used"), 1)
            pe.wait_ge(sem("y_copied"), N_EXP + 1)
            pe.wait_ge(sem("xe_lo"), N_EXP + 1)
            pe.wait_ge(sem("over_ready"), 1)
            n_over = pe.value_load(over_i[0:1, 7:8], min_val=0, max_val=MAX_OVER)
            with pe.If(n_over > 0):
                with pe.Fori(0, MAX_OVER) as b:
                    pe.wait_ge(sem("o_x"), (b + 1) * 16)
                    x_rows(None, 0, "o_xt")
                    pe.wait_ge(sem("o_xe"), b + 1)
                    pe.wait_ge(sem("o_weights"), (b + 1) * 96)
                    for mm in gate_up(gate_bank, XO, [slot_tile(0), slot_tile(1)]):
                        pass
                    for mm in gate_up(up_bank, XO, [slot_tile(2), slot_tile(3)]):
                        pass
                    mm.then_inc(sem("o_gu"), 1)
                    pe.wait_ge(sem("o_h"), b + 1)
                    h_rows("o_ht")
                    pe.wait_ge(sem("o_hte"), b + 1)
                    for mm in down([slot_tile(4), slot_tile(5)]):
                        pass
                    mm.then_inc(sem("o_y"), 1)
                    pe.wait_ge(sem("o_stored"), (b + 1) * 16)
            for m in range(4):
                pe.wait_ge(sem("combined"), m + 1)
                for h in range(2):
                    out = aux(("comb", m, h))
                    for k in range(4):
                        kk_ = 4 * h + k
                        mm = pe.transpose(out[:, P * k:P * k + P], YS[0][:, P * kk_:P * kk_ + P], ident)
                    filled(mm)
            colsum(("ss", 3), lambda k: H[:, k, :], KT, ready_at=("sq3", lambda k: 1 + k // 4))

        YS2, BC = area(4096, 16), area(12288, 4)
        XDT = flat(14336, 4096).rearrange("p (c n) -> p c n", c=4)
        HIN = [flat(18432 + 1024 * c, 1024) for c in range(3)]
        DT = [flat(21504 + 512 * i, 512) for i in range(8)]
        SELH = flat(21504, 2048).rearrange("p (h t) -> p h t", h=16)
        GB = [flat(25600 + 512 * i, 512) for i in range(4)]
        CE = [flat(27648 + 512 * i, 512) for i in range(4)]
        CBM = [flat(29696 + 512 * g, 512) for g in range(2)]
        BTOK = flat(30720, 1024).rearrange("p (c g n) -> p c g n", c=4, g=2)
        XDE = flat(31744, 1024)
        ACST, DTT, DEC, DEE = (flat(32768 + 64 * i, 64) for i in range(4))
        acst, dtt, dee = (t.rearrange("p (c h) -> p c h", c=4) for t in (ACST, DTT, DEE))
        dec = DEC.rearrange("p (h c) -> p h c", h=16)
        ZT = [GB[0], GB[1], GB[2], GB[3]]
        SQ = flat(14336, 4096)
        SQK = area(14336, 8)
        Z_P = parts(18432, 27648, 8)
        YS_HI = [area_r(lo, 8)[:, k, :] for lo in (18432, 27648) for k in range(8)]
        YS_LO = area_r(4096, 16)
        X_P = parts(4096, 8192, 8)
        HID_P = parts(12288, 18432, HS)
        SGT = [flat(24576 + 512 * i, 512) for i in range(2)]
        TH = [flat(25600 + 512 * i, 512) for i in range(2)]
        SQ2K = area(26624, 8)
        PT = area(30720, 2)
        SIG, PT_P = area(12288, 8), parts(18432, 19456, 2)
        Q = area(12288, 8)
        KZ = [flat(16384 + 1024 * m, 1024).rearrange("p (o t) -> p o t", o=2) for m in range(2)]
        VA = flat(18432, 1024).rearrange("p (n v) -> p n v", n=4)
        OA = area(19456, 8)
        BAND = flat(23552, 256)
        CONST_R = area_r(28416, 1)[:, 0, :]
        PB = [flat(23808 + 512 * i, 512) for i in range(4)]
        PTB = [flat(25856 + 512 * i, 512) for i in range(2)]
        ATS = flat(26880, 64 * 8)
        TO = [flat(27392 + 512 * i, 512) for i in range(2)]

        def att(i):
            n, j = i // 8, i % 8
            return n, j, P if n == 0 else 2 * P

        def second_sync(sp_):
            pass

        def second_pool(pool, step):
            pool.wait_ge(sem("ple_done0"), 1)
            step(pool.memset(BAND, 0.0))
            step(pool.affine_select(out=BAND[:, 0:P], in_=BAND[:, 0:P], compare_op=ALU.is_gt, fill=NEG, base=0,
                                    pattern=[[1, P]], channel_multiplier=-1))
            step(pool.affine_select(out=BAND[:, P:2 * P], in_=BAND[:, P:2 * P], compare_op=ALU.is_ge, fill=NEG,
                                    base=0, pattern=[[-1, P]], channel_multiplier=1))
            for m in range(2):
                step(pool.memset(KZ[m][HD:P, 0, :], 0.0))
                step(pool.memset(KZ[m][0:HD, 1, :], 0.0))
            pool.nop().then_inc(sem("att_consts"), 1)

        def second_act(act, step, root, ahead, x_hi):
            for j in range(8):
                g = ("sc_ch", j)
                ahead.enter(g)
                group_ready(act, g)
                if j >= 2:
                    act.wait_ge(sem("sc_prod"), j - 1)
                act.activation(GB[j % 2], dbank(g)[:, 0, :], ACT.Copy).then_inc(sem("sc_c"), 1)
                ahead.leave(g)
            for q in range(12):
                g, b = ("xbc", q // 2), q % 2
                if b == 0:
                    ahead.enter(g)
                    group_ready(act, g)
                dst = YS2[:, q, :] if q < 8 else BC[:, q - 8, :]
                act.activation(dst, dbank(g)[:, b, :], ACT.Identity, scale=pc("conv_w", 36 + q),
                               bias=pc("conv_b", q)).then_inc(sem("conv_a"), 1)
                act.wait_ge(sem("conv_b"), q + 1)
                act.activation(dst, dst, ACT.Silu).then_inc(sem("xbc_done"), 1)
                if b == 1:
                    ahead.leave(g)
            ahead.leave(("dt",))
            act.wait_ge(sem("dt_abs"), 1)
            act.activation(DT[2][0:16], DT[1][0:16], ACT.Exp, scale=-1.0).then_inc(sem("dt_exp"), 1)
            act.activation(gain[0:16, 56:57], pc("a_log")[0:16], ACT.Exp).then_inc(sem("a_exp"), 1)
            for c in range(4):
                n_ = ("bct", c)
                ready(act, n_)
                act.activation(BTOK[:, c].rearrange("p g n -> p (g n)"), bank(n_)[:, 0:256], ACT.Copy)\
                   .then_inc(freed(n_), 1)
            act.wait_ge(sem("last_in"), 1)
            act.activation(DEE, DEE, ACT.Exp).then_inc(sem("last_exp"), 1)
            act.activation(DEC, DEC, ACT.Exp).then_inc(sem("last_exp"), 1)
            for h in range(16):
                n_ = ("acs", h)
                ready(act, n_)
                if h >= 4:
                    ready(act, ("yd", h // 2 - 2))
                act.wait_ge(sem("seg_min"), h + 1)
                act.activation(CE[h % 4], bank(n_), ACT.Exp).then_inc(freed(n_), 1)
                act.wait_ge(sem("seg"), h + 1)
                act.activation(GB[h % 4], GB[h % 4], ACT.Exp).then_inc(sem("seg_exp"), 1)
            ready(act, ("yd", 7))
            for k in range(KT):
                x_hi(Z_P[0][:, k, :], X[:, k, :])
            for j in range(8):
                g = ("z", j // 2)
                if j % 2 == 0:
                    ahead.enter(g)
                    group_ready(act, g)
                if j >= 4:
                    act.wait_ge(sem("z_mul"), j - 3)
                act.activation(ZT[j % 4], dbank(g)[:, j % 2, :], ACT.Silu).then_inc(sem("z_silu"), 1)
                if j % 2 == 1:
                    ahead.leave(g)
            for j in range(8):
                act.wait_ge(sem("z_mul"), j + 1)
                act.activation(SQK[:, j, :], YS2[:, j, :], ACT.Square).then_inc(sem("y_sq"), 1)
            for j in range(8, 16):
                x_hi(YS_HI[j], YS2[:, j, :])
            for g in range(2):
                root(small[:, :])
                for j in range(4 * g, 4 * g + 4):
                    act.wait_ge(sem("y_norm"), j + 1)
                    x_hi(YS_HI[j], YS2[:, j, :])
            ahead.leave(("mix_out", 3))

            def layer_norm(n):
                for k in range(KT):
                    act.wait_ge(sem("ln_c"), KT * n + k + 1)
                    act.activation(SQ2K[:, k, :], X[:, k, :], ACT.Square).then_inc(sem("ln_sq"), 1)
                root(small[:, :])
                which, layer = ("mix", "ffn")[n % 2], n // 2
                bias = [pc(f"ln_{which}_b", 8 * layer + k) for k in range(KT)]
                for k in range(KT):
                    act.wait_ge(sem("ln_s"), KT * n + k + 1)
                    x_hi(X_P[0][:, k, :], X[:, k, :], bias=bias[k])
                for k in range(KT):
                    part_ready(act, (("gu", "ple")[n % 2], layer), k)
                    act.activation(X[:, k, :], X[:, k, :], ACT.Identity, bias=bias[k]).then_inc(sem("ln_x"), 1)

            for layer in range(2):
                if layer == 1:
                    act.wait_ge(sem("att_consts"), 1)
                    act.activation(CONST_R[:, 0:2 * P], BAND, ACT.Copy).then_inc(sem("att_consts"), 1)
                    act.activation(CONST_R[:, 2 * P:3 * P], ident, ACT.Copy).then_inc(sem("att_consts"), 1)
                    ahead.leave(("vv",))
                    for i in range(N_ATT + 4):
                        if i < N_ATT:
                            n, j, w = att(i)
                            pb = PB[i % 4][:, 0:2 * w].rearrange("p (o s) -> p o s", o=2)
                            st = ATS[:, 16 * (i % 4):16 * (i % 4) + 16]
                            n_ = ("sc", i)
                            sc = bank(n_)[:, 0:2 * w].rearrange("p (o s) -> p o s", o=2)
                            act.wait_ge(sem("att_max"), i + 1)
                            if i >= 4:
                                ready(act, ("pt", i - 4))
                            for o_ in range(2):
                                act.activation(pb[:, o_, :], sc[:, o_, :], ACT.Exp, bias=st[:, 2 + o_:3 + o_],
                                               accum_out=st[:, 4 + o_:5 + o_])\
                                   .then_inc(sem("att_exp") if o_ == 0 else freed(n_), 1)
                            act.activation(st[:, 6:8], st[:, 6:8], ACT.Exp).then_inc(sem("att_exp"), 1)
                        if 2 <= i < N_ATT + 2:
                            k = i - 2
                            _, _, w = att(k)
                            n_ = ("pt", k)
                            ready(act, n_)
                            if k >= 2:
                                ready(act, ("pv", k - 2))
                            act.activation(PTB[k % 2][:, 0:2 * w], bank(n_)[:, 0:2 * w], ACT.Copy)\
                               .then_inc(freed(n_), 1)
                        if 3 <= i < N_ATT + 3:
                            k = i - 3
                            n, j, _ = att(k)
                            n_ = ("pv", k)
                            ready(act, n_)
                            act.activation(OA[:, j, P * n:P * n + P], bank(n_)[:, 0:P], ACT.Copy)\
                               .then_inc(freed(n_), 1)
                    n_ = ("pv", N_ATT - 1)
                    act.wait_ge(freed(n_), AUX_NO[n_] // 4 + 1)
                    for k in range(KT):
                        x_hi(X_P[0][:, k, :], OA[:, k, :])
                    for j in range(8):
                        g = ("wo", j // 2)
                        if j % 2 == 0:
                            ahead.enter(g)
                            group_ready(act, g)
                        if j >= 2:
                            act.wait_ge(sem("x_res1"), j - 1)
                        act.activation(TO[j % 2], dbank(g)[:, j % 2, :], ACT.Identity, bias=pc("b_o", j))\
                           .then_inc(sem("wo_bias"), 1)
                        if j % 2 == 1:
                            ahead.leave(g)
                layer_norm(2 * layer)
                act.wait_ge(sem("ln_x"), KT * (2 * layer + 1))
                act.dma_start(PT, p_t[layer]).then_inc(sem("p_in"), 16)
                for j in range(FT):
                    g = ("gu", layer, j)
                    ahead.enter(g)
                    group_ready(act, g)
                    if j >= 2:
                        act.wait_ge(sem(f"hidden{layer}"), j - 1)
                    act.activation(SGT[j % 2], dbank(g)[:, 0, :], ACT.Silu).then_inc(sem("ffn_silu"), 1)
                    act.wait_ge(sem(f"hidden{layer}"), j + 1)
                    x_hi(HID_P[0][:, j % HS, :], TH[j % 2])
                    ahead.leave(g)
                ahead.leave(("down", layer, 1, 3))
                layer_norm(2 * layer + 1)
                act.wait_ge(sem("p_in"), 16 * (layer + 1))
                for k in range(2):
                    x_hi(PT_P[0][:, k, :], PT[:, k, :])
                for j in range(8):
                    g = ("ple_g", layer, j // 2)
                    if j % 2 == 0:
                        ahead.enter(g)
                        group_ready(act, g)
                    ins = act.activation(SIG[:, j, :], dbank(g)[:, j % 2, :], ACT.Sigmoid,
                                         bias=pc("b_ple", 8 * layer + j))
                    if j % 2 == 1:
                        ins.then_inc(group_freed(g), 1)
                    else:
                        ins.then_inc(sem("sig_half"), 1)
                    if j % 2 == 1:
                        ahead.leave(g)
                for j in range(8):
                    g = ("ple_w", layer, j // 2)
                    if j % 2 == 0:
                        ahead.enter(g)
                    if layer == 0:
                        act.wait_ge(sem("x_mid"), j + 1)
                        x_hi(X_P[0][:, j, :], X[:, j, :])
                    if j % 2 == 1:
                        ahead.leave(g)

        def second_vector(dve, step, take, inv_sqrt, ahead, x_lo):
            def done_with(g):
                dve.nop().then_inc(group_freed(g), 1)

            for j in range(8):
                g = ("sc_ch", j)
                ahead.enter(g)
                group_ready(dve, g)
                dve.wait_ge(sem("sc_c"), j + 1)
                pr = GB[2 + j % 2]
                dve.tensor_tensor(pr, GB[j % 2], dbank(g)[:, 1, :], ALU.mult).then_inc(sem("sc_prod"), 1)
                dve.wait_ge(sem("sc_prod"), j + 1)
                done_with(g)
                y = YS2[:, 8 + j, :]
                step(dve.tensor_scalar(y, pr, pc("sc_w", 16 + j), None, ALU.mult))
                for t in (1, 2):
                    step(dve.scalar_tensor_tensor(y[:, t:SEQ], pr[:, 0:SEQ - t], pc("sc_w", 8 * (2 - t) + j),
                                                  y[:, t:SEQ], ALU.mult, ALU.add))
                ahead.leave(g)
            for j in range(8):
                g = ("sc_b", j // 2)
                if j % 2 == 0:
                    ahead.enter(g)
                    group_ready(dve, g)
                step(dve.tensor_tensor(YS2[:, 8 + j, :], YS2[:, 8 + j, :], dbank(g)[:, j % 2, :], ALU.mult))
                if j % 2 == 1:
                    done_with(g)
                    ahead.leave(g)
            for q in range(12):
                g, b = ("xbc", q // 2), q % 2
                dst = YS2[:, q, :] if q < 8 else BC[:, q - 8, :]
                if b == 0:
                    ahead.enter(g)
                dve.wait_ge(sem("conv_a"), q + 1)
                for t in (1, 2, 3):
                    step(dve.scalar_tensor_tensor(dst[:, t:SEQ], dbank(g)[:, b, 0:SEQ - t],
                                                  pc("conv_w", 12 * (3 - t) + q), dst[:, t:SEQ], ALU.mult, ALU.add))
                dve.nop().then_inc(sem("conv_b"), 1)
                if b == 1:
                    done_with(g)
                    ahead.leave(g)
            g = ("dt",)
            ahead.enter(g)
            group_ready(dve, g)
            x, ab, u, s_, s2, q_ = (DT[i][0:16] for i in range(6))
            step(dve.tensor_scalar(x, dbank(g)[0:16, 0, :], pc("dt_b")[0:16], None, ALU.add))
            done_with(g)
            ahead.leave(g)
            dve.scalar_tensor_tensor(ab, x, -1.0, x, ALU.mult, ALU.max).then_inc(sem("dt_abs"), 1)
            dve.wait_ge(sem("dt_exp"), 1)
            step(dve.tensor_scalar(s_, u, 2.0, None, ALU.add))
            step(dve.reciprocal(s_, s_))
            step(dve.tensor_tensor(s_, s_, u, ALU.mult))
            step(dve.tensor_tensor(s2, s_, s_, ALU.mult))
            step(dve.tensor_scalar(q_, s2, 1.0 / 15, None, ALU.mult))
            for n in (13, 11, 9, 7, 5, 3):
                step(dve.scalar_tensor_tensor(q_, q_, 1.0 / n, s2, ALU.add, ALU.mult))
            step(dve.scalar_tensor_tensor(q_, q_, 1.0, s_, ALU.add, ALU.mult))
            step(dve.tensor_scalar(x, x, 0.0, None, ALU.max))
            step(dve.scalar_tensor_tensor(q_, q_, 2.0, x, ALU.mult, ALU.add))
            dve.wait_ge(sem("a_exp"), 1)
            da, acs = DT[6][0:16], DT[7][0:16]
            step(dve.tensor_scalar(da, q_, gain[0:16, 56:57], -1.0, ALU.mult, ALU.mult))
            step(dve.tensor_tensor_scan(acs, reset[0:16, :], da, 0.0, ALU.mult, ALU.add))
            step(dve.tensor_copy(SELH[0:16], ident[0:16, 0:16].unsqueeze(2).to_broadcast([16, 16, P])))
            last = acs.rearrange("h (c t) -> h c t", c=4)[:, :, P - 1]
            dl = DT[6][0:16, 0:64].rearrange("p (h c) -> p h c", h=16)
            step(dve.tensor_tensor(dl, ident[0:16, 0:16].unsqueeze(2).to_broadcast([16, 16, 4]),
                                   last.unsqueeze(1).to_broadcast([16, 16, 4]), ALU.mult))
            dve.nop().then_inc(sem("acs_ready"), 1)
            n_ = ("da_t",)
            ready(dve, n_)
            step(dve.tensor_copy(ACST, bank(n_)[:, 0:64]))
            take(n_, dve.tensor_copy(DTT, bank(n_)[:, 64:128]))
            n_ = ("last",)
            ready(dve, n_)
            step(dve.tensor_copy(DEC, bank(n_)[:, 0:64]))
            take(n_, dve.tensor_tensor(dee, bank(n_)[:, 0:64].rearrange("p (h c) -> p c h", h=16), acst, ALU.subtract))
            dve.nop().then_inc(sem("last_in"), 1)
            for c in range(4):
                for h in range(2):
                    n_ = ("xst", c, h)
                    ready(dve, n_)
                    take(n_, dve.tensor_tensor(
                        XDT[:, c, 512 * h:512 * h + 512].rearrange("p (h v) -> p h v", h=8),
                        bank(n_).rearrange("p (h v) -> p h v", h=8),
                        dtt[:, c, 8 * h:8 * h + 8].unsqueeze(2).to_broadcast([P, 8, HD]), ALU.mult))
            dve.nop().then_inc(sem("xdt"), 1)
            for g in range(2):
                n_ = ("cb", g)
                ready(dve, n_)
                take(n_, dve.tensor_tensor(CBM[g].rearrange("p (c t) -> p c t", c=4),
                                           bank(n_).rearrange("p (c t) -> p c t", c=4),
                                           pair[:, 1, :].unsqueeze(1).to_broadcast([P, 4, P]), ALU.mult))
            dve.wait_ge(sem("last_exp"), 2)
            for c in range(3):
                if c > 0:
                    ready(dve, ("stt", c - 1, 1))
                step(dve.tensor_tensor(XDE.rearrange("p (h v) -> p h v", h=16),
                                       XDT[:, c, :].rearrange("p (h v) -> p h v", h=16),
                                       dee[:, c, :].unsqueeze(2).to_broadcast([P, 16, HD]), ALU.mult))
                dve.nop().then_inc(sem("xde"), 1)
                for g in range(2):
                    n_ = ("stt", c, g)
                    hs_ = slice(512 * g, 512 * g + 512)
                    if c > 0:
                        step(dve.tensor_tensor(HIN[c][:, hs_].rearrange("p (h v) -> p h v", h=8),
                                               HIN[c - 1][:, hs_].rearrange("p (h v) -> p h v", h=8),
                                               dec[:, 8 * g:8 * g + 8, c:c + 1].to_broadcast([P, 8, HD]), ALU.mult))
                        ready(dve, n_)
                        take(n_, dve.tensor_tensor(HIN[c][:, hs_], HIN[c][:, hs_], bank(n_), ALU.add))
                    else:
                        ready(dve, n_)
                        take(n_, dve.tensor_copy(HIN[c][:, hs_], bank(n_)))
            dve.nop().then_inc(sem("hin"), 1)

            def head_out(j):
                n_ = ("yd", j)
                ready(dve, n_)
                take(n_, dve.scalar_tensor_tensor(YS2[:, j, :], YS2[:, j, :], pc("d_skip", j), bank(n_),
                                                  ALU.mult, ALU.add))

            for h in range(16):
                n_ = ("acs", h)
                ready(dve, n_)
                if h >= 4:
                    ready(dve, ("yd", h // 2 - 2))
                gb = GB[h % 4].rearrange("p (c t) -> p c t", c=4)
                sb_ = acst[:, :, h:h + 1].to_broadcast([P, 4, P])
                dve.tensor_tensor(gb, bank(n_).rearrange("p (c t) -> p c t", c=4), sb_, ALU.min)\
                   .then_inc(sem("seg_min"), 1)
                dve.wait_ge(sem("seg_min"), h + 1)
                dve.tensor_tensor(gb, gb, sb_, ALU.subtract).then_inc(sem("seg"), 1)
                dve.wait_ge(freed(n_), AUX_NO[n_] // 4 + 1)
                dve.tensor_tensor(CE[h % 4], CE[h % 4], BC[:, 2 + h // 8, :], ALU.mult).then_inc(sem("head_ce"), 1)
                dve.wait_ge(sem("seg_exp"), h + 1)
                dve.tensor_tensor(GB[h % 4], GB[h % 4], CBM[h // 8], ALU.mult).then_inc(sem("head_g"), 1)
                if h % 2 == 1 and h >= 3:
                    head_out(h // 2 - 1)
            head_out(7)
            for k in range(KT):
                x_lo("z", k, Z_P, X[:, k, :])
            for j in range(8):
                g = ("z", j // 2)
                if j % 2 == 0:
                    ahead.enter(g)
                dve.wait_ge(sem("z_silu"), j + 1)
                if j % 2 == 1:
                    done_with(g)
                dve.tensor_tensor(YS2[:, j, :], YS2[:, j, :], ZT[j % 4], ALU.mult).then_inc(sem("z_mul"), 1)
                if j % 2 == 1:
                    ahead.leave(g)

            def ys_lo(j):
                part_hi_ready(dve, "ys", j)
                dve.tensor_tensor(YS_LO[:, j, :], YS2[:, j, :], YS_HI[j], ALU.subtract)\
                   .then_inc(sem("x_lo"), 1)

            for j in range(8, 16):
                ys_lo(j)
            for g in range(2):
                n_ = ("gss", g)
                ready(dve, n_)
                take(n_, dve.tensor_scalar(small[:, :], bank(n_), 1.0 / 512, 1e-5, ALU.mult, ALU.add))
                inv_sqrt(dve.nop(), small[:, :])
                for j in range(4 * g, 4 * g + 4):
                    dve.scalar_tensor_tensor(YS2[:, j, :], YS2[:, j, :], pc("ssd_nw", j), small[:, :],
                                             ALU.mult, ALU.mult).then_inc(sem("y_norm"), 1)
                for j in range(4 * g, 4 * g + 4):
                    ys_lo(j)

            def layer_norm(n):
                which, layer = ("mix", "ffn")[n % 2], n // 2
                m_, v_ = ("lnm", which, layer), ("lnv", which, layer)
                ready(dve, m_)
                for k in range(KT):
                    dve.scalar_tensor_tensor(X[:, k, :], bank(m_), -1.0 / D, X[:, k, :], ALU.mult, ALU.add)\
                       .then_inc(sem("ln_c"), 1)
                dve.wait_ge(sem("ln_c"), KT * (n + 1))
                dve.nop().then_inc(freed(m_), 1)
                ready(dve, v_)
                take(v_, dve.tensor_scalar(small[:, :], bank(v_), 1.0 / D, 1e-5, ALU.mult, ALU.add))
                inv_sqrt(dve.nop(), small[:, :])
                for k in range(KT + 1):
                    if k < KT:
                        dve.scalar_tensor_tensor(X[:, k, :], X[:, k, :], pc(f"ln_{which}_g", 8 * layer + k),
                                                 small[:, :], ALU.mult, ALU.mult).then_inc(sem("ln_s"), 1)
                    if k >= 1:
                        part_hi_ready(dve, (("gu", "ple")[n % 2], layer), k - 1)
                        dve.scalar_tensor_tensor(X_P[1][:, k - 1, :], X[:, k - 1, :],
                                                 pc(f"ln_{which}_b", 8 * layer + k - 1), X_P[0][:, k - 1, :],
                                                 ALU.add, ALU.subtract).then_inc(sem("x_lo"), 1)

            counts = {"x_res": 0, "x_half": 0}

            def residual(groups, scale, signal, src=None):
                for j in range(8):
                    g = groups[j // 2]
                    if j % 2 == 0:
                        ahead.enter(g)
                        group_ready(dve, g)
                    if src is not None:
                        dve.wait_ge(sem("wo_bias"), j + 1)
                    dve.scalar_tensor_tensor(X[:, j, :], X[:, j, :], scale,
                                             dbank(g)[:, j % 2, :] if src is None else src[j % 2],
                                             ALU.mult, ALU.add).then_inc(sem(signal), 1)
                    counts[signal] += 1
                    dve.wait_ge(sem(signal), counts[signal])
                    if src is not None:
                        dve.nop().then_inc(sem("x_res1"), 1)
                    if j % 2 == 1:
                        done_with(g)
                        ahead.leave(g)

            for layer in range(2):
                if layer == 0:
                    residual([("mix_out", j) for j in range(4)], ALPHA, "x_res")
                else:
                    attention(dve, step, take, done_with, ahead)
                    for k in range(KT):
                        x_lo("oa", k, X_P, OA[:, k, :])
                    residual([("wo", j) for j in range(4)], ALPHA, "x_res", TO)
                layer_norm(2 * layer)
                for half in range(2):
                    for j in GATE_TILES[half]:
                        g = ("gu", layer, j)
                        ahead.enter(g)
                        group_ready(dve, g)
                        dve.wait_ge(sem("ffn_silu"), FT * layer + j + 1)
                        dve.tensor_tensor(TH[j % 2], SGT[j % 2], dbank(g)[:, 1, :], ALU.mult)\
                           .then_inc(sem(f"hidden{layer}"), 1)
                        dve.wait_ge(sem(f"hidden{layer}"), j + 1)
                        done_with(g)
                        part_hi_ready(dve, ("hid", layer), j)
                        dve.tensor_tensor(HID_P[1][:, j % HS, :], TH[j % 2], HID_P[0][:, j % HS, :],
                                          ALU.subtract).then_inc(sem("x_lo"), 1)
                        ahead.leave(g)
                    dve.wait_ge(sem("ln_x"), KT * (2 * layer + 1))
                    residual([("down", layer, half, j) for j in range(4)], (ALPHA, 1.0)[half],
                             ("x_half", "x_res")[half])
                layer_norm(2 * layer + 1)
                for k in range(2):
                    x_lo(("pt", layer), k, PT_P, PT[:, k, :])
                for j in range(4):
                    ahead.leave(("ple_g", layer, j))
                for j in range(8):
                    g = ("ple_w", layer, j // 2)
                    if j % 2 == 0:
                        ahead.enter(g)
                        group_ready(dve, g)
                    if j == 0:
                        gg = ("ple_g", layer, 3)
                        dve.wait_ge(group_freed(gg), GROUP_NO[gg] // 2 + 1)
                        dve.wait_ge(group_freed(("ple_g", layer, 2)), GROUP_NO[("ple_g", layer, 2)] // 2 + 1)
                        dve.wait_ge(sem("ln_x"), KT * (2 * layer + 2))
                    step(dve.tensor_tensor(SIG[:, j, :], SIG[:, j, :], dbank(g)[:, j % 2, :], ALU.mult))
                    step(dve.tensor_tensor(X[:, j, :], X[:, j, :], SIG[:, j, :], ALU.add))
                    if layer == 0:
                        dve.nop().then_inc(sem("x_mid"), 1)
                    if j % 2 == 1:
                        done_with(g)
                        if layer == 0:
                            for k in (j - 1, j):
                                x_lo("q", k, X_P, X[:, k, :])
                        ahead.leave(g)
                if layer == 0:
                    dve.nop().then_inc(sem("ple_done0"), 1)
            dve.nop().then_inc(sem("result"), 1)

        def attention(dve, step, take, done_with, ahead):
            dve.wait_ge(sem("att_consts"), 1)
            for j in range(8):
                g = ("q", j // 2)
                if j % 2 == 0:
                    ahead.enter(g)
                    group_ready(dve, g)
                step(dve.tensor_scalar(Q[:, j, :], dbank(g)[:, j % 2, :], pc("b_q", j), HD ** -0.5, ALU.add, ALU.mult))
                if j % 2 == 1:
                    done_with(g)
                    ahead.leave(g)
            g = ("kk",)
            group_ready(dve, g)
            for m in range(2):
                for o_ in range(2):
                    hp = slice(HD * o_, HD * o_ + HD)
                    step(dve.tensor_scalar(KZ[m][hp, o_, :], dbank(g)[hp, m, :], pc("b_k", m)[hp], None, ALU.add))
            done_with(g)
            ahead.leave(g)
            g = ("vv",)
            group_ready(dve, g)
            for b in range(2):
                step(dve.tensor_tensor(VA[:, 2 * b:2 * b + 2, :],
                                       dbank(g)[:, b, :].rearrange("p (n v) -> p n v", n=2),
                                       pc("b_v").unsqueeze(1).to_broadcast([P, 2, 256]), ALU.add))
            done_with(g)
            dve.nop().then_inc(sem("qkv"), 1)
            ahead.leave(g)

            def scores(i):
                n, j, w = att(i)
                n_ = ("sc", i)
                ready(dve, n_)
                st = ATS[:, 16 * (i % 4):16 * (i % 4) + 16]
                sink = pc("sinks")[:, 2 * j:2 * j + 2]
                step(dve.tensor_reduce(st[:, 0:2], bank(n_)[:, 0:2 * w].rearrange("p (o s) -> p o s", o=2),
                                       AX.X, ALU.max))
                step(dve.tensor_tensor(st[:, 0:2], st[:, 0:2], sink, ALU.max))
                step(dve.tensor_tensor(st[:, 6:8], sink, st[:, 0:2], ALU.subtract))
                dve.tensor_scalar(st[:, 2:4], st[:, 0:2], -1.0, None, ALU.mult).then_inc(sem("att_max"), 1)

            def norm(i):
                n, j, w = att(i)
                pb = PB[i % 4][:, 0:2 * w].rearrange("p (o s) -> p o s", o=2)
                st = ATS[:, 16 * (i % 4):16 * (i % 4) + 16]
                dve.wait_ge(sem("att_exp"), 2 * (i + 1))
                dve.wait_ge(freed(("sc", i)), AUX_NO[("sc", i)] // 4 + 1)
                step(dve.tensor_tensor(st[:, 4:6], st[:, 4:6], st[:, 6:8], ALU.add))
                step(dve.reciprocal(st[:, 4:6], st[:, 4:6]))
                dve.tensor_tensor(pb, pb, st[:, 4:6].unsqueeze(2).to_broadcast([P, 2, w]), ALU.mult)\
                   .then_inc(sem("probs"), 1)

            for i in range(N_ATT + 1):
                if i < N_ATT:
                    scores(i)
                if i >= 1:
                    norm(i - 1)

        def second_tensor(pe, aux, filled, dense, colsum, weights, product, tile_of):
            xr = tile_of(X0_P)
            for j in range(8):
                dense(("sc_ch", j), xr, at="x0" if j == 0 else None)
            for j in range(4):
                dense(("sc_b", j), xr)
            for j in range(6):
                dense(("xbc", j), xr)
            dense(("dt",), xr, (16,))
            for j in range(2):
                dense(("z", j), xr)
            pe.wait_ge(sem("acs_ready"), 1)
            out = aux(("da_t",))
            for c in range(4):
                cs = slice(P * c, P * c + P)
                pe.transpose(out[:, 16 * c:16 * c + 16], DT[7][0:16, cs], ident[0:16, 0:16])
                mm = pe.transpose(out[:, 64 + 16 * c:80 + 16 * c], DT[5][0:16, cs], ident[0:16, 0:16])
            filled(mm)
            filled(pe.matmul(aux(("last",))[:, 0:64], ones[0:16, :], DT[6][0:16, 0:64], start=True, stop=True))
            pe.wait_ge(sem("xbc_done"), 12)
            for c in range(4):
                out = aux(("bct", c))
                for g in range(2):
                    mm = pe.transpose(out[:, P * g:P * g + P], BC[:, g, P * c:P * c + P], ident)
                filled(mm)
            for c in range(4):
                for h in range(2):
                    out = aux(("xst", c, h))
                    for k in range(4):
                        mm = pe.transpose(out[:, P * k:P * k + P], YS2[:, 4 * h + k, P * c:P * c + P], ident)
                    filled(mm)
            for g in range(2):
                out = aux(("cb", g))
                for c in range(4):
                    cs = slice(P * c, P * c + P)
                    mm = pe.matmul(out[:, cs], BC[:, g, cs], BC[:, 2 + g, cs], start=True, stop=True)
                filled(mm)
            for c in range(4):
                n_ = ("bct", c)
                pe.wait_ge(freed(n_), AUX_NO[n_] // 4 + 1)
            for c in range(3):
                pe.wait_ge(sem("xde"), c + 1)
                for g in range(2):
                    filled(pe.matmul(aux(("stt", c, g)), BTOK[:, c, g, :], XDE[:, 512 * g:512 * g + 512],
                                     start=True, stop=True))

            def spread(h):
                filled(pe.matmul(aux(("acs", h)), SELH[0:16, h, :], DT[7][0:16, :], start=True, stop=True))

            spread(0)
            spread(1)
            pe.wait_ge(sem("hin"), 1)
            for j in range(8):
                for h in (2 * j + 2, 2 * j + 3):
                    if h < 16:
                        spread(h)
                out = aux(("yd", j))
                pe.wait_ge(sem("head_ce"), 2 * j + 2)
                pe.wait_ge(sem("head_g"), 2 * j + 2)
                for o_ in range(2):
                    h = 2 * j + o_
                    for c in range(4):
                        cs = slice(P * c, P * c + P)
                        dst = out[HD * o_:HD * o_ + HD, cs]
                        mm = pe.matmul(dst, XDT[:, c, HD * h:HD * h + HD], GB[h % 4][:, cs], start=True, stop=(c == 0))
                        if c > 0:
                            mm = pe.matmul(dst, HIN[c - 1][:, HD * h:HD * h + HD], CE[h % 4][:, cs],
                                           start=False, stop=True)
                filled(mm)
            for j in range(2, 4):
                dense(("z", j), tile_of(Z_P), at="z" if j == 2 else None)
            for g in range(2):
                pe.wait_ge(sem("y_sq"), 4 * g + 4)
                colsum(("gss", g), lambda k: SQK[:, 4 * g + k, :], 4)
            for j in range(4):
                dense(("mix_out", j), lambda k: (YS_HI[k], YS_LO[:, k, :]),
                      at="ys" if j == 0 else None, order=lambda k: (k + 8) % 16)
            xr = tile_of(X_P)

            def layer_norm(n):
                which, layer = ("mix", "ffn")[n % 2], n // 2
                out = aux(("lnm", which, layer))
                for k in range(KT):
                    pe.wait_ge(sem("x_res"), KT * n + k + 1)
                    mm = pe.matmul(out, ones, X[:, k, :], start=(k == 0), stop=(k == KT - 1))
                filled(mm)
                out = aux(("lnv", which, layer))
                for k in range(KT):
                    pe.wait_ge(sem("ln_sq"), KT * n + k + 1)
                    mm = pe.matmul(out, ones, SQ2K[:, k, :], start=(k == 0), stop=(k == KT - 1))
                filled(mm)

            for layer in range(2):
                if layer == 1:
                    for j in range(4):
                        dense(("q", j), xr, at="q" if j == 0 else None)
                    dense(("kk",), xr)
                    g = ("vv",)
                    n = GROUP_NO[g]
                    pe.wait_ge(sem(f"pair_free{n % 2}"), n // 2)
                    u, nk, nco = UNITS_OF[g][0]
                    w = weights(u, nk, nco)
                    for m in range(4):
                        for k in range(KT):
                            mm = product(psD[:, n % 2, m // 2, 256 * (m % 2):256 * (m % 2) + 256],
                                         [v[:, k, P * m:P * m + P] for v in X_P], [v[:, k, :] for v in w],
                                         k == 0, k == KT - 1)
                    mm.then_inc(sem("units_done"), 1)
                    pe.wait_ge(sem("qkv"), 1)
                    pe.wait_ge(sem("att_consts"), 3)
                    for i in range(N_ATT + 3):
                        if i < N_ATT:
                            n, j, w_ = att(i)
                            k0 = P * n + P - w_
                            out = aux(("sc", i))[:, 0:2 * w_].rearrange("p (o s) -> p o s", o=2)
                            pe.matmul(out, Q[:, j, P * n:P * n + P], KZ[j // 4][:, :, k0:k0 + w_],
                                      start=True, stop=False)
                            band = CONST_R[:, 2 * P - w_:2 * P].unsqueeze(1).to_broadcast([P, 2, w_])
                            filled(pe.matmul(out, CONST_R[:, 2 * P:3 * P], band, start=False, stop=True))
                        if 2 <= i < N_ATT + 2:
                            k = i - 2
                            _, _, w_ = att(k)
                            out = aux(("pt", k))
                            pe.wait_ge(sem("probs"), k + 1)
                            for b in range(2 * w_ // P):
                                mm = pe.transpose(out[:, P * b:P * b + P], PB[k % 4][:, P * b:P * b + P], ident)
                            filled(mm)
                        if i >= 3:
                            k = i - 3
                            n, j, w_ = att(k)
                            nb = w_ // P
                            out = aux(("pv", k))
                            n_ = ("pt", k)
                            pe.wait_ge(freed(n_), AUX_NO[n_] // 4 + 1)
                            for o_ in range(2):
                                kv = 2 * (j // 4) + o_
                                for b in range(nb):
                                    mm = pe.matmul(out[HD * o_:HD * o_ + HD, 0:P],
                                                   VA[:, n - nb + 1 + b, HD * kv:HD * kv + HD],
                                                   PTB[k % 2][:, P * (nb * o_ + b):P * (nb * o_ + b) + P],
                                                   start=(b == 0), stop=(b == nb - 1))
                            filled(mm)
                    n_ = ("pv", N_ATT - 1)
                    pe.wait_ge(freed(n_), AUX_NO[n_] // 4 + 1)
                    for j in range(4):
                        dense(("wo", j), xr, at="oa" if j == 0 else None)
                layer_norm(2 * layer)
                for half in range(2):
                    for j in GATE_TILES[half]:
                        dense(("gu", layer, j), xr, at=("gu", layer) if j == 0 else None)
                    for j in range(4):
                        dense(("down", layer, half, j),
                              lambda k: (HID_P[0][:, k % HS, :], HID_P[1][:, k % HS, :]),
                              at=("hid", layer) if j == 0 else None, order=lambda k, half=half: FT // 2 * half + k)
                layer_norm(2 * layer + 1)
                for j in range(4):
                    dense(("ple_g", layer, j), xr, at=("ple", layer) if j == 0 else None)
                for j in range(4):
                    dense(("ple_w", layer, j), tile_of(PT_P), at=("pt", layer) if j == 0 else None)
        block = ctx.enter_context(nc.Block())

        def finish(sp_):
            sp_.wait_ge(sem("result"), 1)
            sp_.dma_start(out_t, XF).then_inc(sem("stored"), 16)
            sp_.wait_ge(sem("stored"), 16)

        @block.sync
        def _(sp_):
            sp_.dma_start(XF, x_t).then_inc(sem("x_in"), 16)
            sp_.dma_start(par[:, :], params).then_inc(sem("par_in"), 16)

            def load(i):
                _, nk, nco, _ = PLAN[i]
                if i >= RAW:
                    if i - RAW in SPLIT_NO:
                        sp_.wait_ge(sem("w_lo"), SPLIT_NO[i - RAW] + 1)
                    else:
                        sp_.wait_ge(sem("units_done"), i - RAW + 1)
                lo = (i % RAW) * UNIT
                sp_.dma_start(ring[:, lo:lo + nk * nco], w_dense[i, :, 0:nk * nco])\
                   .then_inc(sem(f"ring_full{i % RAW}"), 16)

            for i in range(N_FIRST):
                load(i)
                if PLAN[i][0] == ("lora_g",):
                    for n, g in ((1, "lora_wa"), (0, "lora_g")):
                        at = g1_at if n == 0 else g2_at
                        sp_.wait_ge(sem("units_done"), last_unit((g,)) + 1)
                        sp_.dma_start(ring[:, at:at + UNIT], w_dense[len(PLAN) + n]).then_inc(sem(f"gm{n + 1}_in"), 16)
            if stop == 1:
                return finish(sp_)
            moe_sync(sp_)
            if stop == 2:
                return finish(sp_)
            for i in range(N_FIRST, len(PLAN)):
                load(i)
            second_sync(sp_)
            finish(sp_)

        @block.gpsimd
        def _(pool):
            step = Steps(pool, sem("pool_step"))
            step(pool.memset(masks[:, :], 1.0))
            step(pool.memset(blk, 0.0))
            step(pool.memset(blk[0:HD, 0:HD], 1.0))
            step(pool.memset(blk[HD:P, HD:P], 1.0))
            step(pool.memset(reset[:, :], 1.0))
            step(pool.memset(reset[:, :].rearrange("p (c t) -> p c t", c=NCH)[:, :, 0:1], 0.0))
            step(pool.affine_select(out=ident, in_=ident, compare_op=ALU.is_equal, fill=0.0, base=0,
                                    pattern=[[-1, P]], channel_multiplier=1))
            step(pool.affine_select(out=strict_u, in_=strict_u, compare_op=ALU.is_gt, fill=0.0,
                                    base=0, pattern=[[1, P]], channel_multiplier=-1))
            step(pool.affine_select(out=pair[:, 1, :], in_=pair[:, 1, :], compare_op=ALU.is_ge, fill=0.0,
                                    base=0, pattern=[[1, P]], channel_multiplier=-1))
            for i, m in enumerate(level):
                b = 1 << i
                v = m.rearrange("p (n w) -> p n w", w=2 * b)
                step(pool.memset(v[:, :, 0:b], 0.0))
                second = v[:, :, b:2 * b]
                step(pool.affine_select(out=second, in_=second, compare_op=ALU.is_ge, fill=0.0, base=0,
                                        pattern=[[-2 * b, P // (2 * b)], [0, b]], channel_multiplier=1))
                step(pool.affine_select(out=second, in_=second, compare_op=ALU.is_ge, fill=0.0, base=b - 1,
                                        pattern=[[2 * b, P // (2 * b)], [0, b]], channel_multiplier=-1))
            pool.nop().then_inc(sem("consts"), 1)
            pool.wait_ge(sem("gm1_in"), 16)
            ws = G1[:, 0:1024].rearrange("p (h t) -> p h t", h=8)
            pool.affine_select(out=ws, in_=ws, compare_op=ALU.is_ge, fill=0.0, base=0,
                               pattern=[[0, 8], [1, P]], channel_multiplier=-1).then_inc(sem("ws_causal"), 1)
            pool.wait_ge(sem("v_centred"), 1)
            for m in range(4):
                step(pool.tensor_tensor(VTOK[:, m, :], VTOK[:, m, :], G1[:, 1024:1536], ALU.mult))
                pool.tensor_tensor(VTOK[:, m, :], VTOK[:, m, :], G1[:, 1536:2048], ALU.add)\
                    .then_inc(sem("v_norm"), 1)
            if stop == 1:
                return
            moe_pool(pool, step)
            if stop == 2:
                return
            second_pool(pool, step)

        @block.scalar
        def _(act):
            step = Steps(act, sem("act_step"))
            roots = [0]

            def root(ap):
                roots[0] += 1
                act.wait_ge(sem("root_in"), roots[0])
                act.activation(ap, ap, ACT.Sqrt).then_inc(sem("root_out"), 1)

            def cut(n):
                u = SPLIT_UNITS[n]
                _, nk, nco, _ = PLAN[u]
                loaded(act, u)
                if n >= 2:
                    act.wait_ge(sem("units_done"), SPLIT_UNITS[n - 2] + 1)
                act.activation(parts_of(u, nk, nco)[0], ring_of(u, nk, nco), ACT.Copy).then_inc(sem("w_hi"), 1)

            ahead = Ahead(cut)
            ahead.limit = last_unit(("lora_g",))

            def x_hi(dst, src, **kw):
                act.activation(dst, src, ACT.Identity if kw else ACT.Copy, **kw).then_inc(sem("x_hi"), 1)

            act.wait_ge(sem("x_in"), 16)
            act.activation(YF, XF, ACT.Square).then_inc(sem("sq1"), 1)
            act.wait_ge(sem("par_in"), 16)
            root(small[:, :])

            def mod_row(c, j, at, dst):
                n_ = ("mr", c, j)
                ready(act, n_)
                act.activation(dst[0:1, 256 * at:256 * at + 256], bank(n_)[0:1, 0:256], ACT.Copy)\
                   .then_inc(freed(n_), 1)

            for j in range(8):
                mod_row(0, j, j, MROW0)
            ahead(last_unit(("zv",)))
            for k in range(KT):
                act.wait_ge(sem("xn1"), k + 1)
                act.activation(H[:, k, :], H[:, k, :], ACT.Identity, scale=gain[:, k:k + 1],
                               bias=mod[:, k:k + 1]).then_inc(sem("h1"), 1)
                act.wait_ge(sem("h1"), k + 1)
                x_hi(H_P[0][:, k, :], H[:, k, :])
            for h in range(2):
                ahead.enter(("zv", h))
                group_ready(act, ("zv", h))
                act.activation(VTOK[:, 2 * h:2 * h + 2, :], dbank(("zv", h)), ACT.Gelu_apprx_tanh)\
                   .then_inc(group_freed(("zv", h)), 1)
            ahead.leave(("zv", 1))
            for h in range(2):
                ahead.enter(("zu", h))
                group_ready(act, ("zu", h))
                act.activation(YC[:, 2 * h:2 * h + 2, :], dbank(("zu", h)), ACT.Gelu_apprx_tanh)\
                   .then_inc(group_freed(("zu", h)), 1)
                ahead.leave(("zu", h))
            root(small[:, 48:52])
            act.wait_ge(sem("omm"), 1)
            n = 0
            for name, buf in (("r", R), ("k", K), ("v", V)):
                for h in range(2):
                    ahead.enter((name, h))
                    group_ready(act, (name, h))
                    for b in range(2):
                        j = 2 * h + b
                        act.activation(buf[:, j, :], dbank((name, h))[:, b, :], ACT.Identity,
                                       scale=gain[:, 8 + n:9 + n]).then_inc(sem("shift_a"), 1)
                        n += 1
                    ahead.leave((name, h))
            for g, b, w, i in LORAS:
                if b == 0:
                    ahead.enter(g)
                    group_ready(act, g)
                act.activation(LO[0:w, i, :], dbank(g)[0:w, b, :], ACT.Identity,
                               scale=gain[0:w, 8 + n:9 + n]).then_inc(sem("shift_a"), 1)
                n += 1
                ahead.leave(g)
            act.wait_ge(sem("shift_b"), 13)
            act.activation(LO[0:32, 0, :], LO[0:32, 0, :], ACT.Tanh).then_inc(sem("lora_w"), 1)
            act.wait_ge(sem("shift_b"), 15)
            act.activation(LO[0:96, 2, :], LO[0:96, 2, :], ACT.Sigmoid).then_inc(sem("lora_g"), 1)
            for j in range(4):
                ready(act, ("wl", j))
                act.activation(C[:, j, :], bank(("wl", j)), ACT.Sigmoid, bias=pc("w0", j))\
                   .then_inc(freed(("wl", j)), 1)
            for j in range(4):
                ready(act, ("al", j))
                act.activation(A[:, j, :], bank(("al", j)), ACT.Sigmoid, bias=pc("a0", j))\
                   .then_inc(freed(("al", j)), 1)
            act.wait_ge(sem("kk_raw"), 1)
            act.activation(EF, KKF, ACT.Square).then_inc(sem("kk_sq"), 1)
            for j in range(4):
                root(NB[:, j, :])
            act.wait_ge(sem("cum"), 1)
            act.activation(gain[:, 32:48], gain[:, 48:64], ACT.Exp).then_inc(sem("chunk_gain"), 1)
            for k_, name in ((0, "exp_r"), (1, "exp_a"), (2, "exp_b")):
                act.wait_ge(sem("cum"), k_ + 1)
                if k_ == 0:
                    ready(act, ("gm", 3))
                    act.activation(VTMP, EF, ACT.Exp).then_inc(sem(name), 1)
                elif k_ == 1:
                    act.activation(CF, CF, ACT.Exp).then_inc(sem(name), 1)
                else:
                    act.activation(EF, EF, ACT.Exp, scale=-1.0).then_inc(sem(name), 1)
            for c in range(NCH):
                for nm, buf in (("bt", BTK), ("kt", KTK), ("vt", VTK)):
                    ready(act, (nm, c))
                    if c > 0:
                        ready(act, ("st", c - 1))
                    act.activation(buf, bank((nm, c)), ACT.Copy).then_inc(freed((nm, c)), 1)
                for lv in range(LEVELS):
                    for q in range(2):
                        ready(act, ("u", c, lv, q))
                        act.activation(UI[:, 512 * q:512 * q + 512], bank(("u", c, lv, q)), ACT.Copy)\
                           .then_inc(freed(("u", c, lv, q)), 1)
                    if 1 <= lv <= 4:
                        n = lv - 1
                        if lv == 3:
                            ready(act, ("mo", c, 0))
                        mod_row(c + 1, n, n % 2, MROW)
                ready(act, ("u0", c))
                act.activation(UU, bank(("u0", c)), ACT.Copy).then_inc(freed(("u0", c)), 1)
                ready(act, ("sa", c))
                act.activation(SAS, bank(("sa", c)), ACT.Copy).then_inc(freed(("sa", c)), 1)
                ready(act, ("y", c))
                act.activation(V[:, :, P * c:P * c + P],
                               bank(("y", c)).rearrange("p (j t) -> p j t", j=4), ACT.Copy)\
                   .then_inc(freed(("y", c)), 1)
            for j in range(4):
                act.wait_ge(sem("gn_c"), j + 1)
                act.activation(C[:, j, :], E[:, j, :], ACT.Square).then_inc(sem("gn_sq"), 1)
            for j in range(4):
                root(NB[:, j, :])
            act.wait_ge(sem("ya"), 1)
            act.wait_ge(sem("yb"), 1)
            ahead.limit = N_FIRST - 1
            ahead(last_unit(("w_out", 0)))
            for k in range(KT):
                x_hi(YC_P[0][:, k, :], YC[:, k, :])
            ahead(N_FIRST - 1)
            if stop == 1:
                return
            moe_act(act, step, root, ahead, x_hi)
            if stop == 2:
                return
            second_act(act, step, root, ahead, x_hi)

        @block.vector
        def _(dve):
            step = Steps(dve, sem("dve_step"))

            asked = [0]

            def inv_sqrt(ins, ap):
                asked[0] += 1
                ins.then_inc(sem("root_in"), 1)
                dve.wait_ge(sem("root_out"), asked[0])
                step(dve.reciprocal(ap, ap))

            def ask_root():
                asked[0] += 1
                dve.nop().then_inc(sem("root_in"), 1)
                return asked[0]

            def inverse(count, ap):
                dve.wait_ge(sem("root_out"), count)
                step(dve.reciprocal(ap, ap))

            def take(name, ins):
                ins.then_inc(freed(name), 1)
                dve.wait_ge(freed(name), AUX_NO[name] // 4 + 1)

            def cut(n):
                u = SPLIT_UNITS[n]
                _, nk, nco, _ = PLAN[u]
                hi, lo_ = parts_of(u, nk, nco)
                dve.wait_ge(sem("w_hi"), n + 1)
                dve.tensor_tensor(lo_, ring_of(u, nk, nco), hi, ALU.subtract).then_inc(sem("w_lo"), 1)

            ahead = Ahead(cut)
            ahead.limit = last_unit(("lora_g",))

            def x_lo(name, k, both, src):
                part_hi_ready(dve, name, k)
                dve.tensor_tensor(both[1][:, k, :], src, both[0][:, k, :], ALU.subtract).then_inc(sem("x_lo"), 1)

            dve.wait_ge(sem("par_in"), 16)
            lo = PCOL["mu_r"][0]
            dve.tensor_scalar(gain[:, 8:23], par[:, lo:lo + 15], -1.0, 1.0, ALU.mult, ALU.add)\
               .then_inc(sem("omm"), 1)
            step(dve.tensor_scalar(gain[:, 24:28], pc("k_a"), -1.0, 1.0, ALU.mult, ALU.add))
            ready(dve, ("ss", 1))
            take(("ss", 1), dve.tensor_scalar(small[:, :], bank(("ss", 1)), 1.0 / D, 1e-6, ALU.mult, ALU.add))
            inv_sqrt(dve.nop(), small[:, :])
            ready(dve, ("mod",))
            take(("mod",), dve.tensor_tensor(mod[:, 0:16], bank(("mod",))[:, 0:16], pc("ada_b", 0, 16), ALU.add))
            step(dve.scalar_tensor_tensor(gain[:, 0:8], mod[:, 8:16], 1.0, pc("norm1_g"), ALU.add, ALU.mult))
            for k in range(KT):
                dve.tensor_tensor(H[:, k, :], X[:, k, :], small[:, :], ALU.mult).then_inc(sem("xn1"), 1)
            ahead(last_unit(("zv",)))
            for k in range(KT):
                x_lo("h1", k, H_P, H[:, k, :])

            st6, agg = small[:, 0:24], small[:, 32:40]
            for h in range(2):
                ahead.enter(("zv", h))
                dve.wait_ge(group_freed(("zv", h)), GROUP_NO[("zv", h)] // 2 + 1)
            ahead.leave(("zv", 1))
            for m in range(4):
                step(dve.bn_stats(st6[:, 6 * m:6 * m + 6], VTOK[:, m, :]))
                step(dve.bn_aggr(agg[:, 2 * m:2 * m + 2], st6[:, 6 * m:6 * m + 6]))
            var = agg.rearrange("p (m a) -> p m a", a=2)[:, :, 1]
            inv_sqrt(dve.tensor_scalar(small[:, 48:52], var, 1e-5, None, ALU.add), small[:, 48:52])
            for m in range(4):
                step(dve.tensor_scalar(VTOK[:, m, :], VTOK[:, m, :], agg[:, 2 * m:2 * m + 1],
                                       small[:, 48 + m:49 + m], ALU.subtract, ALU.mult))
            dve.nop().then_inc(sem("v_centred"), 1)

            n = 0
            for name, buf in (("r", R), ("k", K), ("v", V)):
                for h in range(2):
                    ahead.enter((name, h))
                    for b in range(2):
                        j = 2 * h + b
                        dve.wait_ge(sem("shift_a"), n + 1)
                        ins = dve.scalar_tensor_tensor(
                            buf[:, j, 1:SEQ], dbank((name, h))[:, b, 0:SEQ - 1], pc("mu_r", n),
                            buf[:, j, 1:SEQ], ALU.mult, ALU.add)
                        ins.then_inc(sem("shift_b"), 1)
                        n += 1
                    dve.wait_ge(sem("shift_b"), n)
                    dve.nop().then_inc(group_freed((name, h)), 1)
                    ahead.leave((name, h))
            for g, b, w, i in LORAS:
                ahead.enter(g)
                dve.wait_ge(sem("shift_a"), n + 1)
                dve.scalar_tensor_tensor(LO[0:w, i, 1:SEQ], dbank(g)[0:w, b, 0:SEQ - 1],
                                         pc("mu_r", n)[0:w], LO[0:w, i, 1:SEQ], ALU.mult, ALU.add)\
                   .then_inc(sem("shift_b"), 1)
                n += 1
                if b == 1 or i == 2:
                    dve.wait_ge(sem("shift_b"), n)
                    dve.nop().then_inc(group_freed(g), 1)
                    ahead.leave(g)

            dve.wait_ge(sem("gm2_in"), 16)
            for j in range(4):
                ins = dve.tensor_scalar(KK[:, j, :], K[:, j, :], pc("k_k", j), None, ALU.mult)
            step(ins)
            dve.nop().then_inc(sem("kk_raw"), 1)
            for j in range(4):
                dve.wait_ge(freed(("al", j)), AUX_NO[("al", j)] // 4 + 1)
                step(dve.tensor_scalar(T1[:, 0, :], A[:, j, :], pc("k_a", j), gain[:, 24 + j:25 + j],
                                       ALU.mult, ALU.add))
                step(dve.tensor_tensor(K[:, j, :], K[:, j, :], T1[:, 0, :], ALU.mult))
            counts_ = []
            for j in range(4):
                ready(dve, ("kn", j))
                take(("kn", j), dve.tensor_scalar(NB[:, j, :], bank(("kn", j)), 1e-24, None, ALU.max))
                counts_.append(ask_root())
            for j in range(4):
                inverse(counts_[j], NB[:, j, :])
                step(dve.tensor_tensor(KK[:, j, :], KK[:, j, :], NB[:, j, :], ALU.mult))
                step(dve.tensor_tensor(A[:, j, :], A[:, j, :], KK[:, j, :], ALU.mult))
            for j in range(4):
                dve.wait_ge(sem("kk_sq"), 1)
                ready(dve, ("kn", 3))
                dve.scalar_tensor_tensor(E[:, j, :], R[:, j, :], pc("r_k", j), K[:, j, :],
                                         ALU.mult, ALU.mult).then_inc(sem("rk"), 1)
            for j in range(4):
                ready(dve, ("bon", j))
                take(("bon", j), dve.tensor_tensor(YC[:, 4 + j, :], bank(("bon", j)), V[:, j, :], ALU.mult))
            step(dve.tensor_scalar(CF, CF, -float(np.exp(-0.5)), None, ALU.mult))
            for j in range(4):
                ready(dve, ("bon", 3))
                step(dve.tensor_tensor_scan(E[:, j, :], reset[:, :], C[:, j, :], 0.0, ALU.mult, ALU.add))
            half = small[:, 64:80]
            cum = EF.rearrange("p (g t) -> p g t", t=P)
            step(dve.tensor_scalar(half, cum[:, :, P - 1], 0.5, None, ALU.mult))
            hv = half.rearrange("p (j c) -> p j c", c=4)
            gv = gain[:, 48:64].rearrange("p (j c) -> p j c", c=4)
            step(dve.tensor_tensor(gv[:, :, 0:3], hv[:, :, 0:3], hv[:, :, 1:4], ALU.add))
            step(dve.tensor_copy(gv[:, :, 3:4], hv[:, :, 3:4]))
            step(dve.tensor_tensor(cum, cum, half.unsqueeze(2).to_broadcast([P, 16, P]), ALU.subtract))
            dve.nop().then_inc(sem("cum"), 1)
            step(dve.tensor_tensor(CF, EF, CF, ALU.subtract))
            dve.nop().then_inc(sem("cum"), 1)
            dve.wait_ge(sem("exp_r"), 1)
            dve.nop().then_inc(sem("cum"), 1)
            arr = [AR[:, j, :, 1, :] for j in range(4)]
            ara = [AR[:, j, :, 0, :] for j in range(4)]

            def cv(t, j):
                return t[:, j, :].rearrange("p (c t) -> p c t", c=4)
            vt = VTMP.rearrange("p (k t) -> p k t", k=4)
            for j in range(4):
                dve.tensor_tensor(arr[j], cv(R, j), cv(vt, j), ALU.mult).then_inc(sem("ar"), 1)
            dve.wait_ge(sem("exp_a"), 1)
            for j in range(4):
                dve.scalar_tensor_tensor(ara[j], cv(KK, j), -1.0, cv(C, j), ALU.mult, ALU.mult)\
                   .then_inc(sem("ar"), 1)
            dve.wait_ge(sem("exp_b"), 1)
            for j in range(4):
                dve.tensor_tensor(A[:, j, :], A[:, j, :], E[:, j, :], ALU.mult).then_inc(sem("bk"), 1)
                dve.tensor_tensor(K[:, j, :], K[:, j, :], E[:, j, :], ALU.mult).then_inc(sem("bk"), 1)
            dve.wait_ge(sem("bk"), 8)
            dve.wait_ge(sem("ar"), 8)
            for c in range(4):
                n_ = ("gm", c)
                ready(dve, n_)
                bs = G2[:, 0, :].rearrange("p (j t) -> p j t", j=4)
                t1 = T1[:, 0, :].rearrange("p (j t) -> p j t", j=4)
                take(n_, dve.tensor_tensor(t1, bank(n_).rearrange("p (j t) -> p j t", j=4), bs, ALU.add))
                step(dve.tensor_tensor(YC[:, 0:4, P * c:P * c + P], YC[:, 0:4, P * c:P * c + P], t1, ALU.mult))
            dve.nop().then_inc(sem("ya"), 1)

            for c in range(NCH):
                for q in range(4):
                    for nm, buf in (("ab", AB), ("ak", AK)):
                        pass
                for nm, buf in (("ab", AB), ("ak", AK)):
                    for q in range(4):
                        n_ = (nm, c, q)
                        ready(dve, n_)
                        if c > 0:
                            ready(dve, ("y", c - 1))
                        take(n_, dve.tensor_tensor(
                            buf[:, 4 * (q // 2) + q % 2:4 * (q // 2) + q % 2 + 3:2], bank(n_).rearrange("p (h a t) -> p h a t", h=2, a=2),
                            pair.unsqueeze(1).to_broadcast([P, 2, 2, P]), ALU.mult))
                idb = ident.unsqueeze(1).to_broadcast([P, 8, P])
                xiv, xtv = (t.rearrange("p (h t) -> p h t", h=8) for t in (XI, XT))
                lmv = [t.rearrange("p (h t) -> p h t", h=8) for t in LM]

                def level_part(lv):
                    if lv >= 2:
                        ready(dve, ("u", c, lv - 2, 1))
                    dve.tensor_tensor(lmv[lv % 2], AB[:, :, 0, :], level[lv].unsqueeze(1).to_broadcast([P, 8, P]),
                                      ALU.mult).then_inc(sem("lm"), 1)

                level_part(0)
                level_part(1)
                for lv in range(LEVELS):
                    if lv == 0:
                        dve.wait_ge(sem("lm"), LEVELS * c + 1)
                        step(dve.tensor_tensor(xtv, lmv[0], idb, ALU.add))
                        for q in range(2):
                            n_ = ("u", c, lv, q)
                            ready(dve, n_)
                            dve.wait_ge(freed(n_), AUX_NO[n_] // 4 + 1)
                            qs = slice(4 * q, 4 * q + 4)
                            dve.tensor_tensor(xiv[:, qs], UI.rearrange("p (h t) -> p h t", h=8)[:, qs],
                                              idb[:, qs], ALU.add).then_inc(sem("x_new"), 1)
                        continue
                    if lv + 1 < LEVELS:
                        level_part(lv + 1)
                    for q in range(2):
                        qs = slice(512 * q, 512 * q + 512)
                        for nm, buf in (("xn", XI), ("xt", XT))[lv == LEVELS - 1:]:
                            n_ = (nm, c, lv, q)
                            ready(dve, n_)
                            if nm == "xn" or lv == LEVELS - 1:
                                dve.wait_ge(sem("x_new"), 2 * (LEVELS * c + lv - 1) + q + 1)
                            dve.tensor_tensor(buf[:, qs], buf[:, qs], bank(n_), ALU.add).then_inc(freed(n_), 1)
                        dve.wait_ge(freed(n_), AUX_NO[n_] // 4 + 1)
                        dve.nop().then_inc(sem("x_new"), 1)
                    if lv in (2, 4):
                        n_ = ("mo", c, lv // 2 - 1)
                        ready(dve, n_)
                        lo = 16 + 8 * c + 4 * (lv // 2 - 1)
                        dve.tensor_tensor(mod[:, lo:lo + 4], bank(n_)[:, 0:4], pc("ada_b", lo, 4), ALU.add)\
                           .then_inc(freed(n_), 1)
                if c < NCH - 1:
                    n_ = ("st", c)
                    ready(dve, n_)
                    fac = gain[:, 32:48].rearrange("p (j c) -> p j c", c=4)[:, :, c:c + 1]\
                        .to_broadcast([P, 4, P])
                    stv = ST.rearrange("p (j v) -> p j v", j=4)
                    t1v = T2[:, :].rearrange("p (j v) -> p j v", j=4)
                    psv = bank(n_).rearrange("p (j v) -> p j v", j=4)
                    blkb = blk.unsqueeze(1).to_broadcast([P, 4, P])
                    dve.wait_ge(sem("chunk_gain"), 1)
                    take(n_, dve.tensor_tensor(t1v, psv, blkb, ALU.mult))
                    if c > 0:
                        step(dve.tensor_tensor(t1v, t1v, stv, ALU.add))
                    step(dve.tensor_tensor(stv, t1v, fac, ALU.mult))
                    dve.nop().then_inc(sem("state"), 1)

            for c in range(NCH):
                dve.wait_ge(freed(("y", c)), AUX_NO[("y", c)] // 4 + 1)
            for j in range(4):
                n_ = ("gnm", j)
                ready(dve, n_)
                take(n_, dve.scalar_tensor_tensor(E[:, j, :], bank(n_), -1.0 / HD, V[:, j, :], ALU.mult, ALU.add))
                dve.nop().then_inc(sem("gn_c"), 1)
            counts_ = []
            for j in range(4):
                n_ = ("gnv", j)
                ready(dve, n_)
                take(n_, dve.tensor_scalar(NB[:, j, :], bank(n_), 1.0 / HD, 64e-5, ALU.mult, ALU.add))
                counts_.append(ask_root())
            for j in range(4):
                inverse(counts_[j], NB[:, j, :])
                step(dve.tensor_tensor(E[:, j, :], E[:, j, :], NB[:, j, :], ALU.mult))
                step(dve.tensor_scalar(E[:, j, :], E[:, j, :], pc("gn_w", j), pc("gn_b", j), ALU.mult, ALU.add))
                step(dve.tensor_tensor(YC[:, 4 + j, :], YC[:, 4 + j, :], E[:, j, :], ALU.add))
            for j in range(4):
                n_ = ("gg", j)
                ready(dve, n_)
                take(n_, dve.tensor_tensor(YC[:, 4 + j, :], YC[:, 4 + j, :], bank(n_), ALU.mult))
            dve.nop().then_inc(sem("yb"), 1)
            ahead.limit = N_FIRST - 1
            ahead(last_unit(("w_out", 0)))
            for k in range(KT):
                x_lo("yc", k, YC_P, YC[:, k, :])
            for h in range(4):
                ahead.enter(("w_out", h))
                group_ready(dve, ("w_out", h))
                for b in range(2):
                    j = 2 * h + b
                    dve.scalar_tensor_tensor(X[:, j, :], dbank(("w_out", h))[:, b, :], mod[:, 16 + j:17 + j],
                                             X[:, j, :], ALU.mult, ALU.add).then_inc(sem("x_mixed"), 1)
                dve.wait_ge(sem("x_mixed"), 2 * h + 2)
                dve.nop().then_inc(group_freed(("w_out", h)), 1)
            if stop == 1:
                dve.nop().then_inc(sem("result"), 1)
                return
            moe_vector(dve, step, take, inv_sqrt, ahead, x_lo)
            if stop == 2:
                return
            second_vector(dve, step, take, inv_sqrt, ahead, x_lo)

        @block.tensor
        def _(pe):
            done_aux = [0]

            def aux(name):
                n = done_aux[0]
                assert AUX[n] == name, (AUX[n], name)
                done_aux[0] += 1
                if n >= 4:
                    pe.wait_ge(sem(f"aux_free{n % 4}"), n // 4)
                return psA[:, n % 4, :]

            def filled(mm):
                mm.then_inc(sem("aux_ready"), 1)

            def weights(u, nk, nco):
                pe.wait_ge(sem("w_lo"), SPLIT_NO[u] + 1)
                return parts_of(u, nk, nco)

            def product(out, w, x, start, stop_):
                for i, (a, b) in enumerate(((1, 0), (0, 1), (0, 0))):
                    mm = pe.matmul(out, w[a], x[b], start=start and i == 0, stop=stop_ and i == 2)
                return mm

            def dense(group, rhs, widths=(P, P), at=None, order=lambda k: k):
                n = GROUP_NO[group]
                if n >= 2:
                    pe.wait_ge(sem(f"pair_free{n % 2}"), n // 2)
                units = UNITS_OF[group]
                k0, total = 0, sum(nk for _, nk, _ in units)
                for u, nk, nco in units:
                    w = weights(u, nk, nco)
                    off = 0
                    for b, width in enumerate(widths):
                        for k in range(nk):
                            if b == 0 and at is not None:
                                part_ready(pe, at, order(k0 + k))
                            mm = product(psD[0:width, n % 2, b, :], [v[:, k, off:off + width] for v in w],
                                         rhs(order(k0 + k)), k0 + k == 0, k0 + k == total - 1)
                        off += width
                    mm.then_inc(sem("units_done"), 1)
                    k0 += nk

            def tile_of(both):
                return lambda k: (both[0][:, k, :], both[1][:, k, :])

            def colsum(name, src, tiles, m=ones, ready_at=None):
                out = aux(name)
                for k in range(tiles):
                    if ready_at is not None:
                        pe.wait_ge(sem(ready_at[0]), ready_at[1](k))
                    mm = pe.matmul(out, m, src(k), start=(k == 0), stop=(k == tiles - 1))
                filled(mm)

            def modulation(c, j, unit):
                out = aux(("mr", c, j))
                u, nk, nco = UNITS_OF[("ada", unit)][0]
                loaded(pe, u)
                w = ring_of(u, nk, nco)
                for k in range(KT):
                    mm = pe.matmul(out[0:1, 0:256], pc("c", k), w[:, k, :], start=(k == 0), stop=(k == KT - 1))
                mm.then_inc(sem("units_done"), 1)
                filled(pe.matmul(out[0:1, 256:257], pc("c", 0), pc("c", 0), start=True, stop=True))

            def to_column(name, row, n, last):
                out = aux(name)
                pe.wait_ge(freed(last), AUX_NO[last] // 4 + 1)
                for i in range(n):
                    mm = pe.matmul(out[:, i:i + 1], row[0:1, P * i:P * i + P], ones[0:1, 0:1], start=True, stop=True)
                filled(mm)

            pe.wait_ge(sem("consts"), 1)
            pe.wait_ge(sem("sq1"), 1)
            colsum(("ss", 1), lambda k: YC[:, k, :], KT)
            pe.wait_ge(sem("par_in"), 16)
            for j in range(8):
                modulation(0, j, j)
            to_column(("mod",), MROW0, 16, ("mr", 0, 7))

            for i, (u, nk, nco) in enumerate(UNITS_OF[("zv",)]):
                w = weights(u, nk, nco)
                for m in range(4):
                    for k in range(nk):
                        kk_ = 4 * i + k
                        if m == 0:
                            part_ready(pe, "h1", kk_)
                        mm = product(psD[:, m // 2, m % 2, :], [v[:, kk_, P * m:P * m + P] for v in H_P],
                                     [v[:, k, :] for v in w], kk_ == 0, kk_ == KT - 1)
                mm.then_inc(sem("units_done"), 1)
            hr = tile_of(H_P)
            for name in ("zu", "r", "k", "v"):
                for h in range(2):
                    dense((name, h), hr)
            dense(("lora_wa",), hr, (32, 32))
            dense(("lora_g",), hr, (96,))

            g2, ws = G2, G1[:, 0:1024].rearrange("p (h t) -> p h t", h=8)
            pe.wait_ge(sem("gm2_in"), 16)
            pe.wait_ge(sem("lora_w"), 1)
            for j in range(4):
                filled(pe.matmul(aux(("wl", j)), g2[0:32, 1, P * j:P * j + P], LO[0:32, 0, :], start=True, stop=True))
            for j in range(4):
                filled(pe.matmul(aux(("al", j)), g2[0:32, 2, P * j:P * j + P], LO[0:32, 1, :], start=True, stop=True))
            pe.wait_ge(sem("kk_sq"), 1)
            for j in range(4):
                filled(pe.matmul(aux(("kn", j)), blk, E[:, j, :], start=True, stop=True))
            for j in range(4):
                pe.wait_ge(sem("rk"), j + 1)
                filled(pe.matmul(aux(("bon", j)), blk, E[:, j, :], start=True, stop=True))
            pe.wait_ge(sem("ws_causal"), 1)
            for c in range(4):
                pe.wait_ge(sem("v_norm"), c + 1)
                out = aux(("gm", c))
                for h in range(8):
                    mm = pe.matmul(out[HD * (h % 2):HD * (h % 2) + HD, P * (h // 2):P * (h // 2) + P],
                                   VTOK[:, c, HD * h:HD * h + HD], ws[:, h, :], start=True, stop=True)
                filled(mm)

            pe.wait_ge(sem("bk"), 8)
            for c in range(NCH):
                tk = slice(P * c, P * c + P)
                for nm, src in (("bt", A), ("kt", K), ("vt", V)):
                    out = aux((nm, c))
                    for j in range(4):
                        mm = pe.transpose(out[:, P * j:P * j + P], src[:, j, tk], ident)
                    filled(mm)
                pe.wait_ge(sem("ar"), 8)
                for nm, src in (("ab", A), ("ak", K)):
                    for q in range(4):
                        out = aux((nm, c, q))
                        hp = slice(HD * (q % 2), HD * (q % 2) + HD)
                        for i in range(2):
                            j = 2 * (q // 2) + i
                            mm = pe.matmul(out[:, 256 * i:256 * i + 256], src[hp, j, tk],
                                           AR[hp, j, c, :, :].rearrange("p a t -> p (a t)"), start=True, stop=True)
                        filled(mm)
                def hs(t, h):
                    return t[:, P * h:P * h + P]
                for lv in range(LEVELS):
                    pe.wait_ge(sem("lm"), LEVELS * c + lv + 1)
                    for q in range(2):
                        out = aux(("u", c, lv, q))
                        if lv > 0:
                            pe.wait_ge(sem("x_new"), 2 * (LEVELS * c + lv - 1) + q + 1)
                        for i in range(4):
                            mm = pe.matmul(out[:, P * i:P * i + P], hs(LM[lv % 2], 4 * q + i),
                                           ident if lv == 0 else hs(XI, 4 * q + i), start=True, stop=True)
                        filled(mm)
                    if 1 <= lv <= 4:
                        modulation(c + 1, lv - 1, 7 + 4 * c + lv)
                    if lv == 0:
                        continue
                    for q in range(2):
                        n_ = ("u", c, lv, q)
                        if lv < LEVELS - 1:
                            out = aux(("xn", c, lv, q))
                            pe.wait_ge(freed(n_), AUX_NO[n_] // 4 + 1)
                            for i in range(4):
                                mm = pe.matmul(out[:, P * i:P * i + P], hs(XT, 4 * q + i), hs(UI, 4 * q + i),
                                               start=True, stop=True)
                            filled(mm)
                        out = aux(("xt", c, lv, q))
                        pe.wait_ge(freed(n_), AUX_NO[n_] // 4 + 1)
                        for i in range(4):
                            mm = pe.matmul(out[:, P * i:P * i + P], hs(UI, 4 * q + i), hs(XT, 4 * q + i),
                                           start=True, stop=True)
                        filled(mm)
                    if lv in (2, 4):
                        to_column(("mo", c, lv // 2 - 1), MROW, 4, ("mr", c + 1, lv - 1))
                pe.wait_ge(sem("x_new"), 2 * LEVELS * (c + 1))
                if c > 0:
                    pe.wait_ge(sem("state"), c)
                out = aux(("u0", c))
                for h in range(8):
                    j = h // 2
                    if c > 0 and h % 2 == 0:
                        pe.matmul(out[:, P * j:P * j + P], AR[:, j, c, 0, :], ST[:, P * j:P * j + P],
                                  start=True, stop=False, skip_group_check=True)
                    mm = pe.matmul(out[:, HD * h:HD * h + HD], AK[:, h, 0, :], VTK[:, HD * h:HD * h + HD],
                                   start=(c == 0), stop=(c == 0 or h % 2 == 1), skip_group_check=(c > 0))
                filled(mm)
                out = aux(("sa", c))
                pe.wait_ge(freed(("u0", c)), AUX_NO[("u0", c)] // 4 + 1)
                for h in range(8):
                    mm = pe.matmul(out[:, HD * h:HD * h + HD], hs(XT, h), UU[:, HD * h:HD * h + HD],
                                   start=True, stop=True)
                filled(mm)
                out = aux(("y", c))
                pe.wait_ge(freed(("sa", c)), AUX_NO[("sa", c)] // 4 + 1)
                for h in range(8):
                    j, hp = h // 2, slice(HD * (h % 2), HD * (h % 2) + HD)
                    o_ = out[hp, P * j:P * j + P]
                    if c > 0:
                        pe.matmul(o_, ST[:, HD * h:HD * h + HD], AR[:, j, c, 1, :], start=True, stop=False)
                    pe.matmul(o_, SAS[:, HD * h:HD * h + HD], AB[:, h, 1, :], start=(c == 0), stop=False)
                    mm = pe.matmul(o_, VTK[:, HD * h:HD * h + HD], AK[:, h, 1, :], start=False, stop=True)
                filled(mm)
                if c < NCH - 1:
                    out = aux(("st", c))
                    for j in range(4):
                        ts_ = slice(P * j, P * j + P)
                        pe.matmul(out[:, ts_], BTK[:, ts_], SAS[:, ts_], start=True, stop=False)
                        mm = pe.matmul(out[:, ts_], KTK[:, ts_], VTK[:, ts_], start=False, stop=True)
                    filled(mm)
            for c in range(NCH):
                pe.wait_ge(freed(("y", c)), AUX_NO[("y", c)] // 4 + 1)
            for j in range(4):
                filled(pe.matmul(aux(("gnm", j)), blk, V[:, j, :], start=True, stop=True))
            for j in range(4):
                pe.wait_ge(sem("gn_sq"), j + 1)
                filled(pe.matmul(aux(("gnv", j)), blk, C[:, j, :], start=True, stop=True))
            pe.wait_ge(sem("lora_g"), 1)
            for j in range(4):
                mm = pe.matmul(aux(("gg", j)), g2[0:96, 3, P * j:P * j + P], LO[0:96, 2, :], start=True, stop=True)
                filled(mm)
            for h in range(4):
                dense(("w_out", h), tile_of(YC_P), at="yc" if h == 0 else None)
            if stop == 1:
                return
            moe_tensor(pe, aux, filled, dense, colsum, product)
            if stop == 2:
                return
            second_tensor(pe, aux, filled, dense, colsum, weights, product, tile_of)

STOP = None



def kernel(**inputs):
    from concourse import bacc
    from concourse.bass_utils import run_bass_kernel_spmd

    a = {k: np.asarray(v) for k, v in inputs.items()}
    dense = np.zeros((len(PLAN) + 2, P, UNIT), np.float32)
    dense[-2], dense[-1] = gm1(a), gm2(a)
    for i, (_, nk, nco, fill) in enumerate(PLAN):
        dense[i, :, 0:nk * nco] = np.asarray(fill(a)).reshape(P, nk * nco)
    arrays = {
        "x_t": np.ascontiguousarray(a["x"][0].T.reshape(KT, P, SEQ).transpose(1, 0, 2)).reshape(P, KT * SEQ),
        "params": np.ascontiguousarray(np.concatenate(
            [np.asarray(fill(a)).reshape(P, w) for _, w, fill in PARAMS], 1)),
        "w_dense": dense,
        "p_t": np.ascontiguousarray(a["p_2"][:, 0].transpose(0, 2, 1).reshape(2, 2, P, SEQ).transpose(0, 2, 1, 3)),
        "moe_gate": np.ascontiguousarray(a["moe_w_gate"][0]),
        "moe_up": np.ascontiguousarray(a["moe_w_up"][0]),
        "moe_down": np.ascontiguousarray(a["moe_w_down"][0]),
    }
    nc = bacc.Bacc("TRN2", target_bir_lowering=False, num_devices=1)
    args = [nc.dram_tensor(n, v.shape, mybir.dt.from_np(v.dtype), kind="ExternalInput").ap()
            for n, v in arrays.items()]
    out = nc.dram_tensor("out_t", (P, KT * SEQ), F32, kind="ExternalOutput").ap()
    build(nc, *args, out, stop=STOP)
    got = run_bass_kernel_spmd(nc, [arrays], core_ids=[0]).results[0]["out_t"]
    return np.ascontiguousarray(np.asarray(got).reshape(P, KT, SEQ).transpose(2, 1, 0)).reshape(1, SEQ, D)
```
